# Optimizing a Trainium2 kernel written in Bass

```python
import jax, jax.numpy as jnp
from jax import lax
import numpy as np

D_MODEL = 1024
BATCH = 1
SEQ = 1024
DEPTH = 1
DEC_BATCH = 8
DEC_SEQ = 16
PAST_LEN = 128

CHUNK = 64
N_META = 16
QBLOCK = 128
H_A = 4
DK_A = 32
DV_A = 64
GATE_RANK = 16
GATE_TAU = 16.0
H_B = 4
DH_B = 64
CONV_W = 4
H_C = 8
HKV_C = 2
DH_C = 64
H_IDX = 4
D_IDX = 32
TOPK_KEYS = 256
N_EXPERTS = 16
N_GROUPS = 4
TOPK_GROUPS = 1
TOP_K = 2
D_EXPERT = 256

W_A = H_A * DV_A
W_B = H_B * DH_B
W_C = H_C * DH_C
D_MIX = W_A + W_B + W_C
LN_EPS = 1e-5
ALPHA = (2 * DEPTH) ** 0.25
BETA = (8 * DEPTH) ** -0.25

_SPLITS = (
    ('a_q', H_A * DK_A), ('a_k', H_A * DK_A), ('a_v', W_A), ('a_g', GATE_RANK), ('a_r', W_A),
    ('b_qk', 2 * W_B), ('b_v', W_B), ('b_i', H_B), ('b_f', H_B), ('b_o', W_B),
    ('c_q', W_C), ('c_k', HKV_C * DH_C), ('c_v', HKV_C * DH_C),
    ('c_qi', H_IDX * D_IDX), ('c_w', H_IDX), ('c_ki', D_IDX),
)
D_IN = sum(n for _, n in _SPLITS)

kernel_name = 'hybrid_gla_mlstm_dsa_moe_stream_step'

def split_cols(u):
    out = {}
    off = 0
    for name, n in _SPLITS:
        out[name] = u[..., off:off + n]
        off += n
    return out

def layer_norm(x, g, b):
    xf = x.astype(jnp.float32)
    mu = xf.mean(-1, keepdims=True)
    var = jnp.square(xf - mu).mean(-1, keepdims=True)
    return ((xf - mu) * lax.rsqrt(var + LN_EPS) * g + b).astype(x.dtype)

def head_norm(h, g):
    mu = h.mean(-1, keepdims=True)
    var = jnp.square(h - mu).mean(-1, keepdims=True)
    y = (h - mu) * lax.rsqrt(var + LN_EPS)
    return y.reshape(*h.shape[:-2], -1) * g.astype(jnp.float32)

def gla_block(S0, q, k, v, la):
    L = q.shape[1]
    b = jnp.cumsum(la, axis=1)
    causal = jnp.tril(jnp.ones((L, L), bool))
    diff = jnp.where(causal[None, :, :, None, None], b[:, :, None] - b[:, None, :], -jnp.inf)
    att = jnp.einsum('bthd,bshd,btshd->bhts', q, k, jnp.exp(diff))
    o = jnp.einsum('bhts,bshv->bthv', att, v) + jnp.einsum('bthd,bhdv->bthv', q * jnp.exp(b), S0)
    bL = b[:, -1]
    S = jnp.exp(bL)[..., None] * S0 + jnp.einsum('bshd,bshv->bhdv', k * jnp.exp(bL[:, None] - b), v)
    return S, o

def mlstm_block(carry, q, k, v, ig, lf):
    C0, n0, m0 = carry
    L = q.shape[1]
    b = jnp.cumsum(lf, axis=1)
    causal = jnp.tril(jnp.ones((L, L), bool))
    logw = jnp.where(causal[None, :, :, None], b[:, :, None] - b[:, None, :] + ig[:, None, :], -jnp.inf)
    log_prev = b + m0[:, None]
    m = jnp.maximum(log_prev, logw.max(axis=2))
    w = jnp.exp(logw - m[:, :, None])
    sp = jnp.exp(log_prev - m)
    qk = jnp.einsum('bthd,bshd->btsh', q, k) * w
    num = jnp.einsum('btsh,bshv->bthv', qk, v) + sp[..., None] * jnp.einsum('bhvd,bthd->bthv', C0, q)
    den = qk.sum(axis=2) + sp * jnp.einsum('bhd,bthd->bth', n0, q)
    h = num / jnp.maximum(jnp.abs(den), jnp.exp(-m))[..., None]
    mL = m[:, -1]
    wL = jnp.exp(b[:, -1:] - b + ig - mL[:, None])
    sL = jnp.exp(b[:, -1] + m0 - mL)
    C = sL[..., None, None] * C0 + jnp.einsum('bsh,bshv,bshd->bhvd', wL, v, k)
    n = sL[..., None] * n0 + jnp.einsum('bsh,bshd->bhd', wL, k)
    return (C, n, mL), h

def scan_stream(block_fn, carry, seqs):
    carry, out_meta = block_fn(carry, *[s[:, :N_META] for s in seqs])
    rest = [s[:, N_META:] for s in seqs]
    B, T = rest[0].shape[:2]
    nc = T // CHUNK
    blocks = tuple(jnp.swapaxes(r.reshape(B, nc, CHUNK, *r.shape[2:]), 0, 1) for r in rest)
    carry, outs = lax.scan(lambda c, xs: block_fn(c, *xs), carry, blocks)
    outs = jnp.swapaxes(outs, 0, 1).reshape(B, T, *outs.shape[3:])
    return carry, jnp.concatenate([out_meta, outs], axis=1)

def causal_conv(u, buf, w, b):
    T = u.shape[1]
    up = jnp.concatenate([buf, u], axis=1)
    y = sum(up[:, j:j + T] * w[j] for j in range(CONV_W)) + b
    return y, up[:, -(CONV_W - 1):]

def dsa_attend(q, qi, wi, qcid, k_all, v_all, ki_all, kcid, n_sel):
    f32 = jnp.float32
    raw = jnp.einsum('bthi,bsi->bths', qi.astype(f32), ki_all.astype(f32))
    iscore = jnp.einsum('bth,bths->bts', wi.astype(f32), jax.nn.relu(raw))
    admissible = kcid[None, :] <= qcid[:, None]
    iscore = jnp.where(admissible[None], iscore, -jnp.inf)
    _, sel = lax.top_k(iscore, n_sel)
    valid = jnp.take(kcid, sel) <= qcid[None, :, None]
    gather = jax.vmap(lambda a, i: a[i])
    k_sel = gather(k_all, sel).astype(f32)
    v_sel = gather(v_all, sel).astype(f32)
    logits = jnp.einsum('btkgd,btnkd->btkgn', q.astype(f32), k_sel) * DH_C ** -0.5
    logits = jnp.where(valid[:, :, None, None, :], logits, -jnp.inf)
    p = jax.nn.softmax(logits, axis=-1)
    o = jnp.einsum('btkgn,btnkd->btkgd', p, v_sel)
    return o.reshape(*o.shape[:2], -1)

def dsa_prompt(q, qi, wi, qcid, k_all, v_all, ki_all, kcid, n_sel):
    B, T = q.shape[:2]
    nb = -(-T // QBLOCK)
    pad = nb * QBLOCK - T

    def blk(a):
        a = jnp.pad(a, [(0, 0), (0, pad)] + [(0, 0)] * (a.ndim - 2))
        return jnp.swapaxes(a.reshape(B, nb, QBLOCK, *a.shape[2:]), 0, 1)

    qcb = jnp.pad(qcid, (0, pad), mode='edge').reshape(nb, QBLOCK)
    out = lax.map(lambda xs: dsa_attend(xs[0], xs[1], xs[2], xs[3], k_all, v_all, ki_all, kcid, n_sel),
                  (blk(q), blk(qi), blk(wi), qcb))
    return jnp.swapaxes(out, 0, 1).reshape(B, nb * QBLOCK, -1)[:, :T]

def token_mixer(h, st, qcid, kcid, n_sel, is_prompt, w_in, b_in, w_gla_gate, b_gla_gate, g_gla_norm,
                conv_w, conv_b, b_forget, g_mlstm_norm, w_out):
    f32 = jnp.float32
    ck, cv, cki, s_gla, s_c, s_n, s_m, s_conv = st
    B, T, _ = h.shape
    c = split_cols(h @ w_in + b_in)
    qa = c['a_q'].reshape(B, T, H_A, DK_A).astype(f32) * DK_A ** -0.5
    ka = c['a_k'].reshape(B, T, H_A, DK_A).astype(f32)
    va = c['a_v'].reshape(B, T, H_A, DV_A).astype(f32)
    la = jax.nn.log_sigmoid((c['a_g'] @ w_gla_gate + b_gla_gate).astype(f32)).reshape(B, T, H_A, DK_A) / GATE_TAU
    seq_a = (qa, ka, va, la)
    if is_prompt:
        S_a, oa = scan_stream(gla_block, s_gla.astype(f32), seq_a)
    else:
        S_a, oa = gla_block(s_gla.astype(f32), *seq_a)
    ya = head_norm(oa, g_gla_norm) * jax.nn.silu(c['a_r'].astype(f32))
    qk_pre = c['b_qk']
    conv_out, conv_buf = causal_conv(qk_pre, s_conv.astype(qk_pre.dtype), conv_w, conv_b)
    conv_out = jax.nn.silu(conv_out.astype(f32))
    qb = conv_out[..., :W_B].reshape(B, T, H_B, DH_B)
    kb = conv_out[..., W_B:].reshape(B, T, H_B, DH_B) * DH_B ** -0.5
    vb = c['b_v'].reshape(B, T, H_B, DH_B).astype(f32)
    ig = c['b_i'].astype(f32)
    lf = jax.nn.log_sigmoid(c['b_f'].astype(f32) + b_forget.astype(f32))
    carry_b = (s_c.astype(f32), s_n.astype(f32), s_m.astype(f32))
    seq_b = (qb, kb, vb, ig, lf)
    if is_prompt:
        (C_b, n_b, m_b), hb = scan_stream(mlstm_block, carry_b, seq_b)
    else:
        (C_b, n_b, m_b), hb = mlstm_block(carry_b, *seq_b)
    yb = head_norm(hb, g_mlstm_norm) * jax.nn.sigmoid(c['b_o'].astype(f32))
    q_c = c['c_q'].reshape(B, T, HKV_C, H_C // HKV_C, DH_C)
    k_new = c['c_k'].reshape(B, T, HKV_C, DH_C)
    v_new = c['c_v'].reshape(B, T, HKV_C, DH_C)
    ki_new = c['c_ki']
    qi = c['c_qi'].reshape(B, T, H_IDX, D_IDX) * D_IDX ** -0.5
    wi = c['c_w'] * H_IDX ** -0.5
    k_all = jnp.concatenate([ck.astype(h.dtype), k_new], axis=1)
    v_all = jnp.concatenate([cv.astype(h.dtype), v_new], axis=1)
    ki_all = jnp.concatenate([cki.astype(h.dtype), ki_new], axis=1)
    if is_prompt:
        yc = dsa_prompt(q_c, qi, wi, qcid, k_all, v_all, ki_all, kcid, n_sel)
    else:
        yc = dsa_attend(q_c, qi, wi, qcid, k_all, v_all, ki_all, kcid, n_sel)
    y = jnp.concatenate([ya, yb, yc], axis=-1).astype(h.dtype) @ w_out
    return y, (k_new, v_new, ki_new, S_a, C_b, n_b, m_b, conv_buf)

def moe(h, w_router, b_router, w_gate, w_up, w_down):
    f32 = jnp.float32
    shp = h.shape
    x = h.reshape(-1, shp[-1])
    s = jax.nn.sigmoid((x @ w_router).astype(f32))
    sb = s + b_router.astype(f32)
    eg = N_EXPERTS // N_GROUPS
    grp_score = lax.top_k(sb.reshape(-1, N_GROUPS, eg), TOP_K)[0].sum(-1)
    _, gsel = lax.top_k(grp_score, TOPK_GROUPS)
    gmask = jax.nn.one_hot(gsel, N_GROUPS, dtype=f32).sum(-2) > 0
    emask = jnp.repeat(gmask, eg, axis=-1)
    _, esel = lax.top_k(jnp.where(emask, sb, -jnp.inf), TOP_K)
    wsel = jnp.take_along_axis(s, esel, axis=-1)
    wsel = wsel / wsel.sum(-1, keepdims=True)
    gates = jnp.einsum('nk,nke->ne', wsel, jax.nn.one_hot(esel, N_EXPERTS, dtype=f32))
    y = jnp.zeros(x.shape, f32)
    for e in range(N_EXPERTS):
        he = jax.nn.silu(x @ w_gate[e]) * (x @ w_up[e])
        y = y + gates[:, e:e + 1] * (he @ w_down[e]).astype(f32)
    return y.astype(h.dtype).reshape(shp)

def trunk(h, caches, qcid, kcid, n_sel, is_prompt, w_in, b_in, w_gla_gate, b_gla_gate, g_gla_norm,
          conv_w, conv_b, b_forget, g_mlstm_norm, w_out, ln1_g, ln1_b, w_router, b_router,
          w_gate, w_up, w_down, ln2_g, ln2_b):
    new = [[] for _ in caches]
    for l in range(DEPTH):
        mix, st = token_mixer(h, tuple(cc[l] for cc in caches), qcid, kcid, n_sel, is_prompt,
                              w_in[l], b_in[l], w_gla_gate[l], b_gla_gate[l], g_gla_norm[l],
                              conv_w[l], conv_b[l], b_forget[l], g_mlstm_norm[l], w_out[l])
        h = layer_norm(ALPHA * h + mix, ln1_g[l], ln1_b[l])
        h = layer_norm(ALPHA * h + moe(h, w_router, b_router, w_gate[l], w_up[l], w_down[l]), ln2_g[l], ln2_b[l])
        for acc, a in zip(new, st):
            acc.append(a.astype(h.dtype))
    return h, [jnp.stack(acc) for acc in new]

def setup_inputs(seed: int = 0) -> dict:
    key = jax.random.key(seed)
    ks = iter(jax.random.split(key, 48))

    def nrm(shape, scale=1.0):
        return jax.random.normal(next(ks), shape, jnp.float32) * scale

    d = {}
    d['x_prompt'] = nrm((BATCH, SEQ, D_MODEL))
    d['x_sample'] = nrm((DEC_BATCH, DEC_SEQ, D_MODEL))
    d['cache_k'] = nrm((DEPTH, DEC_BATCH, PAST_LEN, HKV_C, DH_C))
    d['cache_v'] = nrm((DEPTH, DEC_BATCH, PAST_LEN, HKV_C, DH_C))
    d['cache_kidx'] = nrm((DEPTH, DEC_BATCH, PAST_LEN, D_IDX))
    d['state_gla'] = nrm((DEPTH, DEC_BATCH, H_A, DK_A, DV_A), 0.5)
    d['state_mlstm_c'] = nrm((DEPTH, DEC_BATCH, H_B, DH_B, DH_B), 0.5)
    d['state_mlstm_n'] = nrm((DEPTH, DEC_BATCH, H_B, DH_B), 0.5)
    d['state_mlstm_m'] = nrm((DEPTH, DEC_BATCH, H_B))
    d['state_conv'] = nrm((DEPTH, DEC_BATCH, CONV_W - 1, 2 * W_B))
    d['meta_tokens'] = nrm((N_META, D_MODEL))
    d['ln_in_g'] = 1.0 + nrm((D_MODEL,), 0.02)
    d['ln_in_b'] = nrm((D_MODEL,), 0.02)
    d['w_in'] = nrm((DEPTH, D_MODEL, D_IN), D_MODEL ** -0.5)
    d['b_in'] = nrm((DEPTH, D_IN), 0.02)
    d['w_gla_gate'] = nrm((DEPTH, GATE_RANK, H_A * DK_A), GATE_RANK ** -0.5)
    d['b_gla_gate'] = nrm((DEPTH, H_A * DK_A), 0.1)
    d['g_gla_norm'] = 1.0 + nrm((DEPTH, W_A), 0.02)
    d['conv_w'] = nrm((DEPTH, CONV_W, 2 * W_B), CONV_W ** -0.5)
    d['conv_b'] = nrm((DEPTH, 2 * W_B), 0.02)
    d['b_forget'] = jnp.linspace(3.0, 6.0, H_B, dtype=jnp.float32)[None] + nrm((DEPTH, H_B), 0.1)
    d['g_mlstm_norm'] = 1.0 + nrm((DEPTH, W_B), 0.02)
    d['w_out'] = nrm((DEPTH, D_MIX, D_MODEL), BETA * D_MIX ** -0.5)
    d['ln1_g'] = 1.0 + nrm((DEPTH, D_MODEL), 0.02)
    d['ln1_b'] = nrm((DEPTH, D_MODEL), 0.02)
    d['w_router'] = nrm((D_MODEL, N_EXPERTS), D_MODEL ** -0.5)
    d['b_router'] = nrm((N_EXPERTS,), 0.01)
    d['w_gate'] = nrm((DEPTH, N_EXPERTS, D_MODEL, D_EXPERT), D_MODEL ** -0.5)
    d['w_up'] = nrm((DEPTH, N_EXPERTS, D_MODEL, D_EXPERT), D_MODEL ** -0.5)
    d['w_down'] = nrm((DEPTH, N_EXPERTS, D_EXPERT, D_MODEL), BETA * D_EXPERT ** -0.5)
    d['ln2_g'] = 1.0 + nrm((DEPTH, D_MODEL), 0.02)
    d['ln2_b'] = nrm((DEPTH, D_MODEL), 0.02)
    return d

def reference(x_prompt, x_sample, cache_k, cache_v, cache_kidx, state_gla, state_mlstm_c, state_mlstm_n,
              state_mlstm_m, state_conv, meta_tokens, ln_in_g, ln_in_b, w_in, b_in, w_gla_gate, b_gla_gate,
              g_gla_norm, conv_w, conv_b, b_forget, g_mlstm_norm, w_out, ln1_g, ln1_b, w_router, b_router,
              w_gate, w_up, w_down, ln2_g, ln2_b):
    i32 = jnp.int32
    f32 = jnp.float32
    B, S_p, D = x_prompt.shape
    dt = x_prompt.dtype
    meta = jnp.broadcast_to(meta_tokens.astype(dt)[None], (B, N_META, D))
    hp = layer_norm(jnp.concatenate([meta, x_prompt], axis=1), ln_in_g, ln_in_b)
    cid_p = jnp.concatenate([jnp.full((N_META,), -1, i32), jnp.arange(S_p, dtype=i32) // CHUNK])
    n_sel_p = min(TOPK_KEYS, S_p // 4)
    zero_p = (jnp.zeros((DEPTH, B, 0, HKV_C, DH_C), dt), jnp.zeros((DEPTH, B, 0, HKV_C, DH_C), dt),
              jnp.zeros((DEPTH, B, 0, D_IDX), dt), jnp.zeros((DEPTH, B, H_A, DK_A, DV_A), f32),
              jnp.zeros((DEPTH, B, H_B, DH_B, DH_B), f32), jnp.zeros((DEPTH, B, H_B, DH_B), f32),
              jnp.zeros((DEPTH, B, H_B), f32), jnp.zeros((DEPTH, B, CONV_W - 1, 2 * W_B), dt))
    hp, p_states = trunk(hp, zero_p, cid_p, cid_p, n_sel_p, True, w_in, b_in, w_gla_gate, b_gla_gate,
                         g_gla_norm, conv_w, conv_b, b_forget, g_mlstm_norm, w_out, ln1_g, ln1_b,
                         w_router, b_router, w_gate, w_up, w_down, ln2_g, ln2_b)
    y_prompt = hp[:, N_META:]
    P = cache_k.shape[2]
    Ts = x_sample.shape[1]
    hs = layer_norm(x_sample, ln_in_g, ln_in_b)
    kcid_s = jnp.arange(P + Ts, dtype=i32) // CHUNK
    qcid_s = kcid_s[P:]
    n_sel_s = min(TOPK_KEYS, (P + Ts) // 4)
    caches_s = (cache_k, cache_v, cache_kidx, state_gla, state_mlstm_c, state_mlstm_n, state_mlstm_m, state_conv)
    hs, s_states = trunk(hs, caches_s, qcid_s, kcid_s, n_sel_s, False, w_in, b_in, w_gla_gate, b_gla_gate,
                         g_gla_norm, conv_w, conv_b, b_forget, g_mlstm_norm, w_out, ln1_g, ln1_b,
                         w_router, b_router, w_gate, w_up, w_down, ln2_g, ln2_b)
    y_sample = hs
    p_k, p_v, p_kidx, p_gla, p_c, p_n, p_m, p_conv = p_states
    s_k, s_v, s_kidx, s_gla, s_c, s_n, s_m, s_conv = s_states
    return (y_prompt, y_sample, p_k, p_v, p_kidx, p_gla, p_c, p_n, p_m, p_conv,
            s_k, s_v, s_kidx, s_gla, s_c, s_n, s_m, s_conv)


_drawn_inputs = setup_inputs


def setup_inputs(seed=0):
    import zlib

    import numpy as np

    out = dict(_drawn_inputs(seed))
    spreads = {}
    factors = {'g_gla_norm': 2.965, 'g_mlstm_norm': 7.072, 'ln2_g': 2.766, 'ln2_b': 2.898}
    for name, (base, spread) in spreads.items():
        noise = np.random.default_rng([zlib.crc32(name.encode()), seed]).standard_normal(out[name].shape)
        drawn = base * np.exp(spread * noise) if base else spread * noise
        out[name] = __import__('jax').numpy.asarray(drawn.astype(out[name].dtype))
    for name, factor in factors.items():
        out[name] = (out[name] * factor).astype(out[name].dtype)
    return out
```

```python
from contextlib import ExitStack

import concourse.bass as bass
import numpy as np
from concourse import mybir

F32 = mybir.dt.float32
I32 = mybir.dt.int32
U32 = mybir.dt.uint32
ALU = mybir.AluOpType
ACT = mybir.ActivationFunctionType
AX = mybir.AxisListType
ds = bass.ds

P = 128
D = 1024
KD = D // P
SEQ, NSEQ, SLEN, META = 1024, 8, 16, 16
NT = SEQ // P
SAMPLE = NT
MT = NT + 1
TOK = SEQ + NSEQ * SLEN
TT = TOK // P
ALL = TOK + META
PROMPT = META + SEQ
PAST = 128
HA, DKA, DVA, RANK = 4, 32, 64, 16
HB, DHB = 4, 64
HC, KVC, DHC = 8, 2, 64
HI, DI = 4, 32
TOPK_P, TOPK_S = 256, (PAST + SLEN) // 4
NE, NG, EG, DE = 16, 4, 4, 256
EPS = 1e-5
ALPHA = 2 ** 0.25
NEG = -1e30
TAKEN = -3e38

AV, AR, BV, BO, CV, CK, CI, CW = 0, 256, 512, 768, 1024, 1152, 1280, 1312
TM, TG = 1320, 440
F_AQ, F_AK, F_BQ, F_BK, F_CQ, F_CK, F_QI, F_KI, F_MISC = 0, 1, 2, 4, 6, 10, 11, 12, 13
FM = 14
ROW_I, ROW_F = 32, 64

CONSTS = {}
_at = 0
for _name, _n in (("ident", P), ("headA", HA), ("bdA", 256), ("causal", P), ("blocked", P),
                  ("seqmask", NSEQ), ("bdB", 130), ("headB", 2), ("otherseq", P), ("tri", P),
                  ("iota16", NE), ("tiles128", 9), ("rowid", TT), ("slotid", 33), ("selM", 512), ("selB", 256)):
    CONSTS[_name] = (_at, _at + _n)
    _at += _n
NCONST = _at


class Chain:

    def __init__(self, eng, sem, base=0):
        self.eng, self.sem, self.base, self.k = eng, sem, base, 0

    def link(self, ins):
        self.k += 1
        ins.then_inc(self.sem, 1)
        self.eng.wait_ge(self.sem, self.base + self.k)

    def steps(self, n):
        assert self.k == n, (self.k, n)


class Semaphores:

    def __init__(self, nc, tag):
        self.nc, self.tag, self.made = nc, tag, []

    def __call__(self, name):
        self.made.append(self.nc.alloc_semaphore(self.tag + name))
        return self.made[-1]

    def __enter__(self):
        return self

    def __exit__(self, *error):
        if not any(error):
            self.nc.clear_and_free_semaphores(self.made)
            self.nc.all_engine_barrier()


def cols(m, name):
    a, b = CONSTS[name]
    return m.const[:, a:b]


def phase_project(nc, m, d):
    with ExitStack() as ctx:
        sem = Semaphores(nc, "p1_")
        at = m.at
        wtm = at("wtm", [P, KD, TM], m.FMO)
        o = m.FMO + KD * TM * 4
        x = at("x_ring", [P, 3, D], o)
        sq = at("p1_btm", [P, TM], o + 3 * D * 4)
        o = m.SCR
        gb = at("ln_in_gb", [P, 2, D], o)
        h0 = at("h0_ring", [P, 3, D], o + 8192)
        hr = at("h0T_ring", [P, 3, KD, P], o + 8192 + 12288)
        stats = at("p1_stats", [P, 3, 2, 6], o + 8192 + 24576)
        mv = at("p1_mv", [P, 3, 4], o + 8192 + 24576 + 160)
        btm = sq
        pT = [ctx.enter_context(nc.psum_tensor(f"p1_T{i}", [P, 4, P], F32)) for i in range(2)]
        pU = [ctx.enter_context(nc.psum_tensor(f"p1_U{i}", [P, 512], F32)) for i in range(6)]

        consts_in, x_in = sem("consts_in"), [sem(f"x_in{i}") for i in range(3)]
        wtm_in, h0_out = sem("wtm_in"), [sem(f"h0_out{i}") for i in range(3)]
        dve_own, act_own, pool_own = sem("dve_own"), sem("act_own"), sem("pool_own")
        var_ready, rstd_ready, xn_ready, h0_ready = sem("var_ready"), sem("rstd_ready"), sem("xn_ready"), sem("h0_ready")
        turned, hT_copied, tm_ready, tm_copied = sem("turned"), sem("hT_copied"), sem("tm_ready"), sem("tm_copied")

        ctx.enter_context(sem)
        with nc.Block() as block:
            @block.sync
            def _(sp):
                sp.dma_start(m.const[:, :], d["consts"]).then_inc(consts_in, 16)
                sp.dma_start(gb[:, :, :], d["ln_in_gb"].partition_broadcast(P)).then_inc(consts_in, 16)
                sp.dma_start(btm[:, :], d["b_tm"].partition_broadcast(P)).then_inc(consts_in, 16)

                for u in range(3):
                    sp.dma_start(x[:, u, :], d["x"][u * P:(u + 1) * P, :]).then_inc(x_in[u], 16)
                for k in range(KD):
                    sp.dma_start(wtm[:, k, :], d["w_tm"][:, k, :]).then_inc(wtm_in, 16)
                with sp.Fori(1, 3) as r:
                    for u in range(3):
                        sp.wait_ge(xn_ready, 3 * r + (u - 2))
                        sp.dma_start(x[:, u, :], d["x"][ds((3 * r + u) * P, P), :]).then_inc(x_in[u], 16)
                sp.wait_ge(xn_ready, 7)
                sp.dma_start(x[0:META, 0, :], d["x"][TOK:ALL, :]).then_inc(x_in[0], 16)

            @block.gpsimd
            def _(pool):
                pool.wait_ge(consts_in, 48)

                def scale(r, u, rows=P):
                    t = 3 * r + u
                    own = Chain(pool, pool_own, t)
                    pool.wait_ge(xn_ready, t + 1)
                    own.link(nc.gpsimd.tensor_tensor(h0[0:rows, u, :], h0[0:rows, u, :], gb[0:rows, 0, :], ALU.mult))
                    nc.gpsimd.tensor_tensor(h0[0:rows, u, :], h0[0:rows, u, :], gb[0:rows, 1, :],
                                            ALU.add).then_inc(h0_ready, 1)

                with pool.Fori(0, 3) as r:
                    for u in range(3):
                        scale(r, u)
                scale(3, 0, META)

            @block.vector
            def _(dve):
                dve.wait_ge(consts_in, 48)

                def norm(r, u, rows=P):
                    t = 3 * r + u
                    own = Chain(dve, dve_own, 3 * t)
                    dve.wait_ge(x_in[u], 16 * (r + 1))
                    own.link(nc.vector.bn_stats(stats[0:rows, u, 0, :], x[0:rows, u, 0:512]))
                    own.link(nc.vector.bn_stats(stats[0:rows, u, 1, :], x[0:rows, u, 512:1024]))
                    nc.vector.tensor_copy(mv[0:rows, u, 3:4], stats[0:rows, u, 1, 0:1])
                    own.link(nc.vector.bn_aggr(mv[0:rows, u, 0:2], stats[0:rows, u, :, :]))
                    nc.vector.tensor_scalar(mv[0:rows, u, 2:3], mv[0:rows, u, 1:2], EPS, None,
                                            ALU.add).then_inc(var_ready, 1)
                    dve.wait_ge(rstd_ready, t + 1)
                    if not isinstance(r, int) or r:
                        dve.wait_ge(h0_out[u], 16 * r)
                        dve.wait_ge(turned, 2 * t - 4)
                    nc.vector.tensor_scalar(h0[0:rows, u, :], x[0:rows, u, :], mv[0:rows, u, 0:1], mv[0:rows, u, 3:4],
                                            ALU.subtract, ALU.mult).then_inc(xn_ready, 1)

                def evacuate(r, u, rows=P):
                    t = 3 * r + u
                    for g in range(3):
                        dve.wait_ge(tm_ready, 3 * t + g + 1)
                        nc.vector.tensor_tensor(m.tm[0:rows, t, g * TG:(g + 1) * TG], pU[3 * (u % 2) + g][0:rows, 0:TG],
                                                btm[0:rows, g * TG:(g + 1) * TG], ALU.add).then_inc(tm_copied, 1)
                norm(0, 0)
                for u in range(1, 3):
                    norm(0, u)
                    evacuate(0, u - 1)
                with dve.Fori(1, 3) as r:
                    for u in range(3):
                        norm(r, u)
                        if u:
                            evacuate(r, u - 1)
                        else:
                            evacuate(r - 1, 2)
                norm(3, 0, META)
                evacuate(2, 2)
                evacuate(3, 0, META)

            @block.scalar
            def _(act):
                def rstd(r, u, rows=P):
                    t = 3 * r + u
                    own = Chain(act, act_own, t)
                    act.wait_ge(var_ready, t + 1)
                    own.link(nc.scalar.activation(mv[0:rows, u, 3:4], mv[0:rows, u, 2:3], ACT.Ln))
                    nc.scalar.activation(mv[0:rows, u, 3:4], mv[0:rows, u, 3:4], ACT.Exp, scale=-0.5).then_inc(rstd_ready, 1)

                def copy(r, u, rows=P):
                    t = 3 * r + u
                    if rows == P:
                        dst = m.hT[:, :, ds(META + t * P, P)]
                    else:
                        dst = m.hT[:, :, 0:META]
                    for b in range(2):
                        act.wait_ge(turned, 2 * t + b + 1)
                        if not isinstance(r, int) or r:
                            act.wait_ge(tm_ready, 3 * t - 5)
                        nc.scalar.copy(hr[:, u, 4 * b:4 * b + 4, 0:rows], pT[b][:, :, 0:rows]).then_inc(hT_copied, 1)
                        nc.scalar.copy(dst[:, 4 * b:4 * b + 4, :], pT[b][:, :, 0:rows]).then_inc(hT_copied, 1)
                    act.wait_ge(h0_ready, t + 1)
                    if rows == P:
                        act.dma_start(m.h0_dram[ds(t * P, P), :], h0[:, u, :]).then_inc(h0_out[u], 16)

                rstd(0, 0)
                for u in range(1, 3):
                    rstd(0, u)
                    copy(0, u - 1)
                with act.Fori(1, 3) as r:
                    for u in range(3):
                        rstd(r, u)
                        if u:
                            copy(r, u - 1)
                        else:
                            copy(r - 1, 2)
                rstd(3, 0, META)
                copy(2, 2)
                copy(3, 0, META)
                for u in range(3):
                    act.wait_ge(h0_out[u], 48)

            @block.tensor
            def _(pe):
                pe.wait_ge(consts_in, 48)

                def turn(r, u, rows=P):
                    t = 3 * r + u
                    pe.wait_ge(h0_ready, t + 1)
                    for b in range(2):
                        if not isinstance(r, int) or r or u:
                            pe.wait_ge(hT_copied, 4 * t - 2 + 2 * b)
                        for k in range(4):
                            mm = nc.tensor.transpose(pT[b][:, k, 0:rows], h0[0:rows, u, (4 * b + k) * P:(4 * b + k + 1) * P],
                                                     cols(m, "ident")[0:rows, 0:rows])
                        mm.then_inc(turned, 1)

                def product(r, u, rows=P):
                    t = 3 * r + u
                    pe.wait_ge(hT_copied, 4 * t + 4)
                    for g in range(3):
                        if u == 2:
                            pe.wait_ge(tm_copied, 3 * t - 5 + g)
                        elif u == 0 and not (isinstance(r, int) and r == 0):
                            pe.wait_ge(tm_copied, 3 * t - 2 + g)
                        elif not (isinstance(r, int) and r == 0):
                            pe.wait_ge(tm_copied, 3 * t - 5 + g)
                        for k in range(KD):
                            mm = nc.tensor.matmul(pU[3 * (u % 2) + g][0:rows, 0:TG], hr[:, u, k, 0:rows],
                                                  wtm[:, k, g * TG:(g + 1) * TG], start=k == 0, stop=k == KD - 1)
                        mm.then_inc(tm_ready, 1)
                turn(0, 0)
                pe.wait_ge(wtm_in, 16 * KD)
                for u in range(1, 3):
                    turn(0, u)
                    product(0, u - 1)
                with pe.Fori(1, 3) as r:
                    for u in range(3):
                        turn(r, u)
                        if u:
                            product(r, u - 1)
                        else:
                            product(r - 1, 2)
                turn(3, 0, META)
                product(2, 2)
                product(3, 0, META)


def phase_project_fm(nc, m, d):
    with ExitStack() as ctx:
        sem = Semaphores(nc, "p2_")
        w = m.at("wfm_ring", [P, 2, KD, P], m.SCR)
        bfm = m.at("p2_bfm", [P, FM], m.SCR + 8192)
        ps = [ctx.enter_context(nc.psum_tensor(f"p2_{i}", [P, 512], F32)) for i in range(6)]
        w_in, b_in, rows_out = [sem("w_in0"), sem("w_in1")], sem("b_in"), sem("rows_out")
        fm_ready, fm_copied = sem("fm_ready"), sem("fm_copied")
        spans = [(0, 512), (512, 1024), (1024, ALL)]
        ctx.enter_context(sem)
        with nc.Block() as block:
            @block.sync
            def _(sp):
                sp.dma_start(bfm[:, :], d["b_fm"]).then_inc(b_in, 16)
                for u in range(2):
                    sp.dma_start(w[:, u, :, :], d["w_fm"][u, :, :, :]).then_inc(w_in[u], 16)
                with sp.Fori(1, FM // 2) as r:
                    for u in range(2):
                        sp.wait_ge(fm_ready, 6 * r + (3 * u - 3))
                        sp.dma_start(w[:, u, :, :], d["w_fm"][2 * r + u, :, :, :]).then_inc(w_in[u], 16)

            @block.gpsimd
            def _(pool):
                n = 0
                for name, c, width in (("k", CK, 128), ("v", CV, 128), ("kidx", CI, DI)):
                    out = d["p_" + name]
                    pool.dma_start(out[0:META, :], m.tm[0:META, MT, c:c + width]).then_inc(rows_out, 16)
                    pool.dma_start(out[META:PROMPT, :].rearrange("(j p) c -> p j c", p=P),
                                   m.tm[:, 0:NT, c:c + width]).then_inc(rows_out, 16)
                    pool.dma_start(d["s_" + name], m.tm[:, SAMPLE, c:c + width]).then_inc(rows_out, 16)
                    n += 3
                pool.wait_ge(rows_out, 16 * n)

            @block.tensor
            def _(pe):
                def tile(r, u, first):
                        pe.wait_ge(w_in[u], 16 * r + 16)
                        for c, (a, b) in enumerate(spans):
                            if not first:
                                pe.wait_ge(fm_copied, 6 * r + (3 * u + c - 5))
                            for k in range(KD):
                                mm = nc.tensor.matmul(ps[3 * u + c][:, 0:b - a], w[:, u, k, :], m.hT[:, k, a:b],
                                                      start=k == 0, stop=k == KD - 1)
                            mm.then_inc(fm_ready, 1)
                tile(0, 0, True)
                tile(0, 1, True)
                with pe.Fori(1, FM // 2) as r:
                    for u in range(2):
                        tile(r, u, False)

            @block.scalar
            def _(act):
                act.wait_ge(b_in, 16)
                with act.Fori(0, FM // 2) as r:
                    for u in range(2):
                        for c, (a, b) in enumerate(spans):
                            act.wait_ge(fm_ready, 6 * r + (3 * u + c + 1))
                            nc.scalar.activation(m.fm[:, 2 * r + u, a:b], ps[3 * u + c][:, 0:b - a], ACT.Identity,
                                                 bias=bfm[:, ds(2 * r + u, 1)]).then_inc(fm_copied, 1)


class Bump:

    def __init__(self, m, tag, start, end):
        self.m, self.tag, self.o, self.end = m, tag, start, end

    def __call__(self, name, shape, dtype=F32):
        n = int(np.prod(shape[1:])) * 4
        at = self.o
        self.o = at + (n + 31) // 32 * 32
        assert self.o <= self.end, (self.tag, name, self.o - self.end)
        return self.m.at(self.tag + name, shape, at, dtype)


def over(ap, shape):
    return ap.broadcast_to(shape)


def phase_conv(nc, m, d):
    with ExitStack() as ctx:
        sem = Semaphores(nc, "p3_")
        al = Bump(m, "p3_", m.HTO, m.CO)
        acc, den = al("acc", [P, ALL]), al("den", [P, ALL])
        hist = al("hist", [P, 4, NSEQ, 3])
        up = al("up", [P, NSEQ, SLEN + 3])
        wc = al("wc", [P, 4, 5])
        last_p, last_s = al("last_p", [P, 4, 3]), al("last_s", [P, 4, NSEQ, 3])
        w_in, acc_ready, exp_ready, saved, out, own_s = (sem("w_in"), sem("acc_ready"), sem("exp_ready"),
                                                         sem("saved"), sem("out"), sem("own"))
        ctx.enter_context(sem)
        with nc.Block() as block:
            @block.sync
            def _(sp):
                sp.dma_start(hist[:, :, :, :], d["conv_hist"]).then_inc(w_in, 16)
                sp.dma_start(wc[:, :, :], d["conv_wb"]).then_inc(w_in, 16)
                sp.wait_ge(saved, 4)
                sp.dma_start(d["p_conv"].rearrange("c p j -> p c j"), last_p[:, :, :]).then_inc(out, 16)
                sp.dma_start(d["s_conv"].rearrange("c p i j -> p c i j"), last_s[:, :, :, :]).then_inc(out, 16)
                sp.wait_ge(out, 32)

            @block.vector
            def _(dve):
                dve.wait_ge(w_in, 32)
                with dve.Fori(0, 4) as c:
                    own = Chain(dve, own_s, 11 * c)
                    u = m.fm[:, F_BQ + c, :]
                    us = m.fm[:, F_BQ + c, PROMPT:ALL].rearrange("p (i t) -> p i t", i=NSEQ)
                    tap = lambda j: wc[:, c, j:j + 1]
                    nc.vector.tensor_copy(last_p[:, c, :], u[:, PROMPT - 3:PROMPT])
                    nc.vector.tensor_copy(last_s[:, c, :, :], us[:, :, SLEN - 3:SLEN]).then_inc(saved, 1)
                    nc.vector.tensor_copy(up[:, :, 0:3], hist[:, c, :, :])
                    own.link(nc.vector.tensor_copy(up[:, :, 3:SLEN + 3], us))
                    own.link(nc.vector.tensor_scalar(acc[:, 0:PROMPT], u[:, 0:PROMPT], tap(3), tap(4), ALU.mult, ALU.add))
                    for j in range(1, 4):
                        own.link(nc.vector.scalar_tensor_tensor(acc[:, j:PROMPT], u[:, 0:PROMPT - j], tap(3 - j),
                                                                acc[:, j:PROMPT], ALU.mult, ALU.add))
                    accs = acc[:, PROMPT:ALL].rearrange("p (i t) -> p i t", i=NSEQ)
                    own.link(nc.vector.tensor_scalar(accs, up[:, :, 3:SLEN + 3], tap(3), tap(4), ALU.mult, ALU.add))
                    for j in range(1, 4):
                        ins = nc.vector.scalar_tensor_tensor(accs, up[:, :, 3 - j:SLEN + 3 - j], tap(3 - j), accs,
                                                             ALU.mult, ALU.add)
                        if j < 3:
                            own.link(ins)
                    ins.then_inc(acc_ready, 1)
                    dve.wait_ge(exp_ready, c + 1)
                    own.link(nc.vector.tensor_scalar(den[:, :], den[:, :], 1.0, None, ALU.add))
                    own.link(nc.vector.reciprocal(den[:, :], den[:, :]))
                    own.link(nc.vector.tensor_tensor(u, acc[:, :], den[:, :], ALU.mult))
                    own.steps(11)
                own = Chain(dve, own_s, 11 * 4)
                for c in range(2):
                    own.link(nc.vector.tensor_scalar(m.fm[:, F_BK + c, :], m.fm[:, F_BK + c, :], DHB ** -0.5, None, ALU.mult))

            @block.scalar
            def _(act):
                with act.Fori(0, 4) as c:
                    act.wait_ge(acc_ready, c + 1)
                    nc.scalar.activation(den[:, :], acc[:, :], ACT.Exp, scale=-1.0).then_inc(exp_ready, 1)


def log_sigmoid_act(nc, act, own, out, z):
    own.link(nc.scalar.activation(out, z, ACT.Abs))
    own.link(nc.scalar.activation(out, out, ACT.Exp, scale=-1.0))
    return nc.scalar.activation(out, out, ACT.Ln, bias=1.0)


def phase_gla(nc, m, d):
    with ExitStack() as ctx:
        sem = Semaphores(nc, "p4_")
        al = Bump(m, "p4_", m.HTO, m.CO)
        e_mid, e_neg, e_cum, e_last = (al(n, [P, ALL]) for n in ("e_mid", "e_neg", "e_cum", "e_last"))
        z, soft, cum = al("z", [P, ALL]), al("soft", [P, ALL]), al("cum", [P, ALL])
        keep = al("keep", [P, ALL])
        rel = soft
        al = Bump(m, "p4_", m.SCR, m.END)
        wg, bg = al("wg", [RANK, P]), al("bg", [P, 1])
        ke, qc, kd = (al(n, [P, 2, P]) for n in ("ke", "qc", "kd"))
        qbd, attm = al("qbd", [P, HA, P]), al("attm", [P, 2, HA, P])
        kdT, S, upd = al("kdT", [P, 2, P]), al("S", [P, 256]), al("upd", [P, 256])
        m.o = m.at("heads_o", [P, TT, 256], m.END - TT * 1024)
        al.end = m.END - TT * 1024
        S0 = al("S0", [P, NSEQ, 256])
        qz, vz = al("qz", [P, NSEQ, P]), al("vz", [P, NSEQ, 256])
        pz = [ctx.enter_context(nc.psum_tensor(f"p4_z{i}", [P, 512], F32)) for i in range(4)]
        pA, pK, pO, pS = (ctx.enter_context(nc.psum_tensor("p4_" + n, [P, 512], F32)) for n in "AKOS")

        par_in, s0_in, out = sem("par_in"), sem("s0_in"), sem("out")
        z_ready, soft_ready, cum_ready, exps_ready = sem("z_ready"), sem("soft_ready"), sem("cum_ready"), sem("exps_ready")
        dve_own, act_own, pool_own = sem("dve_own"), sem("act_own"), sem("pool_own")
        zb_ready, rel_ready = sem("zb_ready"), sem("rel_ready")
        oper_ready, att_ready, attm_ready, kdT_ready, kdT_copied = (sem(n) for n in (
            "oper_ready", "att_ready", "attm_ready", "kdT_ready", "kdT_copied"))
        o_ready, o_copied, upd_ready, state_ready = sem("o_ready"), sem("o_copied"), sem("upd_ready"), sem("state_ready")
        zeroed, state_done, vz_ready, sample_upd = sem("zeroed"), sem("state_done"), sem("vz_ready"), sem("sample_upd")
        spans = [(0, 512), (512, 1024), (1024, ALL)]
        tile = lambda ap, t: ap[:, ds(META + t * P, P)] if not isinstance(t, int) else ap[:, META + t * P:META + t * P + P]
        prompt = lambda ap: ap[:, META:PROMPT].rearrange("p (j t) -> p j t", t=P)
        sample = lambda ap: ap[:, PROMPT:ALL].rearrange("p (i t) -> p i t", t=SLEN)
        AQ, AK = m.fm[:, F_AQ, :], m.fm[:, F_AK, :]

        ctx.enter_context(sem)
        with nc.Block() as block:
            @block.sync
            def _(sp):
                sp.dma_start(wg[:, :], d["w_gla_gate"]).then_inc(par_in, 16)
                sp.dma_start(bg[:, :], d["b_gla_gate"]).then_inc(par_in, 16)
                sp.dma_start(S0[:, :, :], d["gla_bd"]).then_inc(s0_in, 16)
                sp.wait_ge(state_ready, 9)
                for h in range(HA):
                    sp.dma_start(d["p_gla"][h, :, :], S[DKA * h:DKA * h + DKA, DVA * h:DVA * h + DVA]).then_inc(out, 16)
                sp.wait_ge(state_done, 1)
                for h in range(HA):
                    sp.dma_start(d["s_gla"][h, :, :, :],
                                 S0[DKA * h:DKA * h + DKA, :, DVA * h:DVA * h + DVA]).then_inc(out, 16)
                sp.wait_ge(out, 16 * 2 * HA)

            @block.gpsimd
            def _(pool):
                nc.gpsimd.memset(qz[:, :, :], 0.0).then_inc(zeroed, 1)
                nc.gpsimd.tensor_tensor(vz[:, :, :], over(m.tm[:, SAMPLE, AV:AV + 256].unsqueeze(1), [P, NSEQ, 256]),
                                        over(cols(m, "seqmask").unsqueeze(2), [P, NSEQ, 256]),
                                        ALU.mult).then_inc(vz_ready, 1)

            @block.vector
            def _(dve):
                own = Chain(dve, dve_own)
                own.link(nc.vector.memset(keep[:, :], 1.0))
                own.link(nc.vector.memset(keep[:, 0:1], 0.0))
                own.link(nc.vector.memset(prompt(keep)[:, :, 0:1], 0.0))
                own.link(nc.vector.memset(sample(keep)[:, :, 0:1], 0.0))
                dve.wait_ge(soft_ready, 1)
                own.link(nc.vector.scalar_tensor_tensor(z[:, :], z[:, :], 0.0, soft[:, :], ALU.min, ALU.subtract))
                own.link(nc.vector.tensor_tensor_scan(cum[:, :], keep[:, :], z[:, :], 0.0, ALU.mult, ALU.add))
                nc.vector.tensor_tensor(prompt(rel), prompt(cum), over(prompt(cum)[:, :, 63:64], [P, NT, P]), ALU.subtract)
                nc.vector.tensor_tensor(sample(rel), sample(cum), over(sample(cum)[:, :, 7:8], [P, NSEQ, SLEN]), ALU.subtract)
                nc.vector.tensor_tensor(prompt(z), over(prompt(cum)[:, :, P - 1:P], [P, NT, P]), prompt(cum), ALU.subtract)
                nc.vector.tensor_tensor(z[:, 0:META], over(cum[:, META - 1:META], [P, META]), cum[:, 0:META], ALU.subtract)
                nc.vector.tensor_tensor(sample(z), over(sample(cum)[:, :, SLEN - 1:SLEN], [P, NSEQ, SLEN]), sample(cum),
                                        ALU.subtract).then_inc(rel_ready, 1)
                dve.wait_ge(exps_ready, 4)
                own.link(nc.vector.scalar_tensor_tensor(e_mid[:, META:ALL], AQ[:, META:ALL], DKA ** -0.5, e_mid[:, META:ALL],
                                                        ALU.mult, ALU.mult))

                own_n = own.k

                def operands(t, u, sampled=False):
                    nc.vector.tensor_tensor(ke[:, u, :], tile(AK, t), tile(e_neg, t), ALU.mult)
                    nc.vector.tensor_tensor(kd[:, u, :], tile(AK, t), tile(e_last, t), ALU.mult)
                    nc.vector.tensor_tensor(qbd[:, :, :], over(tile(e_mid, t).unsqueeze(1), [P, HA, P]),
                                            over(cols(m, "headA").unsqueeze(2), [P, HA, P]), ALU.mult)
                    if sampled:
                        out = bass.AP(qz, 0, [[NSEQ * P, P], [P + SLEN, NSEQ], [1, SLEN]])
                        i0, i1 = sample(AQ), sample(e_cum)
                    else:
                        out, i0, i1 = qc[:, u, :], tile(AQ, t), tile(e_cum, t)
                    nc.vector.scalar_tensor_tensor(out, i0, DKA ** -0.5, i1, ALU.mult, ALU.mult).then_inc(oper_ready, 1)

                nc.vector.tensor_tensor(kd[:, 0, 0:META], AK[:, 0:META], e_last[:, 0:META], ALU.mult).then_inc(oper_ready, 1)
                dve.wait_ge(upd_ready, 1)
                nc.vector.tensor_tensor(S[:, :], pS[:, 0:256], cols(m, "bdA"), ALU.mult).then_inc(state_ready, 1)
                with dve.Fori(0, NT // 2) as r:
                    for u in range(2):
                        t = 2 * r + u
                        operands(t, u)
                        dve.wait_ge(att_ready, t + 1)
                        nc.vector.tensor_tensor(attm[:, u, :, :], pA[:, :].rearrange("p (h t) -> p h t", h=HA),
                                                over(cols(m, "causal").unsqueeze(1), [P, HA, P]),
                                                ALU.mult).then_inc(attm_ready, 1)
                        dve.wait_ge(upd_ready, t + 2)
                        nc.vector.tensor_tensor(upd[:, :], pS[:, 0:256], cols(m, "bdA"), ALU.mult).then_inc(sample_upd, 1)
                        dve.wait_ge(sample_upd, t + 1)
                        dve.wait_ge(o_ready, t + 1)
                        nc.vector.scalar_tensor_tensor(S[:, :], S[:, :], e_cum[:, ds(META + t * P + (P - 1), 1)], upd[:, :],
                                                       ALU.mult, ALU.add).then_inc(state_ready, 1)
                dve.wait_ge(zeroed, 1)
                dve.wait_ge(s0_in, 16)
                operands(NT, 0, sampled=True)
                dve.wait_ge(att_ready, NT + 1)
                nc.vector.tensor_tensor(attm[:, 0, :, :], pA[:, :].rearrange("p (h t) -> p h t", h=HA),
                                        over(cols(m, "blocked").unsqueeze(1), [P, HA, P]), ALU.mult).then_inc(attm_ready, 1)
                dve.wait_ge(o_ready, NT + 1)
                dve.wait_ge(upd_ready, NT + 2)
                
                own = Chain(dve, dve_own, own_n)
                for i in range(NSEQ):
                    own.link(nc.vector.tensor_tensor(upd[:, :], pz[i // 2][:, 256 * (i % 2):256 * (i % 2) + 256],
                                                      cols(m, "bdA"), ALU.mult))
                    ins = nc.vector.scalar_tensor_tensor(S0[:, i, :], S0[:, i, :],
                                                         e_cum[:, PROMPT + SLEN * i + SLEN - 1:PROMPT + SLEN * i + SLEN],
                                                         upd[:, :], ALU.mult, ALU.add)
                    if i < NSEQ - 1:
                        own.link(ins)
                ins.then_inc(state_done, 1)

            @block.scalar
            def _(act):
                own = Chain(act, act_own)
                act.wait_ge(par_in, 32)
                for c, (a, b) in enumerate(spans):
                    act.wait_ge(z_ready, c + 1)
                    own.link(nc.scalar.activation(z[:, a:b], pz[c][:, 0:b - a], ACT.Identity, bias=bg[:, 0:1]))
                log_sigmoid_act(nc, act, own, soft[:, :], z[:, :]).then_inc(soft_ready, 1)
                act.wait_ge(rel_ready, 1)
                tau = 1.0 / 16.0
                nc.scalar.activation(e_mid[:, META:ALL], rel[:, META:ALL], ACT.Exp, scale=tau).then_inc(exps_ready, 1)
                nc.scalar.activation(e_neg[:, META:ALL], rel[:, META:ALL], ACT.Exp, scale=-tau).then_inc(exps_ready, 1)
                nc.scalar.activation(e_cum[:, :], cum[:, :], ACT.Exp, scale=tau).then_inc(exps_ready, 1)
                nc.scalar.activation(e_last[:, :], z[:, :], ACT.Exp, scale=tau).then_inc(exps_ready, 1)

                def copies(t, u, rows=P):
                    act.wait_ge(kdT_ready, t + 1)
                    nc.scalar.copy(kdT[0:rows, u, :], pK[0:rows, 0:P]).then_inc(kdT_copied, 1)

                copies(0, 0, META)
                with act.Fori(0, NT // 2) as r:
                    for u in range(2):
                        t = 2 * r + u
                        copies(t + 1, u)
                        act.wait_ge(o_ready, t + 1)
                        nc.scalar.copy(m.o[:, t, :], pO[:, 0:256]).then_inc(o_copied, 1)
                copies(NT + 1, 0)
                act.wait_ge(o_ready, NT + 1)
                nc.scalar.copy(m.o[:, NT, :], pO[:, 0:256]).then_inc(o_copied, 1)

            @block.tensor
            def _(pe):
                pe.wait_ge(par_in, 32)
                for c, (a, b) in enumerate(spans):
                    nc.tensor.matmul(pz[c][:, 0:b - a], wg[:, :], m.fm[0:RANK, F_MISC, a:b]).then_inc(z_ready, 1)

                def attend(t, u, first=False):
                    pe.wait_ge(oper_ready, t + 2)
                    if not first:
                        pe.wait_ge(attm_ready, t)
                    nc.tensor.matmul(pA[:, :], ke[:, u, :], qbd[:, :, :].rearrange("p h t -> p (h t)")).then_inc(att_ready, 1)
                    pe.wait_ge(kdT_copied, t + 1)
                    nc.tensor.transpose(pK[:, 0:P], kd[:, u, :], cols(m, "ident")).then_inc(kdT_ready, 1)

                def update(t, u):
                    pe.wait_ge(kdT_copied, t + 2)
                    pe.wait_ge(state_ready, t + 1)
                    nc.tensor.matmul(pS[:, 0:256], kdT[:, u, :], m.tm[:, t, AV:AV + 256]).then_inc(upd_ready, 1)

                def heads(t, u):
                    pe.wait_ge(attm_ready, t + 1)
                    for h in range(HA):
                        mm = nc.tensor.matmul(pO[:, DVA * h:DVA * h + DVA], attm[:, u, h, :],
                                              m.tm[:, t, AV + DVA * h:AV + DVA * h + DVA], start=False, stop=h == HA - 1,
                                              skip_group_check=True)
                    mm.then_inc(o_ready, 1)

                pe.wait_ge(oper_ready, 1)
                nc.tensor.transpose(pK[0:META, 0:P], kd[:, 0, 0:META], cols(m, "ident")).then_inc(kdT_ready, 1)
                pe.wait_ge(kdT_copied, 1)
                nc.tensor.matmul(pS[:, 0:256], kdT[0:META, 0, :], m.tm[0:META, MT, AV:AV + 256]).then_inc(upd_ready, 1)

                def prompt_tile(t, u, first=False):
                    attend(t, u, first)
                    pe.wait_ge(state_ready, t + 1)
                    if not first:
                        pe.wait_ge(o_copied, t)
                    nc.tensor.matmul(pO[:, 0:256], qc[:, u, :], S[:, :], start=True, stop=False, skip_group_check=True)
                    heads(t, u)
                    update(t, u)
                prompt_tile(0, 0, True)
                prompt_tile(1, 1)
                with pe.Fori(1, NT // 2) as r:
                    for u in range(2):
                        prompt_tile(2 * r + u, u)
                attend(NT, 0)
                pe.wait_ge(s0_in, 16)
                pe.wait_ge(o_copied, NT)
                for i in range(NSEQ):
                    nc.tensor.matmul(pO[:, 0:256], qz[:, i, :], S0[:, i, :], start=i == 0, stop=False, skip_group_check=True)
                heads(NT, 0)
                pe.wait_ge(kdT_copied, NT + 2)
                pe.wait_ge(vz_ready, 1)
                for j in range(NSEQ // 2):
                    mm = nc.tensor.matmul(pz[j][:, :], kdT[:, 0, :], vz[:, 2 * j:2 * j + 2, :].rearrange("p i c -> p (i c)"))
                mm.then_inc(upd_ready, 1)


def phase_head_norm(nc, m, d, tag, weight, gate, silu):
    with ExitStack() as ctx:
        sem = Semaphores(nc, tag)
        al = Bump(m, tag, m.HTO, m.CO)
        NH = TT * 4
        sq, sig = al("sq", [P, TT, 256]), al("sig", [P, TT, 256])
        g, mean, var = al("g", [P, 256]), al("mean", [P, NH]), al("var", [P, NH])
        g_in, dve_own, act_own = sem("g_in"), sem("dve_own"), sem("act_own")
        var_ready, rstd_ready, sig_ready = sem("var_ready"), sem("rstd_ready"), sem("sig_ready")
        oh = m.o[:, :, :].rearrange("p t (h v) -> p (t h) v", v=64)
        sh = sq[:, :, :].rearrange("p t (h v) -> p (t h) v", v=64)
        each = lambda ap: over(ap.unsqueeze(2), [P, NH, 64])
        r = m.tm[:, 0:TT, gate:gate + 256]
        ctx.enter_context(sem)
        with nc.Block() as block:
            @block.sync
            def _(sp):
                sp.dma_start(g[:, :], d[weight].partition_broadcast(P)).then_inc(g_in, 16)

            @block.vector
            def _(dve):
                own = Chain(dve, dve_own)
                own.link(nc.vector.tensor_reduce(mean[:, :], oh, AX.X, ALU.add))
                own.link(nc.vector.tensor_scalar(mean[:, :], mean[:, :], 1.0 / 64, None, ALU.mult))
                own.link(nc.vector.tensor_tensor(oh, oh, each(mean[:, :]), ALU.subtract))
                own.link(nc.vector.tensor_tensor(sh, oh, oh, ALU.mult))
                own.link(nc.vector.tensor_reduce(var[:, :], sh, AX.X, ALU.add))
                nc.vector.tensor_scalar(var[:, :], var[:, :], 1.0 / 64, EPS, ALU.mult, ALU.add).then_inc(var_ready, 1)
                dve.wait_ge(rstd_ready, 1)
                own.link(nc.vector.tensor_tensor(oh, oh, each(var[:, :]), ALU.mult))
                dve.wait_ge(g_in, 16)
                own.link(nc.vector.tensor_tensor(m.o[:, :, :], m.o[:, :, :], over(g[:, :].unsqueeze(1), [P, TT, 256]), ALU.mult))
                dve.wait_ge(sig_ready, 1)
                if silu:
                    own.link(nc.vector.tensor_tensor(m.o[:, :, :], m.o[:, :, :], r, ALU.mult))
                own.link(nc.vector.tensor_tensor(r, m.o[:, :, :], sig[:, :, :], ALU.mult))

            @block.scalar
            def _(act):
                own = Chain(act, act_own)
                own.link(nc.scalar.activation(sig[:, :, :], r, ACT.Exp, scale=-1.0))
                own.link(nc.scalar.activation(sig[:, :, :], sig[:, :, :], ACT.Ln, bias=1.0))
                nc.scalar.activation(sig[:, :, :], sig[:, :, :], ACT.Exp, scale=-1.0).then_inc(sig_ready, 1)
                act.wait_ge(var_ready, 1)
                own.link(nc.scalar.activation(var[:, :], var[:, :], ACT.Ln))
                nc.scalar.activation(var[:, :], var[:, :], ACT.Exp, scale=-0.5).then_inc(rstd_ready, 1)


def phase_norm_gla(nc, m, d):
    phase_head_norm(nc, m, d, "p4n_", "g_gla_norm", AR, True)


def phase_norm_mlstm(nc, m, d):
    phase_head_norm(nc, m, d, "p5n_", "g_mlstm_norm", BO, False)


def phase_mlstm(nc, m, d):
    with ExitStack() as ctx:
        sem = Semaphores(nc, "p5_")
        nlast, mlast = m.at("p5_nlast", [P, 2, NSEQ], m.HTO + 7 * ALL * 4 + 3264), m.at("p5_mlast", [P, NSEQ + 1], m.HTO + 7 * ALL * 4 + 3328)
        VE = DVA + 1
        al = Bump(m, "p5_", m.HTO, m.CO)
        t1, t2, cum, M, gates, keep, drop = (al(n, [P, ALL]) for n in ("t1", "t2", "cum", "M", "gates", "keep", "drop"))
        gtm = al("gtm", [P, TT + 1, 4, HB])
        slf, slb = al("slf", [P, 17]), al("slb", [P, 2, 17])
        m0, bfg = al("m0", [P, NSEQ]), al("bfg", [P, 1])
        al = Bump(m, "p5_", m.SCR, m.END - TT * 1024)
        vx, C0 = al("vx", [P, TT + 1, HB, VE]), al("C0", [P, 2, NSEQ, 2 * VE])
        vz, qz = al("vz", [P, NSEQ, HB * VE]), al("qz", [P, 2, NSEQ, P])
        al = Bump(m, "p5_", m.FMO, m.FMO + 2 * ALL * 4)
        kr, qr, qbd = al("kr", [P, 2, P]), al("qr", [P, 2, P]), al("qbd", [P, 2, 2, P])
        W, kw = al("W", [P, HB, P]), al("kw", [P, 256])
        tot, C = al("tot", [P, HB, VE]), al("C", [P, 2, 2 * VE])
        upd, den = m.at("p5_upd", [P, 2, 2 * VE], m.HTO + 7 * ALL * 4 + 2048), m.at("p5_den", [P, HB], m.HTO + 7 * ALL * 4 + 3200)
        assert m.HTO + 7 * ALL * 4 + 3400 <= m.CO
        pA, pM, pK, pI, pN, pC, pX, pY = (ctx.enter_context(nc.psum_tensor("p5_" + n, [P, 512], F32)) for n in "AMKINCXY")
        (par_in, c0_in, out, dve_own, act_own, raw_ready, soft_ready, arg_ready, gates_ready, turned, gtm_ready,
         sl_ready, slb_ready, oper_ready, prod_ready, d_ready, w_ready, masked, pm_ready, kw_ready, inter_ready,
         h_ready, num_ready, upd_ready, state_ready, zeroed, vz_ready, kT_ready, m_ready) = (sem(n) for n in (
            "par_in c0_in out dve_own act_own raw_ready soft_ready arg_ready gates_ready turned gtm_ready sl_ready "
            "slb_ready oper_ready prod_ready d_ready w_ready masked pm_ready kw_ready inter_ready h_ready num_ready "
            "upd_ready state_ready zeroed vz_ready kT_ready m_ready").split())
        prompt = lambda ap: ap[:, META:PROMPT].rearrange("p (j t) -> p j t", t=P)
        sample = lambda ap: ap[:, PROMPT:ALL].rearrange("p (i t) -> p i t", t=SLEN)
        H = lambda ap: ap[0:HB, :]
        span = lambda t: ds(META + t * P, P)
        banks = (pA, pM, pK)
        STEPS = 12
        pair_bank = lambda i, p: (pA, pM, pK, pC, pX, pY)[(2 * i + p) // 3][:, 2 * VE * ((2 * i + p) % 3):2 * VE * ((2 * i + p) % 3 + 1)]

        ctx.enter_context(sem)
        with nc.Block() as block:
            @block.sync
            def _(sp):
                sp.dma_start(m0[0:HB, :], d["m0"]).then_inc(par_in, 16)
                sp.dma_start(bfg[ROW_F:ROW_F + HB, :], d["b_forget"]).then_inc(par_in, 16)
                sp.dma_start(C0[:, :, :, :], d["mlstm_bd"]).then_inc(c0_in, 16)
                sp.wait_ge(m_ready, 1)
                sp.dma_start(d["p_m"], mlast[0:HB, NSEQ:NSEQ + 1]).then_inc(out, 16)
                sp.dma_start(d["s_m"], mlast[0:HB, 0:NSEQ]).then_inc(out, 16)
                sp.wait_ge(state_ready, NT + 1)
                for h in range(HB):
                    rows = slice(64 * (h % 2), 64 * (h % 2) + 64)
                    c = VE * (h % 2)
                    sp.dma_start(d["p_c"][h, :, :], C[rows, h // 2, c:c + 64]).then_inc(out, 16)
                    sp.dma_start(d["p_n"][h:h + 1, :].rearrange("a k -> k a"), C[rows, h // 2, c + 64:c + 65]).then_inc(out, 16)
                sp.wait_ge(state_ready, NT + 2)
                for h in range(HB):
                    rows = slice(64 * (h % 2), 64 * (h % 2) + 64)
                    c = VE * (h % 2)
                    sp.dma_start(d["s_c"][h, :, :, :], C0[rows, h // 2, :, c:c + 64]).then_inc(out, 16)
                    sp.dma_start(d["s_n"][h, :, :], nlast[rows, h // 2, :]).then_inc(out, 16)
                sp.wait_ge(out, 16 * (2 + 4 * HB))

            @block.gpsimd
            def _(pool):
                nc.gpsimd.memset(qz[:, :, :, :], 0.0).then_inc(zeroed, 1)
                nc.gpsimd.memset(vx[:, :, :, :], 1.0).then_inc(zeroed, 1)
                pool.wait_ge(zeroed, 2)
                nc.gpsimd.tensor_copy(vx[:, 0:TT, :, 0:DVA],
                                      m.tm[:, 0:TT, BV:BV + 256].rearrange("p t (h v) -> p t h v", v=DVA)).then_inc(zeroed, 1)
                nc.gpsimd.tensor_copy(vx[0:META, MT, :, 0:DVA],
                                      m.tm[0:META, MT, BV:BV + 256].rearrange("p (h v) -> p h v", v=DVA)).then_inc(zeroed, 1)
                pool.wait_ge(zeroed, 4)
                nc.gpsimd.tensor_tensor(vz[:, :, :], over(vx[:, SAMPLE, :, :].rearrange("p h v -> p (h v)").unsqueeze(1),
                                                          [P, NSEQ, HB * VE]),
                                        over(cols(m, "seqmask").unsqueeze(2), [P, NSEQ, HB * VE]),
                                        ALU.mult).then_inc(vz_ready, 1)

                def mask(t, which):
                    pool.wait_ge(w_ready, t + 1)
                    nc.gpsimd.tensor_tensor(W[:, :, :], W[:, :, :], over(cols(m, which).unsqueeze(1), [P, HB, P]),
                                            ALU.mult).then_inc(masked, 1)
                with pool.Fori(0, NT) as t:
                    mask(t, "causal")
                mask(NT, "blocked")

            @block.vector
            def _(dve):
                own = Chain(dve, dve_own)
                own.link(nc.vector.memset(gates[:, :], 0.0))
                own.link(nc.vector.memset(H(keep), 1.0))
                own.link(nc.vector.memset(sample(keep)[0:HB, :, 0:1], 0.0))
                own.link(nc.vector.memset(H(drop), 0.0))
                nc.vector.memset(sample(drop)[0:HB, :, 0:1], NEG).then_inc(raw_ready, 1)
                dve.wait_ge(soft_ready, 1)
                own.link(nc.vector.scalar_tensor_tensor(H(t1), H(t1), 0.0, H(t2), ALU.min, ALU.subtract))
                own.link(nc.vector.tensor_tensor_scan(H(cum), H(keep), H(t1), 0.0, ALU.mult, ALU.add))
                own.link(nc.vector.tensor_tensor(H(gates), H(gates), H(cum), ALU.subtract))
                own.link(nc.vector.tensor_copy(H(t2), H(gates)))
                own.link(nc.vector.tensor_scalar(t2[0:HB, 0:1], t2[0:HB, 0:1], 0.0, None, ALU.max))
                dve.wait_ge(par_in, 32)
                own.link(nc.vector.tensor_tensor(sample(t2)[0:HB, :, 0], sample(t2)[0:HB, :, 0], m0[0:HB, :], ALU.max))
                own.link(nc.vector.tensor_tensor_scan(H(M), H(drop), H(t2), NEG, ALU.add, ALU.max))
                own.link(nc.vector.tensor_tensor(t1[0:HB, 0:META], gates[0:HB, 0:META], over(M[0:HB, META - 1:META], [HB, META]),
                                                 ALU.subtract))
                own.link(nc.vector.tensor_tensor(prompt(t1)[0:HB], prompt(gates)[0:HB],
                                                 over(prompt(M)[0:HB, :, P - 1:P], [HB, NT, P]), ALU.subtract))
                own.link(nc.vector.tensor_tensor(sample(t1)[0:HB], sample(gates)[0:HB],
                                                 over(sample(M)[0:HB, :, SLEN - 1:SLEN], [HB, NSEQ, SLEN]), ALU.subtract))
                own.link(nc.vector.tensor_scalar(keep[0:HB, 0:META], M[0:HB, 0:META], -1.0, None, ALU.mult))
                before = M[0:HB, META - 1:META - 1 + SEQ].rearrange("p (j t) -> p j t", t=P)[:, :, 0:1]
                own.link(nc.vector.tensor_tensor(prompt(keep)[0:HB], over(before, [HB, NT, P]), prompt(M)[0:HB], ALU.subtract))
                own.link(nc.vector.tensor_tensor(sample(keep)[0:HB], over(m0[0:HB, :].unsqueeze(2), [HB, NSEQ, SLEN]),
                                                 sample(M)[0:HB], ALU.subtract))
                own.link(nc.vector.tensor_copy(slf[0:HB, 0:1], keep[0:HB, META - 1:META]))
                own.link(nc.vector.tensor_copy(slf[0:HB, 1:9], prompt(keep)[0:HB, :, P - 1]))
                own.link(nc.vector.tensor_copy(slf[0:HB, 9:17], sample(keep)[0:HB, :, SLEN - 1]))
                own.link(nc.vector.tensor_tensor(H(t2), H(M), H(cum), ALU.add))
                nc.vector.tensor_copy(mlast[0:HB, NSEQ:NSEQ + 1], t2[0:HB, PROMPT - 1:PROMPT]).then_inc(arg_ready, 1)
                nc.vector.tensor_copy(mlast[0:HB, 0:NSEQ], sample(t2)[0:HB, :, SLEN - 1]).then_inc(m_ready, 1)
                for g in range(3):
                    dve.wait_ge(turned, g + 1)
                    n = min(4, TT + 1 - 4 * g)
                    src = banks[g][:, :].rearrange("p (t k c) -> p t k c", t=4, k=4)
                    nfull = min(n, TT - 4 * g)
                    own.link(nc.vector.tensor_copy(gtm[:, 4 * g:4 * g + nfull, :, :], src[:, 0:nfull, :, 0:HB]))
                own.link(nc.vector.tensor_copy(gtm[0:META, MT, :, :], src[0:META, 1, :, 0:HB]))
                dve.wait_ge(sl_ready, 1)
                nc.vector.tensor_copy(slb[:, :, :], pX[:, 0:34].rearrange("p (a b) -> p a b", a=2)).then_inc(gtm_ready, 1)
                dve.wait_ge(gtm_ready, 1)

                head = lambda ap: over(ap.unsqueeze(2), [ap.shape[0], HB, 64])
                heads4 = lambda ap: ap.rearrange("p (h v) -> p h v", v=64)
                bd = over(cols(m, "bdB").unsqueeze(1), [P, 2, 2 * VE])
                kwt = kw[:, :]

                nc.vector.tensor_copy(kr[:, :, 0:META], m.fm[:, F_BK:F_BK + 2, 0:META]).then_inc(oper_ready, 1)
                dve.wait_ge(kT_ready, 1)
                nc.vector.tensor_tensor(heads4(kw[0:META, :]), heads4(pK[0:META, 0:256]), head(gtm[0:META, MT, 1, :]),
                                        ALU.mult).then_inc(kw_ready, 1)
                dve.wait_ge(upd_ready, 1)
                nc.vector.tensor_tensor(C[:, :, :], pC[:, 0:4 * VE].rearrange("p (a b) -> p a b", a=2), bd,
                                        ALU.mult).then_inc(state_ready, 1)

                def tile(t, own, sampled):
                    sl = span(t)
                    own.link(nc.vector.tensor_copy(kr[:, :, :], m.fm[:, F_BK:F_BK + 2, sl]))
                    if sampled:
                        for p in range(2):
                            own.link(nc.vector.tensor_copy(bass.AP(qz, p * NSEQ * P, [[2 * NSEQ * P, P], [P + SLEN, NSEQ], [1, SLEN]]),
                                                           sample(m.fm[:, F_BQ + p, :])))
                    else:
                        own.link(nc.vector.tensor_copy(qr[:, :, :], m.fm[:, F_BQ:F_BQ + 2, sl]))
                    for p in range(2):
                        ins = nc.vector.tensor_tensor(qbd[:, p, :, :], over(m.fm[:, F_BQ + p, sl].unsqueeze(1), [P, 2, P]),
                                                      over(cols(m, "headB").unsqueeze(2), [P, 2, P]), ALU.mult)
                        if p == 0:
                            own.link(ins)
                    ins.then_inc(oper_ready, 1)
                    dve.wait_ge(prod_ready, t + 1)
                    own.link(nc.vector.tensor_tensor(W[:, :, :], over(gtm[:, t, 0, :].unsqueeze(2), [P, HB, P]),
                                                     pM[:, :].rearrange("p (h t) -> p h t", h=HB), ALU.subtract))
                    nc.vector.tensor_scalar(W[:, :, :], W[:, :, :], 0.0, None, ALU.min).then_inc(d_ready, 1)
                    dve.wait_ge(kT_ready, t + 2)
                    nc.vector.tensor_tensor(heads4(kwt), heads4(pK[:, 0:256]), head(gtm[:, t, 1, :]), ALU.mult).then_inc(kw_ready, 1)
                    dve.wait_ge(masked, t + 1)
                    nc.vector.tensor_tensor(W[:, :, :], W[:, :, :], pA[:, :].rearrange("p (h t) -> p h t", h=HB),
                                            ALU.mult).then_inc(pm_ready, 1)
                    dve.wait_ge(inter_ready, t + 1)
                    own.link(nc.vector.tensor_tensor(tot[:, :, :], pI[:, 0:4 * VE].rearrange("p (h v) -> p h v", v=VE),
                                                     over(gtm[:, t, 2, :].unsqueeze(2), [P, HB, VE]), ALU.mult))
                    dve.wait_ge(num_ready, t + 1)
                    own.link(nc.vector.tensor_tensor(tot[:, :, :], tot[:, :, :], pN[:, 0:4 * VE].rearrange("p (h v) -> p h v", v=VE),
                                                     ALU.add))
                    own.link(nc.vector.scalar_tensor_tensor(den[:, :], tot[:, :, DVA], -1.0, tot[:, :, DVA], ALU.mult, ALU.max))
                    own.link(nc.vector.tensor_tensor(den[:, :], den[:, :], gtm[:, t, 3, :], ALU.max))
                    own.link(nc.vector.reciprocal(den[:, :], den[:, :]))
                    own.link(nc.vector.tensor_tensor(heads4(m.o[:, t, :]), tot[:, :, 0:DVA], head(den[:, :]), ALU.mult))
                    if sampled:
                        nc.vector.tensor_copy(upd[:, 0, 0:1], den[:, 0:1]).then_inc(h_ready, 1)
                    dve.wait_ge(upd_ready, t + 2)
                first = own.k
                with dve.Fori(0, NT) as t:
                    own = Chain(dve, dve_own, first + STEPS * t)
                    tile(t, own, False)
                    own.link(nc.vector.tensor_tensor(upd[:, :, :], pC[:, 0:4 * VE].rearrange("p (a b) -> p a b", a=2), bd, ALU.mult))
                    own.link(nc.vector.scalar_tensor_tensor(C[:, 0, :], C[:, 0, :], slb[:, 0, ds(t + 1, 1)], upd[:, 0, :],
                                                            ALU.mult, ALU.add))
                    nc.vector.scalar_tensor_tensor(C[:, 1, :], C[:, 1, :], slb[:, 1, ds(t + 1, 1)], upd[:, 1, :],
                                                   ALU.mult, ALU.add).then_inc(state_ready, 1)
                    dve.wait_ge(state_ready, t + 2)
                    own.steps(STEPS)
                own = Chain(dve, dve_own, first + STEPS * NT)
                dve.wait_ge(zeroed, 4)
                tile(NT, own, True)
                dve.wait_ge(c0_in, 16)
                cell = over(cols(m, "bdB"), [P, 2 * VE])
                for i in range(NSEQ):
                    for p in range(2):
                        n = 2 * i + p
                        own.link(nc.vector.tensor_tensor(upd[:, p, :], pair_bank(i, p), cell, ALU.mult))
                        own.link(nc.vector.scalar_tensor_tensor(C0[:, p, i, :], C0[:, p, i, :], slb[:, p, 9 + i:10 + i], upd[:, p, :],
                                                                ALU.mult, ALU.add))
                own.link(nc.vector.tensor_copy(nlast[0:64, :, :], C0[0:64, :, :, DVA]))
                nc.vector.tensor_copy(nlast[64:P, :, :], C0[64:P, :, :, 2 * VE - 1]).then_inc(state_ready, 1)

            @block.scalar
            def _(act):
                own = Chain(act, act_own)
                act.wait_ge(raw_ready, 1)
                act.wait_ge(par_in, 32)
                own.link(nc.scalar.activation(H(t1), m.fm[ROW_F:ROW_F + HB, F_MISC, :], ACT.Identity, bias=bfg[ROW_F:ROW_F + HB, :]))
                own.link(nc.scalar.copy(H(gates), m.fm[ROW_I:ROW_I + HB, F_MISC, :]))
                log_sigmoid_act(nc, act, own, H(t2), H(t1)).then_inc(soft_ready, 1)
                act.wait_ge(arg_ready, 1)
                nc.scalar.activation(gates[32:32 + HB, :], H(t1), ACT.Exp).then_inc(gates_ready, 1)
                nc.scalar.activation(gates[64:64 + HB, :], H(keep), ACT.Exp).then_inc(gates_ready, 1)
                nc.scalar.activation(gates[96:96 + HB, :], H(t2), ACT.Exp, scale=-1.0).then_inc(gates_ready, 1)
                nc.scalar.activation(slf[0:HB, :], slf[0:HB, :], ACT.Exp).then_inc(gates_ready, 1)
                with act.Fori(0, TT) as t:
                    act.wait_ge(d_ready, t + 1)
                    nc.scalar.activation(W[:, :, :], W[:, :, :], ACT.Exp).then_inc(w_ready, 1)

            @block.tensor
            def _(pe):
                pe.wait_ge(gates_ready, 4)
                for g in range(3):
                    for t in range(4 * g, min(4 * g + 4, TT)):
                        mm = nc.tensor.transpose(banks[g][:, P * (t % 4):P * (t % 4) + P], gates[:, META + t * P:META + t * P + P],
                                                 cols(m, "ident"))
                    if g == 2:
                        mm = nc.tensor.transpose(banks[g][0:META, P:2 * P], gates[:, 0:META], cols(m, "ident"))
                    mm.then_inc(turned, 1)
                for p in range(2):
                    mm = nc.tensor.matmul(pX[:, 17 * p:17 * p + 17], cols(m, "selB")[0:HB, P * p:P * p + P], slf[0:HB, :])
                mm.then_inc(sl_ready, 1)

                def keys(t, rows=P):
                    for p in range(2):
                        mm = nc.tensor.transpose(pK[0:rows, P * p:P * p + P], kr[:, p, 0:rows], cols(m, "ident"))
                    mm.then_inc(kT_ready, 1)

                pe.wait_ge(gtm_ready, 1)
                pe.wait_ge(oper_ready, 1)
                keys(-1, META)
                pe.wait_ge(kw_ready, 1)
                pe.wait_ge(zeroed, 4)
                for p in range(2):
                    mm = nc.tensor.matmul(pC[:, 2 * VE * p:2 * VE * (p + 1)], kw[0:META, P * p:P * p + P],
                                          vx[0:META, MT, 2 * p:2 * p + 2, :].rearrange("p h v -> p (h v)"))
                mm.then_inc(upd_ready, 1)

                def scores(t):
                    pe.wait_ge(oper_ready, t + 2)
                    pe.wait_ge(state_ready, t + 1)
                    for h in range(HB):
                        nc.tensor.matmul(pM[:, P * h:P * h + P], cols(m, "selM")[0:HB, P * h:P * h + P], M[0:HB, span(t)])
                    for p in range(2):
                        mm = nc.tensor.matmul(pA[:, 256 * p:256 * p + 256], kr[:, p, :],
                                              qbd[:, p, :, :].rearrange("p h t -> p (h t)"))
                    mm.then_inc(prod_ready, 1)
                    keys(t)

                def numerators(t):
                    pe.wait_ge(pm_ready, t + 1)
                    for h in range(HB):
                        mm = nc.tensor.matmul(pN[:, VE * h:VE * h + VE], W[:, h, :], vx[:, t, h, :])
                    mm.then_inc(num_ready, 1)

                with pe.Fori(0, NT) as t:
                    scores(t)
                    for p in range(2):
                        mm = nc.tensor.matmul(pI[:, 2 * VE * p:2 * VE * (p + 1)], qr[:, p, :], C[:, p, :])
                    mm.then_inc(inter_ready, 1)
                    pe.wait_ge(kw_ready, t + 2)
                    numerators(t)
                    for p in range(2):
                        mm = nc.tensor.matmul(pC[:, 2 * VE * p:2 * VE * (p + 1)], kw[:, P * p:P * p + P],
                                              vx[:, t, 2 * p:2 * p + 2, :].rearrange("p h v -> p (h v)"))
                    mm.then_inc(upd_ready, 1)
                scores(NT)
                pe.wait_ge(c0_in, 16)
                for p in range(2):
                    for i in range(NSEQ):
                        mm = nc.tensor.matmul(pI[:, 2 * VE * p:2 * VE * (p + 1)], qz[:, p, i, :], C0[:, p, i, :],
                                              start=i == 0, stop=i == NSEQ - 1)
                mm.then_inc(inter_ready, 1)
                numerators(NT)
                pe.wait_ge(kw_ready, NT + 2)
                pe.wait_ge(vz_ready, 1)
                pe.wait_ge(h_ready, 1)
                for i in range(NSEQ):
                    for p in range(2):
                        mm = nc.tensor.matmul(pair_bank(i, p), kw[:, P * p:P * p + P], vz[:, i, 2 * VE * p:2 * VE * (p + 1)])
                mm.then_inc(upd_ready, 1)


def spans_of(n):
    parts = -(-n // 512)
    width = -(-n // parts // 16) * 16
    return [(a, min(a + width, n)) for a in range(0, n, width)]


def phase_dsa(nc, m, d):
    with ExitStack() as ctx:
        sem = Semaphores(nc, "p6_")
        SK = 2 * P
        NK = [META + P * (t + 1) for t in range(NT)] + [SK]
        GQ = HC // KVC
        al = Bump(m, "p6_", m.HTO, m.CO)
        qz, qiz = al("qz", [P, 4, NSEQ, P]), al("qiz", [P, NSEQ, P])
        kC, kiC, vC = al("kC", [P, NSEQ, P]), al("kiC", [P, NSEQ, P]), al("vC", [P, NSEQ, P])
        al = Bump(m, "p6_", m.SCR, m.END)
        score, work, bias = al("score", [P, PROMPT]), al("work", [P, PROMPT]), al("bias", [P, PROMPT])
        relu, logit = al("relu", [P, 2, 512]), al("logit", [P, 2, PROMPT])
        pT = al("pT", [P, 2, NT + 1, P])
        top, pmax, nmax, total, rden = (al(n, s) for n, s in (("top", [P, 8]), ("pmax", [P, 2, 4]), ("nmax", [P, 2]),
                                                               ("total", [P, 2, HC]), ("rden", [P, HC])))
        pTz = m.at("p6_pTz", [P, NSEQ, P], m.FMO)
        pR = [ctx.enter_context(nc.psum_tensor(f"p6_R{i}", [P, 512], F32)) for i in range(2)]
        pL = [ctx.enter_context(nc.psum_tensor(f"p6_L{i}", [P, 512], F32)) for i in range(3)]
        pP = [ctx.enter_context(nc.psum_tensor(f"p6_P{i}", [P, 4, P], F32)) for i in range(2)]
        pO = ctx.enter_context(nc.psum_tensor("p6_O", [P, 512], F32))

        (caches_in, zeroed, qz_ready, raw_ready, relu_ready, relu_used, dve_own, round_own, bias_ready, logit_ready,
         masked, nmax_ready, exp_ready, turned, pT_copied, o_ready, o_used, act_own) = (sem(n) for n in (
            "caches_in zeroed qz_ready raw_ready relu_ready relu_used dve_own round_own bias_ready logit_ready "
            "masked nmax_ready exp_ready turned pT_copied o_ready o_used act_own").split())
        q_cols = lambda t: slice(META + P * t, META + P * t + P)
        kv_rows = lambda h: slice(64 * (h // GQ), 64 * (h // GQ) + 64)
        i_rows = lambda h: slice(DI * h, DI * h + DI)

        def key_spans(t):
            return spans_of(NK[t]) if t < NT else [(0, SK)]

        raws = [(t, s, h) for t in range(TT) for s in range(len(key_spans(t))) for h in range(HI)]
        heads = [(t, h) for t in range(TT) for h in range(HC)]
        logits = [(t, h, s) for t, h in heads for s in range(len(key_spans(t)))]
        n_logits = {(t, h): sum(1 for x in logits if x[:2] <= (t, h)) for t, h in heads}

        def blocks(t):
            return [(META + P * j, P) for j in range(t + 1)] + [(0, META)] if t < NT else [(0, P), (P, P)]
        groups = [(n, g) for n, (t, h) in enumerate(heads) for g in range(-(-len(blocks(t)) // 4))]

        ctx.enter_context(sem)
        with nc.Block() as block:
            @block.sync
            def _(sp):
                sp.dma_start(kC[:, :, :], d["kT_cache"]).then_inc(caches_in, 16)
                sp.dma_start(kiC[:, :, :], d["kiT_cache"]).then_inc(caches_in, 16)
                sp.dma_start(vC[:, :, :], d["v_cache"]).then_inc(caches_in, 16)
                sp.wait_ge(caches_in, 48)

            @block.gpsimd
            def _(pool):
                nc.gpsimd.memset(pTz[:, :, :], 0.0).then_inc(zeroed, 1)
                nc.gpsimd.memset(qiz[:, :, :], 0.0).then_inc(zeroed, 1)
                nc.gpsimd.memset(qz[:, :, :, :], 0.0).then_inc(zeroed, 1)
                pool.wait_ge(zeroed, 3)
                own = lambda ap: ap[:, PROMPT:ALL].rearrange("p (i t) -> p i t", t=SLEN)
                for c in range(4):
                    nc.gpsimd.tensor_copy(bass.AP(qz, c * NSEQ * P, [[4 * NSEQ * P, P], [P + SLEN, NSEQ], [1, SLEN]]),
                                          own(m.fm[:, F_CQ + c, :])).then_inc(qz_ready, 1)
                nc.gpsimd.tensor_copy(bass.AP(qiz, 0, [[NSEQ * P, P], [P + SLEN, NSEQ], [1, SLEN]]),
                                      own(m.fm[:, F_QI, :])).then_inc(qz_ready, 1)

            def finish(dve, own, t):
                dve.wait_ge(o_ready, (t + 1) * HC)
                own.link(nc.vector.reciprocal(rden[:, :], total[:, t % 2, :]))
                for c, first in ((AV, 0), (BV, GQ)):
                    ins = nc.vector.tensor_tensor(m.tm[:, t, c:c + 256].rearrange("p (h v) -> p h v", v=64),
                                                  pO[:, 64 * first:64 * first + 256].rearrange("p (h v) -> p h v", v=64),
                                                  over(rden[:, first:first + GQ].unsqueeze(2), [P, GQ, 64]), ALU.mult)
                    ins.then_inc(o_used, 1)
                dve.wait_ge(o_used, 2 * t + 2)

            @block.vector
            def _(dve):
                own = Chain(dve, dve_own)
                n_raw = n_log = 0
                for t in range(TT):
                    N = NK[t]
                    for a, b in key_spans(t):
                        for h in range(HI):
                            n_raw += 1
                            dve.wait_ge(relu_ready, n_raw)
                            w = m.tm[:, t, CW + h:CW + h + 1]
                            r = relu[:, h % 2, 0:b - a]
                            if h == 0:
                                ins = nc.vector.tensor_scalar(score[:, a:b], r, w, None, ALU.mult)
                            else:
                                ins = nc.vector.scalar_tensor_tensor(score[:, a:b], r, w, score[:, a:b], ALU.mult, ALU.add)
                            ins.then_inc(relu_used, 1)
                            dve.wait_ge(relu_used, n_raw)
                    K, extra = TOPK_P, 0
                    if t < NT:
                        own.link(nc.vector.memset(score[0:64, N - 64:N], NEG))
                    else:
                        K, extra = TOPK_S, 4
                        own.link(nc.vector.memset(score[:, N:N + extra], 3e38))
                        own.link(nc.vector.tensor_tensor(score[:, P:N], score[:, P:N], cols(m, "otherseq"), ALU.add))
                    if N > K:
                        n = (K + extra) // 8
                        src = score[:, 0:N + extra]
                        dst = work[:, 0:N + extra]
                        own.link(nc.vector.max(top[:, :], src))
                        own.link(nc.vector.match_replace(dst, top[:, :], src, TAKEN))

                        def a_round(k):
                            nc.vector.max(top[:, :], dst).then_inc(round_own, 1)
                            dve.wait_ge(round_own, 2 * k + 1)
                            nc.vector.match_replace(dst, top[:, :], dst, TAKEN).then_inc(round_own, 1)
                            dve.wait_ge(round_own, 2 * k + 2)
                        if n > 8:
                            for k in range(7):
                                a_round(k)
                            nc.vector.sem_clear(round_own)
                            with dve.Fori(0, (n - 8) // 8) as r:
                                for k in range(8):
                                    a_round(k)
                                nc.vector.sem_clear(round_own)
                        else:
                            for k in range(n - 1):
                                a_round(k)
                            nc.vector.sem_clear(round_own)
                        own.link(nc.vector.tensor_scalar(bias[:, 0:N], work[:, 0:N], TAKEN, NEG, ALU.not_equal, ALU.mult))
                    else:
                        own.link(nc.vector.memset(bias[:, 0:N], 0.0))
                    if t < NT:
                        own.link(nc.vector.memset(bias[0:64, N - 64:N], NEG))
                    else:
                        own.link(nc.vector.tensor_tensor(bias[:, P:N], bias[:, P:N], cols(m, "otherseq"), ALU.add))
                    for h in range(HC):
                        g = t * HC + h
                        if g >= 2:
                            dve.wait_ge(exp_ready, g - 1)
                            dve.wait_ge(turned, sum(1 for x in groups if x[0] <= g - 2))
                        ks = key_spans(t)
                        for s, (a, b) in enumerate(ks):
                            dve.wait_ge(logit_ready, n_log + 1)
                            nc.vector.tensor_tensor_reduce(logit[:, g % 2, a:b], pL[n_log % 3][:, 0:b - a], bias[:, a:b], 1.0,
                                                           -3e38, ALU.add, ALU.max, pmax[:, g % 2, s:s + 1]).then_inc(masked, 1)
                            n_log += 1
                        dve.wait_ge(masked, n_log)
                        if len(ks) > 1:
                            own.link(nc.vector.tensor_reduce(pmax[:, g % 2, 3:4], pmax[:, g % 2, 0:len(ks)], AX.X, ALU.max))
                            top_col = 3
                        else:
                            top_col = 0
                        nc.vector.tensor_scalar(nmax[:, g % 2:g % 2 + 1], pmax[:, g % 2, top_col:top_col + 1], -DHC ** -0.5, None,
                                                ALU.mult).then_inc(nmax_ready, 1)
                        if h == 1 and t > 0:
                            finish(dve, own, t - 1)
                finish(dve, own, TT - 1)

            @block.scalar
            def _(act):
                n_raw = 0

                def relus(t):
                    nonlocal n_raw
                    for a, b in key_spans(t):
                        for h in range(HI):
                            act.wait_ge(raw_ready, n_raw + 1)
                            if n_raw >= 2:
                                act.wait_ge(relu_used, n_raw - 1)
                            nc.scalar.activation(relu[:, h % 2, 0:b - a], pR[h % 2][:, 0:b - a], ACT.Relu,
                                                 scale=DI ** -0.5 * HI ** -0.5).then_inc(relu_ready, 1)
                            n_raw += 1

                def exponent(g):
                    t, h = heads[g]
                    act.wait_ge(nmax_ready, g + 1)
                    if t >= 2 and h == 0:
                        act.wait_ge(o_used, 2 * (t - 2) + 2)
                    nc.scalar.activation(logit[:, g % 2, 0:NK[t]], logit[:, g % 2, 0:NK[t]], ACT.Exp, scale=DHC ** -0.5,
                                         bias=nmax[:, g % 2:g % 2 + 1], accum_out=total[:, t % 2, h:h + 1]).then_inc(exp_ready, 1)

                n_turned = 0

                def copies(g):
                    nonlocal n_turned
                    t, h = heads[g]
                    bl = blocks(t)
                    for k in range(-(-len(bl) // 4)):
                        act.wait_ge(turned, n_turned + 1)
                        if g >= 2:
                            act.wait_ge(o_ready, g - 1)
                        part = bl[4 * k:4 * k + 4]
                        bank = pP[n_turned % 2]
                        full = [x for x in part if x[1] == P]
                        if t == NT:
                            act.wait_ge(zeroed, 3)
                            if g > NT * HC:
                                act.wait_ge(o_ready, g)
                            nc.scalar.copy(bass.AP(pTz, 0, [[NSEQ * P, P], [P + SLEN, NSEQ], [1, SLEN]]),
                                           bank[:, 0, :].rearrange("p (i t) -> p i t", t=SLEN)).then_inc(act_own, 1)
                            nc.scalar.copy(pT[:, g % 2, 0, :], bank[:, 1, :]).then_inc(pT_copied, 1)
                        else:
                            if full:
                                ins = nc.scalar.copy(pT[:, g % 2, 4 * k:4 * k + len(full), :], bank[:, 0:len(full), :])
                            if len(full) < len(part):
                                if full:
                                    ins.then_inc(act_own, 1)
                                ins = nc.scalar.copy(pT[0:META, g % 2, 4 * k + len(full), :], bank[0:META, len(full), :])
                            ins.then_inc(pT_copied, 1)
                        n_turned += 1
                relus(0)
                for g in range(len(heads)):
                    t, h = heads[g]
                    exponent(g)
                    if g:
                        copies(g - 1)
                    if h == HC - 1 and t + 1 < TT:
                        relus(t + 1)
                copies(len(heads) - 1)

            @block.tensor
            def _(pe):
                n_raw = n_log = 0

                def indexer(t):
                    nonlocal n_raw
                    if t == NT:
                        pe.wait_ge(caches_in, 48)
                        pe.wait_ge(qz_ready, 5)
                    for a, b in key_spans(t):
                        for h in range(HI):
                            if n_raw >= 2:
                                pe.wait_ge(relu_ready, n_raw - 1)
                            bank = pR[h % 2]
                            if t < NT:
                                mm = nc.tensor.matmul(bank[:, 0:b - a], m.fm[i_rows(h), F_QI, q_cols(t)], m.fm[i_rows(h), F_KI, a:b])
                            else:
                                for i in range(NSEQ):
                                    nc.tensor.matmul(bank[:, 0:P], qiz[i_rows(h), i, :], kiC[i_rows(h), i, :],
                                                     start=i == 0, stop=i == NSEQ - 1)
                                mm = nc.tensor.matmul(bank[:, P:SK], m.fm[i_rows(h), F_QI, q_cols(t)],
                                                      m.fm[i_rows(h), F_KI, PROMPT:ALL])
                            mm.then_inc(raw_ready, 1)
                            n_raw += 1

                def logit_products(g):
                    nonlocal n_log
                    t, h = heads[g]
                    q = m.fm[kv_rows(h), F_CQ + h % GQ, q_cols(t)]
                    for a, b in key_spans(t):
                        if n_log >= 3:
                            pe.wait_ge(masked, n_log - 2)
                        bank = pL[n_log % 3]
                        if t < NT:
                            mm = nc.tensor.matmul(bank[:, 0:b - a], q, m.fm[kv_rows(h), F_CK, a:b])
                        else:
                            for i in range(NSEQ):
                                nc.tensor.matmul(bank[:, 0:P], qz[kv_rows(h), h % GQ, i, :], kC[kv_rows(h), i, :],
                                                 start=i == 0, stop=i == NSEQ - 1)
                            mm = nc.tensor.matmul(bank[:, P:SK], q, m.fm[kv_rows(h), F_CK, PROMPT:ALL])
                        mm.then_inc(logit_ready, 1)
                        n_log += 1

                n_turned = 0

                def turn(g):
                    nonlocal n_turned
                    t, h = heads[g]
                    bl = blocks(t)
                    pe.wait_ge(exp_ready, g + 1)
                    for k in range(-(-len(bl) // 4)):
                        if n_turned >= 2:
                            pe.wait_ge(pT_copied, n_turned - 1)
                        for j, (a, n) in enumerate(bl[4 * k:4 * k + 4]):
                            mm = nc.tensor.transpose(pP[n_turned % 2][0:n, j, :], logit[:, g % 2, a:a + n], cols(m, "ident"))
                        mm.then_inc(turned, 1)
                        n_turned += 1

                def values(g):
                    t, h = heads[g]
                    bl = blocks(t)
                    pe.wait_ge(pT_copied, sum(1 for x in groups if x[0] <= g))
                    if h == 0 and t:
                        pe.wait_ge(o_used, 2 * t)
                    out = pO[:, 64 * h:64 * h + 64]
                    c = CV + 64 * (h // GQ)
                    if t == NT:
                        pe.wait_ge(act_own, sum(1 for tt, hh in heads[:NT * HC] if len(blocks(tt)) % 4 != 1) + h + 1)
                        for i in range(NSEQ):
                            nc.tensor.matmul(out, pTz[:, i, :], vC[:, i, c - CV:c - CV + 64], start=i == 0, stop=False)
                        mm = nc.tensor.matmul(out, pT[:, g % 2, 0, :], m.tm[:, SAMPLE, c:c + 64], start=False, stop=True)
                    else:
                        for j, (a, n) in enumerate(bl):
                            src = m.tm[0:n, j if n == P else MT, c:c + 64]
                            mm = nc.tensor.matmul(out, pT[0:n, g % 2, j, :], src, start=j == 0, stop=j == len(bl) - 1)
                    mm.then_inc(o_ready, 1)

                indexer(0)
                for g in range(len(heads)):
                    t, h = heads[g]
                    logit_products(g)
                    if g:
                        turn(g - 1)
                    if g > 1:
                        values(g - 2)
                    if h == HC - 1 and t + 1 < TT:
                        indexer(t + 1)
                turn(len(heads) - 1)
                values(len(heads) - 2)
                values(len(heads) - 1)


def phase_out(nc, m, d):
    with ExitStack() as ctx:
        sem = Semaphores(nc, "p7_")
        al = Bump(m, "p7_", m.FMO, m.CO)
        w, wr, gb = al("w_out", [P, KD, D]), al("w_router", [P, KD, NE]), al("gb", [P, 2, D])
        h0, yr, pre, h1 = (al(n, [P, 3, D]) for n in ("h0", "yr", "pre", "h1"))
        al = Bump(m, "p7_", m.SCR, m.END)
        yT, hT = al("yT", [P, 2, KD, P]), al("h1T", [P, KD, P])
        stats, mv = al("stats", [P, 3, 2, 6]), al("mv", [P, 3, 4])
        m.rl = m.at("router_logits", [P, TT, NE], m.END - 1024)
        pT, pH = ctx.enter_context(nc.psum_tensor("p7_T", [P, KD, P], F32)), ctx.enter_context(nc.psum_tensor("p7_H", [P, KD, P], F32))
        pY, pR = ctx.enter_context(nc.psum_tensor("p7_Y", [P, 2, 512], F32)), ctx.enter_context(nc.psum_tensor("p7_R", [P, 512], F32))
        (w_in, dve_own, act_own, pool_own, y_copied, y_turned, yT_copied, mixed, pre_ready, var_ready, rstd_ready, xn_ready,
         h1_ready, h1_turned, h1T_copied, routed, r_copied) = (sem(n) for n in (
            "w_in dve_own act_own pool_own y_copied y_turned yT_copied mixed pre_ready var_ready rstd_ready xn_ready "
            "h1_ready h1_turned h1T_copied routed r_copied").split())
        h0_in, h1_out = [sem(f"h0_in{u}") for u in range(3)], [sem(f"h1_out{u}") for u in range(3)]
        R = TT // 3

        def turns(eng, first, rest):
            for u in range(3):
                first(0, u)
            with eng.Fori(1, R) as r:
                for u in range(3):
                    rest(r, u)

        ctx.enter_context(sem)
        with nc.Block() as block:
            @block.sync
            def _(sp):
                for k in range(KD):
                    sp.dma_start(w[:, k, :], d["w_out"][:, k, :]).then_inc(w_in, 16)
                sp.dma_start(wr[:, :, :], d["w_router"]).then_inc(w_in, 16)
                sp.dma_start(gb[:, :, :], d["ln1_gb"].partition_broadcast(P)).then_inc(w_in, 16)

                def load(r, u, wait):
                    if wait:
                        sp.wait_ge(pre_ready, 3 * r + (u - 2))
                    sp.dma_start(h0[:, u, :], m.h0_dram[ds((3 * r + u) * P, P), :]).then_inc(h0_in[u], 16)
                turns(sp, lambda r, u: load(r, u, False), lambda r, u: load(r, u, True))

            @block.gpsimd
            def _(pool):
                pool.wait_ge(w_in, 16 * (KD + 2))

                def step(r, u, later):
                    t = 3 * r + u
                    own = Chain(pool, pool_own, t)
                    if later:
                        pool.wait_ge(y_turned, t - 2)
                    nc.gpsimd.tensor_copy(yr[:, u, :], m.tm[:, t, 0:D]).then_inc(y_copied, 1)
                    pool.wait_ge(xn_ready, t + 1)
                    own.link(nc.gpsimd.tensor_tensor(h1[:, u, :], h1[:, u, :], gb[:, 0, :], ALU.mult))
                    nc.gpsimd.tensor_tensor(h1[:, u, :], h1[:, u, :], gb[:, 1, :], ALU.add).then_inc(h1_ready, 1)
                turns(pool, lambda r, u: step(r, u, False), lambda r, u: step(r, u, True))

            @block.vector
            def _(dve):
                def step(r, u, later):
                    t = 3 * r + u
                    own = Chain(dve, dve_own, 4 * t)
                    dve.wait_ge(h0_in[u], 16 * r + 16)
                    dve.wait_ge(mixed, t + 1)
                    nc.vector.scalar_tensor_tensor(pre[:, u, :], h0[:, u, :], ALPHA, pY[:, :, :].rearrange("p a b -> p (a b)"),
                                                   ALU.mult, ALU.add).then_inc(pre_ready, 1)
                    dve.wait_ge(pre_ready, t + 1)
                    own.link(nc.vector.bn_stats(stats[:, u, 0, :], pre[:, u, 0:512]))
                    own.link(nc.vector.bn_stats(stats[:, u, 1, :], pre[:, u, 512:1024]))
                    own.link(nc.vector.tensor_copy(mv[:, u, 3:4], stats[:, u, 1, 0:1]))
                    nc.vector.tensor_copy(mv[:, u, 2:3], stats[:, u, 1, 0:1])
                    own.link(nc.vector.bn_aggr(mv[:, u, 0:2], stats[:, u, :, :]))
                    nc.vector.tensor_scalar(mv[:, u, 3:4], mv[:, u, 1:2], EPS, None, ALU.add).then_inc(var_ready, 1)
                    dve.wait_ge(rstd_ready, t + 1)
                    if later:
                        dve.wait_ge(h1_out[u], 16 * r)
                        dve.wait_ge(h1_turned, t - 2)
                    nc.vector.tensor_scalar(h1[:, u, :], pre[:, u, :], mv[:, u, 0:1], mv[:, u, 3:4],
                                            ALU.subtract, ALU.mult).then_inc(xn_ready, 1)
                    dve.wait_ge(routed, t + 1)
                    nc.vector.tensor_copy(m.rl[:, t, :], pR[:, 0:NE]).then_inc(r_copied, 1)
                turns(dve, lambda r, u: step(r, u, False), lambda r, u: step(r, u, True))

            @block.scalar
            def _(act):
                def step(r, u):
                    t = 3 * r + u
                    own = Chain(act, act_own, t)
                    act.wait_ge(y_turned, t + 1)
                    if u or not isinstance(r, int):
                        act.wait_ge(mixed, t)
                    for b in range(2):
                        nc.scalar.copy(yT[:, 0, 4 * b:4 * b + 4, :], pT[:, 4 * b:4 * b + 4, :]).then_inc(yT_copied, 1)
                    act.wait_ge(var_ready, t + 1)
                    own.link(nc.scalar.activation(mv[:, u, 3:4], mv[:, u, 3:4], ACT.Ln))
                    nc.scalar.activation(mv[:, u, 3:4], mv[:, u, 3:4], ACT.Exp, scale=-0.5).then_inc(rstd_ready, 1)
                    act.wait_ge(h1_ready, t + 1)
                    act.dma_start(m.h1_dram[ds(t * P, P), :], h1[:, u, :]).then_inc(h1_out[u], 16)
                    act.wait_ge(h1_turned, t + 1)
                    if u or not isinstance(r, int):
                        act.wait_ge(routed, t)
                    for b in range(2):
                        nc.scalar.copy(hT[:, 4 * b:4 * b + 4, :], pH[:, 4 * b:4 * b + 4, :]).then_inc(h1T_copied, 1)
                turns(act, step, step)
                for u in range(3):
                    act.wait_ge(h1_out[u], 16 * R)

            @block.tensor
            def _(pe):
                pe.wait_ge(w_in, 16 * (KD + 2))

                def mix(t, u):
                    pe.wait_ge(y_copied, t + 1)
                    if not isinstance(t, int) or t:
                        pe.wait_ge(yT_copied, 2 * t)
                    for k in range(KD):
                        mm = nc.tensor.transpose(pT[:, k, :], yr[:, u, k * P:(k + 1) * P], cols(m, "ident"))
                    mm.then_inc(y_turned, 1)
                    pe.wait_ge(yT_copied, 2 * t + 2)
                    if not isinstance(t, int) or t:
                        pe.wait_ge(pre_ready, t)
                    for b in range(2):
                        for k in range(KD):
                            mm = nc.tensor.matmul(pY[:, b, :], yT[:, 0, k, :], w[:, k, 512 * b:512 * b + 512],
                                                  start=k == 0, stop=k == KD - 1)
                    mm.then_inc(mixed, 1)

                def route(t, u):
                    pe.wait_ge(h1_ready, t + 1)
                    if not isinstance(t, int) or t:
                        pe.wait_ge(h1T_copied, 2 * t)
                    for k in range(KD):
                        mm = nc.tensor.transpose(pH[:, k, :], h1[:, u, k * P:(k + 1) * P], cols(m, "ident"))
                    mm.then_inc(h1_turned, 1)
                    pe.wait_ge(h1T_copied, 2 * t + 2)
                    if not isinstance(t, int) or t:
                        pe.wait_ge(r_copied, t)
                    for k in range(KD):
                        mm = nc.tensor.matmul(pR[:, 0:NE], hT[:, k, :], wr[:, k, :], start=k == 0, stop=k == KD - 1)
                    mm.then_inc(routed, 1)

                def step(r, u):
                    mix(3 * r + u, u)
                    route(3 * r + u, u)
                turns(pe, step, step)


SLOTS = (2 * TOK + NE * (P - 1)) // P


def phase_route(nc, m, d):
    with ExitStack() as ctx:
        sem = Semaphores(nc, "p8_")
        al = Bump(m, "p8_", m.SCR, m.END - 1024)
        T16 = lambda n: al(n, [P, TT, NE])
        s, sb, e1, e2, both, tmp, pos = (T16(n) for n in ("s", "sb", "e1", "e2", "both", "tmp", "pos"))
        br = al("b_router", [P, NE])
        hi, lo = al("hi", [P, TT, NG, 2]), al("lo", [P, TT, NG, 2])
        gs, gm, g1t = al("gs", [P, TT, NG]), al("gm", [P, TT, NG]), al("g1t", [P, TT, NG])
        idx, w1, w2, tot = al("idx", [P, TT]), al("w1", [P, TT]), al("w2", [P, TT]), al("tot", [P, TT])
        ones = al("ones", [P, P])
        before, count = al("before", [P, TT, NE]), al("count", [P, NE])
        ge, ntile, cum, start = al("ge", [P, NE, 9]), al("ntile", [P, NE]), al("cum", [P, NE]), al("start", [P, NE])
        tge, eidf = al("tge", [P, SLOTS, NE]), al("eidf", [P, SLOTS])
        slotf = al("slotf", [P, 2, TT])
        rows = al("rows", [P, 2, TT, 2], I32)
        fill = al("fill", [P, SLOTS * 2], I32)
        m.slot = m.at("slot", [P, 2, TT], m.TMO, U32)
        m.eid = m.at("eid", [P, SLOTS], m.TMO + 128, I32)
        m.table = m.at("table", [P, SLOTS, 2], m.TMO + 320, I32)
        p1 = ctx.enter_context(nc.psum_tensor("p8_1", [P, 512], F32))
        p2 = ctx.enter_context(nc.psum_tensor("p8_2", [P, 512], F32))
        own_s, b_in, exp_in, exp_out, both_ready, ranked, table_ready, filled, scattered, table_in = (sem(n) for n in (
            "own b_in exp_in exp_out both_ready ranked table_ready filled scattered table_in").split())
        flat = lambda ap: ap.rearrange("p t e -> p (t e)")

        ctx.enter_context(sem)
        with nc.Block() as block:
            @block.sync
            def _(sp):
                sp.dma_start(br[:, :], d["b_router"].partition_broadcast(P)).then_inc(b_in, 16)
                sp.wait_ge(filled, 1)
                sp.dma_start(m.table_dram.rearrange("(i p) c -> p i c", p=P), fill[:, :].rearrange("p (i c) -> p i c", c=2)).then_inc(filled, 16)
                sp.wait_ge(scattered, 16 * 2 * TT)
                sp.dma_start(m.table[:, :, :], m.table_dram.rearrange("(i p) c -> p i c", p=P)).then_inc(table_in, 16)
                sp.wait_ge(table_in, 16)

            @block.gpsimd
            def _(pool):
                nc.gpsimd.memset(fill[:, :], 0).then_inc(filled, 1)
                pool.wait_ge(filled, 17)
                pool.wait_ge(table_ready, 1)
                for k in range(2):
                    for t in range(TT):
                        pool.indirect_dma_start(m.table_dram[:, :], bass.IndirectOffsetOnAxis(m.slot[:, k, t:t + 1], 0),
                                                rows[:, k, t, :], None).then_inc(scattered, 16)

            @block.scalar
            def _(act):
                act.wait_ge(exp_in, 1)
                nc.scalar.activation(s[:, :, :], m.rl[:, :, :], ACT.Exp, scale=-1.0).then_inc(exp_out, 1)

            @block.tensor
            def _(pe):
                pe.wait_ge(both_ready, 1)
                nc.tensor.matmul(p1[:, 0:TT * NE], cols(m, "tri"), flat(both[:, :, :]))
                nc.tensor.matmul(p2[:, 0:TT * NE], ones[:, :], flat(both[:, :, :])).then_inc(ranked, 1)

            @block.vector
            def _(dve):
                own = Chain(dve, own_s)
                V = nc.vector
                L = own.link
                L(V.memset(ones[:, :], 1.0))
                V.memset(before[:, 0, :], 0.0).then_inc(exp_in, 1)
                dve.wait_ge(exp_in, 1)
                dve.wait_ge(exp_out, 1)
                L(V.tensor_scalar(s[:, :, :], s[:, :, :], 1.0, None, ALU.add))
                L(V.reciprocal(s[:, :, :], s[:, :, :]))
                dve.wait_ge(b_in, 16)
                L(V.tensor_tensor(sb[:, :, :], s[:, :, :], over(br[:, :].unsqueeze(1), [P, TT, NE]), ALU.add))
                q = sb[:, :, :].rearrange("p t (g a b) -> p (t g) a b", g=NG, a=2)
                hv, lv = hi[:, :, :, :].rearrange("p t g a -> p (t g) a"), lo[:, :, :, :].rearrange("p t g a -> p (t g) a")
                gv, tv = gs[:, :, :].rearrange("p t g -> p (t g)"), g1t[:, :, :].rearrange("p t g -> p (t g)")
                L(V.tensor_tensor(hv, q[:, :, :, 0], q[:, :, :, 1], ALU.max))
                L(V.tensor_tensor(lv, q[:, :, :, 0], q[:, :, :, 1], ALU.min))
                L(V.tensor_tensor(gv, hv[:, :, 0], hv[:, :, 1], ALU.max))
                L(V.tensor_tensor(tv, hv[:, :, 0], hv[:, :, 1], ALU.min))
                L(V.tensor_tensor(lv[:, :, 0], lv[:, :, 0], lv[:, :, 1], ALU.max))
                L(V.tensor_tensor(tv, tv, lv[:, :, 0], ALU.max))
                L(V.tensor_tensor(gv, gv, tv, ALU.add))

                def first_max(out, val, n):
                    iota = over(cols(m, "iota16")[:, 0:n].unsqueeze(1), [P, TT, n])
                    L(V.tensor_reduce(idx[:, :], val, AX.X, ALU.max))
                    L(V.tensor_tensor(out, val, over(idx[:, :].unsqueeze(2), [P, TT, n]), ALU.is_equal))
                    L(V.scalar_tensor_tensor(out, out, -100.0, iota, ALU.mult, ALU.add))
                    L(V.tensor_reduce(idx[:, :], out, AX.X, ALU.min))
                    L(V.tensor_tensor(out, out, over(idx[:, :].unsqueeze(2), [P, TT, n]), ALU.is_equal))
                first_max(gm[:, :, :], gs[:, :, :], NG)
                L(V.tensor_scalar(gm[:, :, :], gm[:, :, :], -NEG, NEG, ALU.mult, ALU.add))
                L(V.tensor_tensor(sb[:, :, :].rearrange("p t (g e) -> p (t g) e", g=NG), sb[:, :, :].rearrange("p t (g e) -> p (t g) e", g=NG),
                                  over(gm[:, :, :].rearrange("p t g -> p (t g)").unsqueeze(2), [P, TT * NG, EG]), ALU.add))
                first_max(e1[:, :, :], sb[:, :, :], NE)
                L(V.scalar_tensor_tensor(sb[:, :, :], e1[:, :, :], -1e35, sb[:, :, :], ALU.mult, ALU.add))
                first_max(e2[:, :, :], sb[:, :, :], NE)
                for e, wk in ((e1, w1), (e2, w2)):
                    L(V.tensor_tensor(tmp[:, :, :], e[:, :, :], s[:, :, :], ALU.mult))
                    L(V.tensor_reduce(wk[:, :], tmp[:, :, :], AX.X, ALU.add))
                L(V.tensor_tensor(tot[:, :], w1[:, :], w2[:, :], ALU.add))
                L(V.reciprocal(tot[:, :], tot[:, :]))
                gate = lambda k: rows[:, k, :, 1].bitcast(F32)
                L(V.tensor_tensor(gate(0), w1[:, :], tot[:, :], ALU.mult))
                L(V.tensor_tensor(gate(1), w2[:, :], tot[:, :], ALU.mult))
                for k in range(2):
                    L(V.tensor_copy(rows[:, k, :, 0], cols(m, "rowid")))
                V.tensor_tensor(both[:, :, :], e1[:, :, :], e2[:, :, :], ALU.add).then_inc(both_ready, 1)
                dve.wait_ge(ranked, 1)
                tot16 = p2[:, 0:TT * NE].rearrange("p (t e) -> p t e", e=NE)
                for t in range(1, TT):
                    L(V.tensor_tensor(before[:, t, :], before[:, t - 1, :], tot16[:, t - 1, :], ALU.add))
                L(V.tensor_tensor(count[:, :], before[:, TT - 1, :], tot16[:, TT - 1, :], ALU.add))
                L(V.tensor_tensor(ge[:, :, :], over(count[:, :].unsqueeze(2), [P, NE, 9]),
                                  over(cols(m, "tiles128").unsqueeze(1), [P, NE, 9]), ALU.is_gt))
                L(V.tensor_reduce(ntile[:, :], ge[:, :, :], AX.X, ALU.add))
                L(V.tensor_tensor_scan(cum[:, :], ones[:, 0:NE], ntile[:, :], 0.0, ALU.mult, ALU.add))
                L(V.tensor_tensor(start[:, :], cum[:, :], ntile[:, :], ALU.subtract))
                L(V.tensor_tensor(pos[:, :, :], p1[:, 0:TT * NE].rearrange("p (t e) -> p t e", e=NE), before[:, :, :], ALU.add))
                L(V.scalar_tensor_tensor(pos[:, :, :], over(start[:, :].unsqueeze(1), [P, TT, NE]), float(P), pos[:, :, :],
                                         ALU.mult, ALU.add))
                for k, e in enumerate((e1, e2)):
                    L(V.tensor_tensor(tmp[:, :, :], e[:, :, :], pos[:, :, :], ALU.mult))
                    L(V.tensor_reduce(slotf[:, k, :], tmp[:, :, :], AX.X, ALU.add))
                L(V.tensor_tensor(tge[:, :, :], over(cum[:, :].unsqueeze(1), [P, SLOTS, NE]),
                                  over(cols(m, "slotid").unsqueeze(2), [P, SLOTS, NE]), ALU.is_le))
                L(V.tensor_reduce(eidf[:, :], tge[:, :, :], AX.X, ALU.add))
                L(V.tensor_scalar(eidf[:, :], eidf[:, :], float(NE - 1), None, ALU.min))
                L(V.tensor_copy(m.eid[:, :], eidf[:, :]))
                V.tensor_copy(m.slot[:, :, :], slotf[:, :, :]).then_inc(table_ready, 1)


def phase_moe(nc, m, d):
    with ExitStack() as ctx:
        sem = Semaphores(nc, "p9_")
        al = Bump(m, "p9_", m.TMO + 1024, m.CO)
        wgu, wd = al("wgu", [P, 3, KD, 2 * DE]), al("wd", [P, 3, 2, D])
        x, xT, ys = al("x", [P, 3, D]), al("xT", [P, 3, KD, P]), al("ys", [P, 3, D])
        al = Bump(m, "p9_", m.SCR, m.END)
        he, sg, heT = al("he", [P, 3, DE]), al("sg", [P, 3, DE]), al("heT", [P, 3, 2, P])
        entry = al("entry", [P, 3, 2], I32)
        pT = ctx.enter_context(nc.psum_tensor("p9_T", [P, KD, P], F32))
        pG = [ctx.enter_context(nc.psum_tensor(f"p9_G{i}", [P, 512], F32)) for i in range(3)]
        pH = ctx.enter_context(nc.psum_tensor("p9_H", [P, 2, P], F32))
        pY = ctx.enter_context(nc.psum_tensor("p9_Y", [P, 2, 512], F32))
        (entry_ready, turned, xT_copied, gu_ready, silu_ready, he_ready, h_turned, heT_ready, y_ready, ys_ready, held) = (
            sem(n) for n in "entry_ready turned xT_copied gu_ready silu_ready he_ready h_turned heT_ready y_ready ys_ready held".split())
        w_in, x_in, ys_out = ([sem(f"{n}{u}") for u in range(3)] for n in ("w_in", "x_in", "ys_out"))
        R = SLOTS // 3
        assert SLOTS == 3 * R

        def turns(eng, step):
            for u in range(3):
                step(0, u, False)
            with eng.Fori(1, R) as r:
                for u in range(3):
                    step(r, u, True)

        ctx.enter_context(sem)
        with nc.Block() as block:
            @block.sync
            def _(sp):
                def step(r, u, later):
                    t = 3 * r + u
                    e = sp.value_load(m.eid[0:1, ds(t, 1)], min_val=0, max_val=NE - 1)
                    if later:
                        sp.wait_ge(y_ready, t - 2)
                    sp.dma_start(wgu[:, u, :, :], d["w_gu"][ds(e, 1), :, :, :].rearrange("a p k n -> p (a k) n")).then_inc(w_in[u], 16)
                    sp.dma_start(wd[:, u, :, :], d["w_down"][ds(e, 1), :, :, :].rearrange("a p k n -> p (a k) n")).then_inc(w_in[u], 16)
                turns(sp, step)

            @block.gpsimd
            def _(pool):
                def step(r, u, later):
                    t = 3 * r + u
                    if later:
                        pool.wait_ge(turned, t - 2)
                    pool.wait_ge(entry_ready, t + 1)
                    pool.sem_inc(held, 1)
                    pool.indirect_dma_start(x[:, u, :], None, m.h1_dram[:, :],
                                            bass.IndirectOffsetOnAxis(entry[:, u, 0:1].bitcast(U32), 0)).then_inc(x_in[u], 16)
                turns(pool, step)

            @block.vector
            def _(dve):
                def entries(r, u, later):
                    t = 3 * r + u
                    if later:
                        dve.wait_ge(he_ready, t - 2)
                        dve.wait_ge(x_in[u], 16 * r)
                    nc.vector.tensor_copy(entry[:, u, :], m.table[:, t, :]).then_inc(entry_ready, 1)

                def step(r, u, later):
                    t = 3 * r + u
                    dve.wait_ge(silu_ready, t + 1)
                    if later:
                        dve.wait_ge(h_turned, t - 2)
                    nc.vector.scalar_tensor_tensor(he[:, u, :], sg[:, u, :], entry[:, u, 1:2].bitcast(F32), pG[u][:, DE:2 * DE],
                                                   ALU.mult, ALU.mult).then_inc(he_ready, 1)
                    dve.wait_ge(h_turned, t + 1)
                    if later:
                        dve.wait_ge(y_ready, t - 2)
                    nc.vector.tensor_copy(heT[:, u, :, :], pH[:, :, :]).then_inc(heT_ready, 1)
                    dve.wait_ge(y_ready, t + 1)
                    if later:
                        dve.wait_ge(ys_out[u], 16 * r)
                    nc.vector.tensor_copy(ys[:, u, :], pY[:, :, :].rearrange("p a b -> p (a b)")).then_inc(ys_ready, 1)
                for u in range(3):
                    entries(0, u, False)
                for u in range(3):
                    step(0, u, False)
                    entries(1, u, True)
                with dve.Fori(1, R - 1) as r:
                    for u in range(3):
                        step(r, u, True)
                        entries(r + 1, u, True)
                for u in range(3):
                    step(R - 1, u, True)

            @block.scalar
            def _(act):
                def copy_x(r, u, later):
                    t = 3 * r + u
                    act.wait_ge(turned, t + 1)
                    if later:
                        act.wait_ge(gu_ready, t - 2)
                    for b in range(2):
                        nc.scalar.copy(xT[:, u, 4 * b:4 * b + 4, :], pT[:, 4 * b:4 * b + 4, :]).then_inc(xT_copied, 1)

                def step(r, u, later):
                    t = 3 * r + u
                    act.wait_ge(gu_ready, t + 1)
                    if later:
                        act.wait_ge(he_ready, t - 2)
                    nc.scalar.activation(sg[:, u, :], pG[u][:, 0:DE], ACT.Silu).then_inc(silu_ready, 1)

                def store(r, u):
                    t = 3 * r + u
                    act.wait_ge(ys_ready, t + 1)
                    act.dma_start(m.ys_dram[ds(t * P, P), :], ys[:, u, :]).then_inc(ys_out[u], 16)
                copy_x(0, 0, False)
                copy_x(0, 1, False)
                step(0, 0, False)
                copy_x(0, 2, False)
                step(0, 1, False)
                store(0, 0)
                copy_x(1, 0, True)
                step(0, 2, False)
                store(0, 1)
                with act.Fori(1, R - 1) as r:
                    for u in range(3):
                        if u < 2:
                            copy_x(r, u + 1, True)
                        else:
                            copy_x(r + 1, 0, True)
                        step(r, u, True)
                        if u:
                            store(r, u - 1)
                        else:
                            store(r - 1, 2)
                r = R - 1
                copy_x(r, 1, True)
                step(r, 0, True)
                store(r - 1, 2)
                copy_x(r, 2, True)
                step(r, 1, True)
                store(r, 0)
                step(r, 2, True)
                store(r, 1)
                store(r, 2)
                for u in range(3):
                    act.wait_ge(ys_out[u], 16 * R)

            @block.tensor
            def _(pe):
                def turn(r, u, later):
                    t = 3 * r + u
                    pe.wait_ge(x_in[u], 16 * r + 16)
                    if later or u:
                        pe.wait_ge(xT_copied, 2 * t)
                    for k in range(KD):
                        mm = nc.tensor.transpose(pT[:, k, :], x[:, u, k * P:(k + 1) * P], cols(m, "ident"))
                    mm.then_inc(turned, 1)

                def up(r, u, later):
                    t = 3 * r + u
                    pe.wait_ge(xT_copied, 2 * t + 2)
                    pe.wait_ge(w_in[u], 32 * r + 32)
                    if later:
                        pe.wait_ge(he_ready, t - 2)
                    for k in range(KD):
                        mm = nc.tensor.matmul(pG[u][:, :], xT[:, u, k, :], wgu[:, u, k, :], start=k == 0, stop=k == KD - 1)
                    mm.then_inc(gu_ready, 1)

                def down(r, u, later):
                    t = 3 * r + u
                    pe.wait_ge(he_ready, t + 1)
                    if later or u:
                        pe.wait_ge(heT_ready, t)
                    for k in range(2):
                        mm = nc.tensor.transpose(pH[:, k, :], he[:, u, k * P:(k + 1) * P], cols(m, "ident"))
                    mm.then_inc(h_turned, 1)
                    pe.wait_ge(heT_ready, t + 1)
                    if later or u:
                        pe.wait_ge(ys_ready, t)
                    for b in range(2):
                        for k in range(2):
                            mm = nc.tensor.matmul(pY[:, b, :], heT[:, u, k, :], wd[:, u, k, 512 * b:512 * b + 512],
                                                  start=k == 0, stop=k == 1)
                    mm.then_inc(y_ready, 1)
                turn(0, 0, False)
                turn(0, 1, False)
                up(0, 0, False)
                turn(0, 2, False)
                up(0, 1, False)
                down(0, 0, False)
                turn(1, 0, True)
                up(0, 2, False)
                down(0, 1, False)
                with pe.Fori(1, R - 1) as r:
                    for u in range(3):
                        if u < 2:
                            turn(r, u + 1, True)
                        else:
                            turn(r + 1, 0, True)
                        up(r, u, True)
                        if u:
                            down(r, u - 1, True)
                        else:
                            down(r - 1, 2, True)
                r = R - 1
                turn(r, 1, True)
                up(r, 0, True)
                down(r - 1, 2, True)
                turn(r, 2, True)
                up(r, 1, True)
                down(r, 0, True)
                up(r, 2, True)
                down(r, 1, True)
                down(r, 2, True)


def phase_finish(nc, m, d):
    with ExitStack() as ctx:
        sem = Semaphores(nc, "pa_")
        al = Bump(m, "pa_", m.TMO + 1024, m.CO)
        gb = al("gb", [P, 2, D])
        a, b, h1, pre, y = (al(n, [P, 3, D]) for n in ("a", "b", "h1", "pre", "y"))
        entry = al("entry", [P, 3, 2], U32)
        stats, mv = al("stats", [P, 3, 2, 6]), al("mv", [P, 3, 4])
        (g_in, dve_own, act_own, pool_own, sum_ready, var_ready, rstd_ready, xn_ready, y_ready, entry_ready, held) = (sem(n) for n in (
            "g_in dve_own act_own pool_own sum_ready var_ready rstd_ready xn_ready y_ready entry_ready held").split())
        ab_in, h1_in, y_out = ([sem(f"{n}{u}") for u in range(3)] for n in ("ab_in", "h1_in", "y_out"))
        R = TT // 3

        def turns(eng, step):
            for u in range(3):
                step(0, u, False)
            with eng.Fori(1, R) as r:
                for u in range(3):
                    step(r, u, True)

        ctx.enter_context(sem)
        with nc.Block() as block:
            @block.sync
            def _(sp):
                sp.dma_start(gb[:, :, :], d["ln2_gb"].partition_broadcast(P)).then_inc(g_in, 16)

                def load(r, u, later):
                    t = 3 * r + u
                    if later:
                        sp.wait_ge(sum_ready, t - 2)
                    sp.dma_start(h1[:, u, :], m.h1_dram[ds(t * P, P), :]).then_inc(h1_in[u], 16)
                turns(sp, load)

            @block.gpsimd
            def _(pool):
                def gather(r, u, later):
                    t = 3 * r + u
                    pool.wait_ge(entry_ready, t + 1)
                    if later:
                        pool.wait_ge(sum_ready, t - 2)
                    pool.sem_inc(held, 1)
                    for k, dst in ((0, a), (1, b)):
                        pool.indirect_dma_start(dst[:, u, :], None, m.ys_dram[:, :],
                                                bass.IndirectOffsetOnAxis(entry[:, u, k:k + 1], 0)).then_inc(ab_in[u], 16)
                turns(pool, gather)

            @block.vector
            def _(dve):
                def entries(r, u, later):
                    t = 3 * r + u
                    if later:
                        dve.wait_ge(ab_in[u], 32 * r)
                    nc.vector.tensor_copy(entry[:, u, :], m.slot[:, :, t]).then_inc(entry_ready, 1)

                def step(r, u, later):
                    t = 3 * r + u
                    own = Chain(dve, dve_own, 7 * t)
                    dve.wait_ge(ab_in[u], 32 * r + 32)
                    dve.wait_ge(h1_in[u], 16 * r + 16)
                    own.link(nc.vector.tensor_tensor(pre[:, u, :], a[:, u, :], b[:, u, :], ALU.add))
                    nc.vector.scalar_tensor_tensor(pre[:, u, :], h1[:, u, :], ALPHA, pre[:, u, :],
                                                   ALU.mult, ALU.add).then_inc(sum_ready, 1)
                    dve.wait_ge(sum_ready, t + 1)
                    own.link(nc.vector.bn_stats(stats[:, u, 0, :], pre[:, u, 0:512]))
                    own.link(nc.vector.bn_stats(stats[:, u, 1, :], pre[:, u, 512:1024]))
                    own.link(nc.vector.tensor_copy(mv[:, u, 3:4], stats[:, u, 1, 0:1]))
                    nc.vector.tensor_copy(mv[:, u, 2:3], stats[:, u, 1, 0:1])
                    own.link(nc.vector.bn_aggr(mv[:, u, 0:2], stats[:, u, :, :]))
                    nc.vector.tensor_scalar(mv[:, u, 3:4], mv[:, u, 1:2], EPS, None, ALU.add).then_inc(var_ready, 1)
                    dve.wait_ge(rstd_ready, t + 1)
                    if later:
                        dve.wait_ge(y_out[u], 16 * r)
                    own.link(nc.vector.tensor_scalar(y[:, u, :], pre[:, u, :], mv[:, u, 0:1], mv[:, u, 3:4], ALU.subtract, ALU.mult))
                    own.link(nc.vector.tensor_tensor(y[:, u, :], y[:, u, :], gb[:, 0, :], ALU.mult))
                    nc.vector.tensor_tensor(y[:, u, :], y[:, u, :], gb[:, 1, :], ALU.add).then_inc(y_ready, 1)
                    own.steps(7)
                dve.wait_ge(g_in, 16)
                for u in range(3):
                    entries(0, u, False)
                for u in range(3):
                    step(0, u, False)
                    entries(1, u, True)
                for r in range(1, R):
                    for u in range(3):
                        step(r, u, True)
                        if r + 1 < R:
                            entries(r + 1, u, True)

            @block.scalar
            def _(act):
                def step(r, u, later):
                    t = 3 * r + u
                    own = Chain(act, act_own, t)
                    act.wait_ge(var_ready, t + 1)
                    own.link(nc.scalar.activation(mv[:, u, 3:4], mv[:, u, 3:4], ACT.Ln))
                    nc.scalar.activation(mv[:, u, 3:4], mv[:, u, 3:4], ACT.Exp, scale=-0.5).then_inc(rstd_ready, 1)
                    act.wait_ge(y_ready, t + 1)
                    act.dma_start(d["y"][ds(t * P, P), :], y[:, u, :]).then_inc(y_out[u], 16)
                turns(act, step)
                for u in range(3):
                    act.wait_ge(y_out[u], 16 * R)


class Shared:
    pass


def build(nc, d):
    m = Shared()
    base = (nc.sbuf_base + 63) // 64 * 64

    def at(name, shape, offset, dtype=F32):
        return nc.alloc_sbuf_tensor_at(name, shape, dtype, offset=base + offset)
    m.at = at
    m.TMO = 0
    m.FMO = m.TMO + (TT + 1) * TM * 4
    m.HTO = m.FMO + FM * ALL * 4
    m.CO = m.HTO + KD * ALL * 4
    m.SCR = m.CO + (NCONST * 4 + 63) // 64 * 64
    m.END = (nc.sbuf_usable_end - base) // 64 * 64
    m.tm = at("tm", [P, TT + 1, TM], m.TMO)
    m.fm = at("fm", [P, FM, ALL], m.FMO)
    m.hT = at("hT", [P, KD, ALL], m.HTO)
    m.const = at("const", [P, NCONST], m.CO)
    m.h0_dram = nc.dram_tensor("h0_rows", (TOK, D), F32, kind="Internal").ap()
    m.h1_dram = nc.dram_tensor("h1_rows", (TOK, D), F32, kind="Internal").ap()
    m.table_dram = nc.dram_tensor("slot_table", (SLOTS * P, 2), I32, kind="Internal").ap()
    m.ys_dram = nc.dram_tensor("expert_rows", (SLOTS * P, D), F32, kind="Internal").ap()
    for phase in PHASES:
        phase(nc, m, d)


OUTS = {
    "y": (TOK, D),
    "p_k": (PROMPT, 128), "p_v": (PROMPT, 128), "p_kidx": (PROMPT, DI),
    "p_gla": (HA, DKA, DVA), "p_c": (HB, DHB, DHB), "p_n": (HB, DHB), "p_m": (HB, 1), "p_conv": (4, P, 3),
    "s_k": (P, 128), "s_v": (P, 128), "s_kidx": (P, DI),
    "s_gla": (HA, DKA, NSEQ, DVA), "s_c": (HB, DHB, NSEQ, DHB), "s_n": (HB, DHB, NSEQ), "s_m": (HB, NSEQ),
    "s_conv": (4, P, NSEQ, 3),
}


def constants():
    p = np.arange(P)[:, None]
    c = lambda n: np.arange(n)[None, :]
    selM = np.zeros((P, 512), np.float32)
    selM[0:HB] = c(512) // P == np.arange(HB)[:, None]
    selB = np.zeros((P, 256), np.float32)
    selB[0:HB] = c(256) // DHB == np.arange(HB)[:, None]
    v = {
        "ident": p == c(P), "headA": p // DKA == c(HA), "bdA": p // DKA == c(256) // DVA,
        "causal": p <= c(P), "blocked": (p <= c(P)) & (p // SLEN == c(P) // SLEN),
        "seqmask": p // SLEN == c(NSEQ), "bdB": p // DHB == c(130) // 65, "headB": p // DHB == c(2),
        "otherseq": np.where(p // SLEN == c(P) // SLEN, 0.0, NEG), "tri": p < c(P),
        "iota16": c(NE) + 0 * p, "tiles128": P * c(9) + 0 * p, "rowid": p + P * c(TT), "slotid": c(33) + 0 * p, "selM": selM, "selB": selB,
    }
    return np.ascontiguousarray(np.concatenate([np.asarray(v[n], np.float32) for n in CONSTS], axis=1))


def lay_out(q):
    w, b = q["w_in"][0], q["b_in"][0]
    names = (('a_q', 128), ('a_k', 128), ('a_v', 256), ('a_g', 16), ('a_r', 256), ('b_qk', 512), ('b_v', 256),
             ('b_i', 4), ('b_f', 4), ('b_o', 256), ('c_q', 512), ('c_k', 128), ('c_v', 128), ('c_qi', 128),
             ('c_w', 4), ('c_ki', 32))
    s, at = {}, 0
    for n, k in names:
        s[n] = np.arange(at, at + k)
        at += k

    def pick(parts):
        return (np.concatenate([w[:, x] if not isinstance(x, int) else np.zeros((D, x), w.dtype) for x in parts], axis=1),
                np.concatenate([b[x] if not isinstance(x, int) else np.zeros((x,), b.dtype) for x in parts]))

    wt, bt = pick([s["a_v"], s["a_r"], s["b_v"], s["b_o"], s["c_v"], s["c_k"], s["c_ki"], s["c_w"], TM - CW - 4])
    cq = [np.concatenate([s["c_q"][64 * j:64 * j + 64], s["c_q"][64 * (j + 4):64 * (j + 4) + 64]]) for j in range(4)]
    wf, bf = pick([s["a_q"], s["a_k"], s["b_qk"]] + cq + [s["c_k"], s["c_qi"]] + [s["c_ki"]] * HI
                  + [s["a_g"], 16, s["b_i"], 28, s["b_f"], 60])
    o = {
        "consts": constants(),
        "x": np.concatenate([q["x_prompt"][0], q["x_sample"].reshape(P, D), q["meta_tokens"]]),
        "ln_in_gb": np.stack([q["ln_in_g"], q["ln_in_b"]]),
        "w_tm": wt.reshape(KD, P, TM).transpose(1, 0, 2), "b_tm": bt,
        "w_fm": wf.reshape(KD, P, FM, P).transpose(2, 1, 0, 3), "b_fm": bf.reshape(FM, P).T,
    }
    o.update(lay_out_rest(q))
    return {k: np.ascontiguousarray(v) for k, v in o.items()}


def kernel(**inputs):
    import concourse.bacc as bacc
    from concourse.bass_utils import run_bass_kernel_spmd

    q = {k: np.asarray(v) for k, v in inputs.items()}
    arrays = lay_out(q)
    nc = bacc.Bacc("TRN2", target_bir_lowering=False, num_devices=1)
    d = {k: nc.dram_tensor("in_" + k, v.shape, F32, kind="ExternalInput").ap() for k, v in arrays.items()}
    d.update({k: nc.dram_tensor("out_" + k, s, F32, kind="ExternalOutput").ap() for k, s in OUTS.items()})
    build(nc, d)
    r = run_bass_kernel_spmd(nc, [{"in_" + k: v for k, v in arrays.items()}], core_ids=[0]).results[0]
    g = {k: np.asarray(r["out_" + k]) for k in OUTS}
    rows = lambda n, *s: g[n].reshape(*s)
    return (
        g["y"][0:SEQ].reshape(1, SEQ, D), g["y"][SEQ:TOK].reshape(NSEQ, SLEN, D),
        rows("p_k", 1, 1, PROMPT, KVC, DHC), rows("p_v", 1, 1, PROMPT, KVC, DHC), rows("p_kidx", 1, 1, PROMPT, DI),
        g["p_gla"][None, None], g["p_c"].transpose(0, 2, 1)[None, None], g["p_n"][None, None],
        g["p_m"].reshape(1, 1, HB), g["p_conv"].transpose(2, 0, 1).reshape(1, 1, 3, 512),
        rows("s_k", 1, NSEQ, SLEN, KVC, DHC), rows("s_v", 1, NSEQ, SLEN, KVC, DHC), rows("s_kidx", 1, NSEQ, SLEN, DI),
        g["s_gla"].transpose(2, 0, 1, 3)[None], g["s_c"].transpose(2, 0, 3, 1)[None], g["s_n"].transpose(2, 0, 1)[None],
        g["s_m"].T[None], g["s_conv"].transpose(2, 3, 0, 1).reshape(1, NSEQ, 3, 512),
    )
def lay_out_rest(q):
    P, NSEQ = 128, 8
    cw, cb = q["conv_w"][0], q["conv_b"][0]
    bd = np.zeros((HA, DKA, NSEQ, HA, DVA), np.float32)
    for h in range(HA):
        bd[h, :, :, h, :] = q["state_gla"][0][:, h].transpose(1, 0, 2)
    cbd = np.zeros((2, 2, DHB, NSEQ, 2, DHB + 1), np.float32)
    for h in range(HB):
        cbd[h // 2, h % 2, :, :, h % 2, 0:DHB] = q["state_mlstm_c"][0][:, h].transpose(2, 0, 1)
        cbd[h // 2, h % 2, :, :, h % 2, DHB] = q["state_mlstm_n"][0][:, h].T
    wo = q["w_out"][0]
    wo = np.concatenate([wo[512:768], wo[0:256], wo[768:1024], wo[256:512]])
    e = lambda w, k: w.reshape(NE, k, P, -1).transpose(0, 2, 1, 3)
    return {
        "w_out": wo.reshape(KD, P, D).transpose(1, 0, 2), "ln1_gb": np.stack([q["ln1_g"][0], q["ln1_b"][0]]),
        "w_router": q["w_router"].reshape(KD, P, NE).transpose(1, 0, 2), "b_router": q["b_router"],
        "w_gu": e(np.concatenate([q["w_gate"][0], q["w_up"][0]], axis=2), KD), "w_down": e(q["w_down"][0], 2),
        "ln2_gb": np.stack([q["ln2_g"][0], q["ln2_b"][0]]),
        "kT_cache": q["cache_k"][0].transpose(2, 3, 0, 1).reshape(P, NSEQ, P),
        "kiT_cache": np.concatenate([q["cache_kidx"][0].transpose(2, 0, 1)] * HI),
        "v_cache": q["cache_v"][0].transpose(1, 0, 2, 3).reshape(P, NSEQ, P),
        "mlstm_bd": cbd.reshape(2, P, NSEQ, 2 * DHB + 2).transpose(1, 0, 2, 3), "m0": q["state_mlstm_m"][0].T,
        "b_forget": q["b_forget"][0].reshape(HB, 1), "g_gla_norm": q["g_gla_norm"][0], "g_mlstm_norm": q["g_mlstm_norm"][0],
        "conv_hist": q["state_conv"][0].reshape(NSEQ, 3, 4, P).transpose(3, 2, 0, 1),
        "conv_wb": np.concatenate([cw, cb[None]]).reshape(5, 4, P).transpose(2, 1, 0),
        "w_gla_gate": q["w_gla_gate"][0], "b_gla_gate": q["b_gla_gate"][0].reshape(P, 1),
        "gla_bd": bd.reshape(P, NSEQ, 256),
    }
PHASES = [phase_project, phase_project_fm, phase_conv, phase_gla, phase_norm_gla, phase_mlstm, phase_norm_mlstm, phase_dsa,
          phase_out, phase_route, phase_moe, phase_finish]
```

```python
from contextlib import ExitStack

import concourse.bass as bass
import numpy as np
from concourse import mybir

F32 = mybir.dt.float32
I32 = mybir.dt.int32
U32 = mybir.dt.uint32
BF16 = mybir.dt.bfloat16
ALU = mybir.AluOpType
ACT = mybir.ActivationFunctionType
AX = mybir.AxisListType
ds = bass.ds

P = 128
D = 1024
KD = D // P
SEQ, NSEQ, SLEN, META = 1024, 8, 16, 16
NT = SEQ // P
SAMPLE = NT
MT = NT + 1
TOK = SEQ + NSEQ * SLEN
TT = TOK // P
ALL = TOK + META
PROMPT = META + SEQ
PAST = 128
HA, DKA, DVA, RANK = 4, 32, 64, 16
HB, DHB = 4, 64
HC, KVC, DHC = 8, 2, 64
HI, DI = 4, 32
TOPK_P, TOPK_S = 256, (PAST + SLEN) // 4
NE, NG, EG, DE = 16, 4, 4, 256
EPS = 1e-5
ALPHA = 2 ** 0.25
NEG = -1e30
BIAS_BYTES = 10240
TAKEN = -3e38

AV, AR, BV, BO, CV, CK, CI, CW = 0, 256, 512, 768, 1024, 1152, 1280, 1312
TM, TG = 1320, 440
F_QI, F_KI, F_AQ, F_AK, F_BQ, F_BK, F_CQ, F_CK, F_MISC = 0, 1, 2, 3, 4, 6, 8, 12, 13
FM = 14
ROW_I, ROW_F = 32, 64

CONSTS = {}
_at = 0
for _name, _n in (("ident", P), ("headA", HA), ("bdA", 256), ("causal", P), ("blocked", P),
                  ("seqmask", NSEQ), ("bdB", 130), ("headB", 2), ("otherseq", P), ("tri", P),
                  ("iota16", NE), ("tiles128", 9), ("rowid", TT), ("slotid", 33), ("selM", 512), ("selB", 256)):
    CONSTS[_name] = (_at, _at + _n)
    _at += _n
NCONST = _at


class Chain:

    def __init__(self, eng, sem, base=0):
        self.eng, self.sem, self.base, self.k = eng, sem, base, 0

    def link(self, ins):
        self.k += 1
        ins.then_inc(self.sem, 1)
        self.eng.wait_ge(self.sem, self.base + self.k)

    def steps(self, n):
        assert self.k == n, (self.k, n)


class Semaphores:

    def __init__(self, nc, tag):
        self.nc, self.tag, self.made = nc, tag, []

    def __call__(self, name):
        self.made.append(self.nc.alloc_semaphore(self.tag + name))
        return self.made[-1]

    def __enter__(self):
        return self

    def __exit__(self, *error):
        if not any(error):
            self.nc.clear_and_free_semaphores(self.made)
            self.nc.all_engine_barrier()


def cols(m, name):
    a, b = CONSTS[name]
    return m.const[:, a:b]


class Bump:

    def __init__(self, m, tag, start, end):
        self.m, self.tag, self.o, self.end = m, tag, start, end

    def __call__(self, name, shape, dtype=F32):
        n = int(np.prod(shape[1:])) * 4
        at = self.o
        self.o = at + (n + 31) // 32 * 32
        assert self.o <= self.end, (self.tag, name, self.o - self.end)
        return self.m.at(self.tag + name, shape, at, dtype)


def over(ap, shape):
    return ap.broadcast_to(shape)


def phase_norm_in(nc, m, d):
    with ExitStack() as ctx:
        sem = Semaphores(nc, "p1_")
        al = Bump(m, "p1_", m.FMO + F_AQ * ALL * 4, m.HTO)
        m.wtm, m.btm = al("wtm", [P, KD, TM]), al("btm", [P, TM])
        m.own_o = al.o
        al = Bump(m, "p1_", m.SCR, m.END)
        gb, x, h0 = al("gb", [P, 2, D]), al("x", [P, 3, D]), al("h0", [P, 3, D])
        stats, mv = al("stats", [P, 3, 2, 6]), al("mv", [P, 3, 4])
        pT = [ctx.enter_context(nc.psum_tensor(f"p1_T{i}", [P, 4, P], F32)) for i in range(4)]
        gb_in, consts_in, w_in = sem("gb_in"), sem("consts_in"), sem("w_in")
        x_in, h0_out = [sem(f"x_in{i}") for i in range(3)], [sem(f"h0_out{i}") for i in range(3)]
        dve_own, act_own, pool_own = sem("dve_own"), sem("act_own"), sem("pool_own")
        var_ready, rstd_ready, xn_ready, h0_ready = sem("var_ready"), sem("rstd_ready"), sem("xn_ready"), sem("h0_ready")
        turned, hT_copied = sem("turned"), sem("hT_copied")

        ctx.enter_context(sem)
        with nc.Block() as block:
            @block.sync
            def _(sp):
                for u in range(3):
                    sp.dma_start(x[:, u, :], d["x"][u * P:(u + 1) * P, :]).then_inc(x_in[u], 16)
                    if u == 0:
                        sp.dma_start(gb[:, :, :], d["ln_in_gb"].partition_broadcast(P)).then_inc(gb_in, 16)
                        sp.dma_start(m.const[:, :], d["consts"]).then_inc(consts_in, 16)
                with sp.Fori(1, 3) as r:
                    for u in range(3):
                        sp.wait_ge(xn_ready, 3 * r + (u - 2))
                        sp.dma_start(x[:, u, :], d["x"][ds((3 * r + u) * P, P), :]).then_inc(x_in[u], 16)
                sp.wait_ge(xn_ready, 7)
                sp.dma_start(x[0:META, 0, :], d["x"][TOK:ALL, :]).then_inc(x_in[0], 16)
                for k in range(KD):
                    sp.dma_start(m.wtm[:, k, :], d["w_tm"][:, k, :]).then_inc(w_in, 16)
                sp.dma_start(m.btm[:, :], d["b_tm"].partition_broadcast(P)).then_inc(w_in, 16)
                sp.wait_ge(w_in, 16 * (KD + 1))

            @block.gpsimd
            def _(pool):
                pool.wait_ge(gb_in, 16)

                def scale(r, u, rows=P):
                    t = 3 * r + u
                    own = Chain(pool, pool_own, t)
                    pool.wait_ge(xn_ready, t + 1)
                    own.link(nc.gpsimd.tensor_tensor(h0[0:rows, u, :], h0[0:rows, u, :], gb[0:rows, 0, :], ALU.mult))
                    nc.gpsimd.tensor_tensor(h0[0:rows, u, :], h0[0:rows, u, :], gb[0:rows, 1, :],
                                            ALU.add).then_inc(h0_ready, 1)

                with pool.Fori(0, 3) as r:
                    for u in range(3):
                        scale(r, u)
                scale(3, 0, META)

            @block.vector
            def _(dve):
                def variance(r, u, rows=P):
                    t = 3 * r + u
                    own = Chain(dve, dve_own, 3 * t)
                    dve.wait_ge(x_in[u], 16 * (r + 1))
                    own.link(nc.vector.bn_stats(stats[0:rows, u, 0, :], x[0:rows, u, 0:512]))
                    own.link(nc.vector.bn_stats(stats[0:rows, u, 1, :], x[0:rows, u, 512:1024]))
                    nc.vector.tensor_copy(mv[0:rows, u, 3:4], stats[0:rows, u, 1, 0:1])
                    own.link(nc.vector.bn_aggr(mv[0:rows, u, 0:2], stats[0:rows, u, :, :]))
                    nc.vector.tensor_scalar(mv[0:rows, u, 2:3], mv[0:rows, u, 1:2], EPS, None,
                                            ALU.add).then_inc(var_ready, 1)

                def normal(r, u, rows=P, fresh=False):
                    t = 3 * r + u
                    dve.wait_ge(rstd_ready, t + 1)
                    if not fresh:
                        dve.wait_ge(h0_out[u], 16 * r)
                        dve.wait_ge(turned, 2 * t - 4)
                    nc.vector.tensor_scalar(h0[0:rows, u, :], x[0:rows, u, :], mv[0:rows, u, 0:1], mv[0:rows, u, 3:4],
                                            ALU.subtract, ALU.mult).then_inc(xn_ready, 1)
                variance(0, 0)
                for u in range(3):
                    if u < 2:
                        variance(0, u + 1)
                    normal(0, u, fresh=True)
                with dve.Fori(1, 3) as r:
                    for u in range(3):
                        variance(r, u)
                        normal(r, u)
                variance(3, 0, META)
                normal(3, 0, META)

            @block.scalar
            def _(act):
                def rstd(r, u, rows=P):
                    t = 3 * r + u
                    own = Chain(act, act_own, t)
                    act.wait_ge(var_ready, t + 1)
                    own.link(nc.scalar.activation(mv[0:rows, u, 3:4], mv[0:rows, u, 2:3], ACT.Ln))
                    nc.scalar.activation(mv[0:rows, u, 3:4], mv[0:rows, u, 3:4], ACT.Exp, scale=-0.5).then_inc(rstd_ready, 1)

                def copy(r, u, rows=P):
                    t = 3 * r + u
                    dst = m.hT[:, :, ds(META + t * P, P)] if rows == P else m.hT[:, :, 0:META]
                    act.wait_ge(h0_ready, t + 1)
                    if rows == P:
                        act.dma_start(m.h0_dram[ds(t * P, P), :], h0[:, u, :]).then_inc(h0_out[u], 16)
                    for b in range(2):
                        act.wait_ge(turned, 2 * t + b + 1)
                        nc.scalar.copy(dst[:, 4 * b:4 * b + 4, :], pT[b][:, :, 0:rows]).then_inc(hT_copied, 1)

                rstd(0, 0)
                for u in range(1, 3):
                    rstd(0, u)
                    copy(0, u - 1)
                with act.Fori(1, 3) as r:
                    for u in range(3):
                        rstd(r, u)
                        if u:
                            copy(r, u - 1)
                        else:
                            copy(r - 1, 2)
                rstd(3, 0, META)
                copy(2, 2)
                copy(3, 0, META)
                for u in range(3):
                    act.wait_ge(h0_out[u], 48)

            @block.tensor
            def _(pe):
                pe.wait_ge(consts_in, 16)

                def turn(r, u, rows=P):
                    t = 3 * r + u
                    pe.wait_ge(h0_ready, t + 1)
                    for b in range(2):
                        if not isinstance(r, int) or r or u:
                            pe.wait_ge(hT_copied, 2 * t - 1 + b)
                        for k in range(4):
                            mm = nc.tensor.transpose(pT[b][:, k, 0:rows], h0[0:rows, u, (4 * b + k) * P:(4 * b + k + 1) * P],
                                                     cols(m, "ident")[0:rows, 0:rows])
                        mm.then_inc(turned, 1)
                for u in range(3):
                    turn(0, u)
                with pe.Fori(1, 3) as r:
                    for u in range(3):
                        turn(r, u)
                turn(3, 0, META)


SK = 2 * P
NK = [META + P * (t + 1) for t in range(NT)] + [SK]
KEY_AT = [sum(NK[:t]) for t in range(TT + 1)]


def spans_of(n):
    parts = -(-n // 512)
    width = -(-n // parts // 16) * 16
    return [(a, min(a + width, n)) for a in range(0, n, width)]


def key_spans(t):
    return spans_of(NK[t]) if t < NT else [(0, SK)]


def q_cols(t):
    return slice(META + P * t, META + P * t + P)


def phase_project(nc, m, d):
    with ExitStack() as ctx:
        sem = Semaphores(nc, "p2_")
        m.bias = m.at("key_bias", [P, KEY_AT[TT]], m.END - TT * 1024 - BIAS_BYTES, BF16)
        al = Bump(m, "p2_", m.SCR, m.END - TT * 1024 - BIAS_BYTES)
        score, w = al("score", [P, KEY_AT[TT] + 4]), al("w", [P, 2, KD, P])
        al = Bump(m, "p2_", m.END - TT * 1024, m.END)
        relu, bfm, top, wt = al("relu", [P, 2, 512]), al("bfm", [P, FM]), al("top", [P, 8]), al("wt", [P, TT, HI])
        al = Bump(m, "p2_", m.own_o, m.HTO)
        qiz, kiC = al("qiz", [P, NSEQ, P]), al("kiC", [P, NSEQ, P])
        ps = [ctx.enter_context(nc.psum_tensor(f"p2_{i}", [P, 512], F32)) for i in range(6)]
        pR = [ctx.enter_context(nc.psum_tensor(f"p2_R{i}", [P, 512], F32)) for i in range(2)]
        w_in = [sem("w_in0"), sem("w_in1")]
        (b_in, rows_out, kiC_in, wt_ready, wt_copied, fm_ready, fm_copied, tm_ready, tm_copied, bias_added, zeroed, qiz_ready,
         raw_ready, relu_ready, relu_used, dve_own, round_own) = (sem(n) for n in (
            "b_in rows_out kiC_in wt_ready wt_copied fm_ready fm_copied tm_ready tm_copied bias_added zeroed qiz_ready "
            "raw_ready relu_ready relu_used dve_own round_own").split())
        spans = [(0, 512), (512, 1024), (1024, ALL)]
        i_rows = lambda h: slice(DI * h, DI * h + DI)
        groups = [(t, g) for t in range(TT + 1) for g in range(3)]
        rows_of = lambda t: META if t == MT else P
        ctx.enter_context(sem)
        with nc.Block() as block:
            @block.sync
            def _(sp):
                for u in range(2):
                    sp.dma_start(w[:, u, :, :], d["w_fm"][u, :, :, :]).then_inc(w_in[u], 16)
                sp.dma_start(bfm[:, :], d["b_fm"]).then_inc(b_in, 16)
                sp.dma_start(kiC[:, :, :], d["kiT_cache"]).then_inc(kiC_in, 16)
                with sp.Fori(1, FM // 2) as r:
                    for u in range(2):
                        sp.wait_ge(fm_ready, 6 * r + (3 * u - 3))
                        sp.dma_start(w[:, u, :, :], d["w_fm"][2 * r + u, :, :, :]).then_inc(w_in[u], 16)

            @block.gpsimd
            def _(pool):
                nc.gpsimd.memset(qiz[:, :, :], 0.0).then_inc(zeroed, 1)
                pool.wait_ge(zeroed, 1)
                pool.wait_ge(fm_copied, 3)
                nc.gpsimd.tensor_copy(bass.AP(qiz, 0, [[NSEQ * P, P], [P + SLEN, NSEQ], [1, SLEN]]),
                                      m.fm[:, F_QI, PROMPT:ALL].rearrange("p (i t) -> p i t", t=SLEN)).then_inc(qiz_ready, 1)
                for n, (t, g) in enumerate(groups):
                    rows, c = rows_of(t), slice(g * TG, (g + 1) * TG)
                    pool.wait_ge(tm_copied, n + 1)
                    nc.gpsimd.tensor_tensor(m.tm[0:rows, t, c], m.tm[0:rows, t, c], m.btm[0:rows, c], ALU.add).then_inc(bias_added, 1)
                pool.wait_ge(bias_added, len(groups))
                n = 0
                for name, c, width in (("k", CK, 128), ("v", CV, 128), ("kidx", CI, DI)):
                    out = d["p_" + name]
                    pool.dma_start(out[0:META, :], m.tm[0:META, MT, c:c + width]).then_inc(rows_out, 16)
                    pool.dma_start(out[META:PROMPT, :].rearrange("(j p) c -> p j c", p=P),
                                   m.tm[:, 0:NT, c:c + width]).then_inc(rows_out, 16)
                    pool.dma_start(d["s_" + name], m.tm[:, SAMPLE, c:c + width]).then_inc(rows_out, 16)
                    n += 3
                pool.wait_ge(rows_out, 16 * n)

            @block.tensor
            def _(pe):
                for t in range(TT):
                    for k in range(KD):
                        mm = nc.tensor.matmul(ps[5][:, HI * t:HI * t + HI], m.hT[:, k, q_cols(t)], m.wtm[:, k, CW:CW + HI],
                                              start=k == 0, stop=k == KD - 1)
                mm.then_inc(wt_ready, 1)

                def tile(r, u, free):
                    pe.wait_ge(w_in[u], 16 * r + 16)
                    for c, (a, b) in enumerate(spans):
                        free(c)
                        for k in range(KD):
                            mm = nc.tensor.matmul(ps[3 * u + c][:, 0:b - a], w[:, u, k, :], m.hT[:, k, a:b],
                                                  start=k == 0, stop=k == KD - 1)
                        mm.then_inc(fm_ready, 1)
                tile(0, 0, lambda c: None)
                tile(0, 1, lambda c: pe.wait_ge(wt_copied, 1) if c == 2 else None)
                n_raw = 0
                pe.wait_ge(fm_copied, 6)
                for t in range(TT):
                    if t == NT:
                        pe.wait_ge(kiC_in, 16)
                        pe.wait_ge(qiz_ready, 1)
                    for a, b in key_spans(t):
                        for h in range(HI):
                            if n_raw >= 2:
                                pe.wait_ge(relu_ready, n_raw - 1)
                            bank = pR[h % 2]
                            if t < NT:
                                mm = nc.tensor.matmul(bank[:, 0:b - a], m.fm[i_rows(h), F_QI, q_cols(t)], m.fm[i_rows(h), F_KI, a:b])
                            else:
                                for i in range(NSEQ):
                                    nc.tensor.matmul(bank[:, 0:P], qiz[i_rows(h), i, :], kiC[i_rows(h), i, :],
                                                     start=i == 0, stop=i == NSEQ - 1)
                                mm = nc.tensor.matmul(bank[:, P:SK], m.fm[i_rows(h), F_QI, q_cols(t)],
                                                      m.fm[i_rows(h), F_KI, PROMPT:ALL])
                            mm.then_inc(raw_ready, 1)
                            n_raw += 1
                for n, (t, g) in enumerate(groups):
                    if n >= 6:
                        pe.wait_ge(tm_copied, n - 5)
                    rows = rows_of(t)
                    for k in range(KD):
                        stream = m.hT[:, k, q_cols(t)] if rows == P else m.hT[:, k, 0:META]
                        mm = nc.tensor.matmul(ps[n % 6][0:rows, 0:TG], stream, m.wtm[:, k, g * TG:(g + 1) * TG],
                                              start=k == 0, stop=k == KD - 1)
                    mm.then_inc(tm_ready, 1)
                for u in range(2):
                    tile(1, u, lambda c: pe.wait_ge(tm_copied, len(groups) - 5 + 3 * u + c))
                with pe.Fori(2, FM // 2) as r:
                    for u in range(2):
                        tile(r, u, lambda c: pe.wait_ge(fm_copied, 6 * r + (3 * u + c - 5)))

            @block.scalar
            def _(act):
                act.wait_ge(b_in, 16)

                def feature_tile(r, u):
                    for c, (a, b) in enumerate(spans):
                        act.wait_ge(fm_ready, 6 * r + (3 * u + c + 1))
                        nc.scalar.activation(m.fm[:, 2 * r + u, a:b], ps[3 * u + c][:, 0:b - a], ACT.Identity,
                                             bias=bfm[:, ds(2 * r + u, 1)]).then_inc(fm_copied, 1)
                for u in range(2):
                    feature_tile(0, u)
                n_raw = 0
                for t in range(TT):
                    for a, b in key_spans(t):
                        for h in range(HI):
                            act.wait_ge(raw_ready, n_raw + 1)
                            if n_raw >= 2:
                                act.wait_ge(relu_used, n_raw - 1)
                            nc.scalar.activation(relu[:, h % 2, 0:b - a], pR[h % 2][:, 0:b - a], ACT.Relu,
                                                 scale=DI ** -0.5 * HI ** -0.5).then_inc(relu_ready, 1)
                            n_raw += 1
                for n, (t, g) in enumerate(groups):
                    act.wait_ge(tm_ready, n + 1)
                    nc.scalar.copy(m.tm[0:rows_of(t), t, g * TG:(g + 1) * TG], ps[n % 6][0:rows_of(t), 0:TG]).then_inc(tm_copied, 1)
                act.wait_ge(bias_added, len(groups))
                with act.Fori(1, FM // 2) as r:
                    for u in range(2):
                        feature_tile(r, u)

            @block.vector
            def _(dve):
                own = Chain(dve, dve_own)
                dve.wait_ge(wt_ready, 1)
                nc.vector.tensor_tensor(wt[:, :, :], ps[5][:, 0:TT * HI].rearrange("p (t h) -> p t h", h=HI),
                                        over(m.btm[:, CW:CW + HI].unsqueeze(1), [P, TT, HI]), ALU.add).then_inc(wt_copied, 1)
                dve.wait_ge(wt_copied, 1)
                n_raw = 0
                for t in range(TT):
                    for a, b in key_spans(t):
                        for h in range(HI):
                            n_raw += 1
                            dve.wait_ge(relu_ready, n_raw)
                            r, out = relu[:, h % 2, 0:b - a], score[:, KEY_AT[t] + a:KEY_AT[t] + b]
                            if h == 0:
                                ins = nc.vector.tensor_scalar(out, r, wt[:, t, h:h + 1], None, ALU.mult)
                            else:
                                ins = nc.vector.scalar_tensor_tensor(out, r, wt[:, t, h:h + 1], out, ALU.mult, ALU.add)
                            ins.then_inc(relu_used, 1)
                            dve.wait_ge(relu_used, n_raw)
                for t in range(TT):
                    N, K, extra, at = NK[t], TOPK_P, 0, KEY_AT[t]
                    if t < NT:
                        own.link(nc.vector.memset(score[0:64, at + N - 64:at + N], NEG))
                    else:
                        K, extra = TOPK_S, 4
                        own.link(nc.vector.memset(score[:, at + N:at + N + extra], 3e38))
                        own.link(nc.vector.tensor_tensor(score[:, at + P:at + N], score[:, at + P:at + N], cols(m, "otherseq"), ALU.add))
                    if N > K:
                        n = (K + extra) // 8
                        src = score[:, at:at + N + extra]

                        def a_round(k):
                            nc.vector.max(top[:, :], src).then_inc(round_own, 1)
                            dve.wait_ge(round_own, 2 * k + 1)
                            nc.vector.match_replace(src, top[:, :], src, TAKEN).then_inc(round_own, 1)
                            dve.wait_ge(round_own, 2 * k + 2)
                        if n > 8:
                            with dve.Fori(0, n // 8) as r:
                                for k in range(8):
                                    a_round(k)
                                nc.vector.sem_clear(round_own)
                        else:
                            for k in range(n):
                                a_round(k)
                            nc.vector.sem_clear(round_own)
                        own.link(nc.vector.tensor_scalar(m.bias[:, at:at + N], src[:, 0:N], TAKEN, NEG, ALU.not_equal, ALU.mult))
                    else:
                        own.link(nc.vector.memset(m.bias[:, at:at + N], 0.0))
                    if t < NT:
                        own.link(nc.vector.memset(m.bias[0:64, at + N - 64:at + N], NEG))
                    else:
                        own.link(nc.vector.tensor_tensor(m.bias[:, at + P:at + N], m.bias[:, at + P:at + N], cols(m, "otherseq"), ALU.add))


def phase_conv(nc, m, d):
    with ExitStack() as ctx:
        sem = Semaphores(nc, "p3_")
        al = Bump(m, "p3_", m.HTO, m.CO)
        acc, den = al("acc", [P, ALL]), al("den", [P, ALL])
        hist = al("hist", [P, 4, NSEQ, 3])
        up = al("up", [P, NSEQ, SLEN + 3])
        wc = al("wc", [P, 4, 5])
        last_p, last_s = al("last_p", [P, 4, 3]), al("last_s", [P, 4, NSEQ, 3])
        w_in, acc_ready, exp_ready, saved, out, own_s = (sem("w_in"), sem("acc_ready"), sem("exp_ready"),
                                                         sem("saved"), sem("out"), sem("own"))
        ctx.enter_context(sem)
        with nc.Block() as block:
            @block.sync
            def _(sp):
                sp.dma_start(hist[:, :, :, :], d["conv_hist"]).then_inc(w_in, 16)
                sp.dma_start(wc[:, :, :], d["conv_wb"]).then_inc(w_in, 16)
                sp.wait_ge(saved, 4)
                sp.dma_start(d["p_conv"].rearrange("c p j -> p c j"), last_p[:, :, :]).then_inc(out, 16)
                sp.dma_start(d["s_conv"].rearrange("c p i j -> p c i j"), last_s[:, :, :, :]).then_inc(out, 16)
                sp.wait_ge(out, 32)

            @block.vector
            def _(dve):
                dve.wait_ge(w_in, 32)
                with dve.Fori(0, 4) as c:
                    own = Chain(dve, own_s, 11 * c)
                    u = m.fm[:, F_BQ + c, :]
                    us = m.fm[:, F_BQ + c, PROMPT:ALL].rearrange("p (i t) -> p i t", i=NSEQ)
                    tap = lambda j: wc[:, c, j:j + 1]
                    nc.vector.tensor_copy(last_p[:, c, :], u[:, PROMPT - 3:PROMPT])
                    nc.vector.tensor_copy(last_s[:, c, :, :], us[:, :, SLEN - 3:SLEN]).then_inc(saved, 1)
                    nc.vector.tensor_copy(up[:, :, 0:3], hist[:, c, :, :])
                    own.link(nc.vector.tensor_copy(up[:, :, 3:SLEN + 3], us))
                    own.link(nc.vector.tensor_scalar(acc[:, 0:PROMPT], u[:, 0:PROMPT], tap(3), tap(4), ALU.mult, ALU.add))
                    for j in range(1, 4):
                        own.link(nc.vector.scalar_tensor_tensor(acc[:, j:PROMPT], u[:, 0:PROMPT - j], tap(3 - j),
                                                                acc[:, j:PROMPT], ALU.mult, ALU.add))
                    accs = acc[:, PROMPT:ALL].rearrange("p (i t) -> p i t", i=NSEQ)
                    own.link(nc.vector.tensor_scalar(accs, up[:, :, 3:SLEN + 3], tap(3), tap(4), ALU.mult, ALU.add))
                    for j in range(1, 4):
                        ins = nc.vector.scalar_tensor_tensor(accs, up[:, :, 3 - j:SLEN + 3 - j], tap(3 - j), accs,
                                                             ALU.mult, ALU.add)
                        if j < 3:
                            own.link(ins)
                    ins.then_inc(acc_ready, 1)
                    dve.wait_ge(exp_ready, c + 1)
                    own.link(nc.vector.tensor_scalar(den[:, :], den[:, :], 1.0, None, ALU.add))
                    own.link(nc.vector.reciprocal(den[:, :], den[:, :]))
                    own.link(nc.vector.tensor_tensor(u, acc[:, :], den[:, :], ALU.mult))
                    own.steps(11)
                own = Chain(dve, own_s, 11 * 4)
                for c in range(2):
                    own.link(nc.vector.tensor_scalar(m.fm[:, F_BK + c, :], m.fm[:, F_BK + c, :], DHB ** -0.5, None, ALU.mult))

            @block.scalar
            def _(act):
                with act.Fori(0, 4) as c:
                    act.wait_ge(acc_ready, c + 1)
                    nc.scalar.activation(den[:, :], acc[:, :], ACT.Exp, scale=-1.0).then_inc(exp_ready, 1)


def log_sigmoid_act(nc, act, own, out, z):
    own.link(nc.scalar.activation(out, z, ACT.Abs))
    own.link(nc.scalar.activation(out, out, ACT.Exp, scale=-1.0))
    return nc.scalar.activation(out, out, ACT.Ln, bias=1.0)


def phase_gla(nc, m, d):
    with ExitStack() as ctx:
        sem = Semaphores(nc, "p4_")
        al = Bump(m, "p4_", m.HTO, m.CO)
        e_mid, e_neg, e_cum, e_last = (al(n, [P, ALL]) for n in ("e_mid", "e_neg", "e_cum", "e_last"))
        z, soft, cum = al("z", [P, ALL]), al("soft", [P, ALL]), al("cum", [P, ALL])
        keep = al("keep", [P, ALL])
        rel = soft
        al = Bump(m, "p4_", m.SCR, m.END - TT * 1024 - BIAS_BYTES)
        wg, bg = al("wg", [RANK, P]), al("bg", [P, 1])
        ke, qc, kd = (al(n, [P, 2, P]) for n in ("ke", "qc", "kd"))
        qbd, attm = al("qbd", [P, HA, P]), al("attm", [P, 2, HA, P])
        kdT, S, upd = al("kdT", [P, 2, P]), al("S", [P, 256]), al("upd", [P, 256])
        m.o = m.at("heads_o", [P, TT, 256], m.END - TT * 1024)
        S0 = Bump(m, "p4_", m.FMO, m.FMO + F_AQ * ALL * 4)("S0", [P, NSEQ, 256])
        qz, vz = al("qz", [P, NSEQ, P]), al("vz", [P, NSEQ, 256])
        pz = [ctx.enter_context(nc.psum_tensor(f"p4_z{i}", [P, 512], F32)) for i in range(4)]
        pA, pK, pO, pS = (ctx.enter_context(nc.psum_tensor("p4_" + n, [P, 512], F32)) for n in "AKOS")

        par_in, s0_in, out = sem("par_in"), sem("s0_in"), sem("out")
        z_ready, soft_ready, cum_ready, exps_ready = sem("z_ready"), sem("soft_ready"), sem("cum_ready"), sem("exps_ready")
        dve_own, act_own, pool_own = sem("dve_own"), sem("act_own"), sem("pool_own")
        zb_ready, rel_ready = sem("zb_ready"), sem("rel_ready")
        oper_ready, att_ready, attm_ready, kdT_ready, kdT_copied = (sem(n) for n in (
            "oper_ready", "att_ready", "attm_ready", "kdT_ready", "kdT_copied"))
        o_ready, o_copied, upd_ready, state_ready = sem("o_ready"), sem("o_copied"), sem("upd_ready"), sem("state_ready")
        zeroed, state_done, vz_ready, sample_upd = sem("zeroed"), sem("state_done"), sem("vz_ready"), sem("sample_upd")
        spans = [(0, 512), (512, 1024), (1024, ALL)]
        tile = lambda ap, t: ap[:, ds(META + t * P, P)] if not isinstance(t, int) else ap[:, META + t * P:META + t * P + P]
        prompt = lambda ap: ap[:, META:PROMPT].rearrange("p (j t) -> p j t", t=P)
        sample = lambda ap: ap[:, PROMPT:ALL].rearrange("p (i t) -> p i t", t=SLEN)
        AQ, AK = m.fm[:, F_AQ, :], m.fm[:, F_AK, :]

        ctx.enter_context(sem)
        with nc.Block() as block:
            @block.sync
            def _(sp):
                sp.dma_start(wg[:, :], d["w_gla_gate"]).then_inc(par_in, 16)
                sp.dma_start(bg[:, :], d["b_gla_gate"]).then_inc(par_in, 16)
                sp.dma_start(S0[:, :, :], d["gla_bd"]).then_inc(s0_in, 16)
                sp.wait_ge(state_ready, 9)
                for h in range(HA):
                    sp.dma_start(d["p_gla"][h, :, :], S[DKA * h:DKA * h + DKA, DVA * h:DVA * h + DVA]).then_inc(out, 16)
                sp.wait_ge(state_done, 1)
                for h in range(HA):
                    sp.dma_start(d["s_gla"][h, :, :, :],
                                 S0[DKA * h:DKA * h + DKA, :, DVA * h:DVA * h + DVA]).then_inc(out, 16)
                sp.wait_ge(out, 16 * 2 * HA)

            @block.gpsimd
            def _(pool):
                nc.gpsimd.memset(qz[:, :, :], 0.0).then_inc(zeroed, 1)
                nc.gpsimd.tensor_tensor(vz[:, :, :], over(m.tm[:, SAMPLE, AV:AV + 256].unsqueeze(1), [P, NSEQ, 256]),
                                        over(cols(m, "seqmask").unsqueeze(2), [P, NSEQ, 256]),
                                        ALU.mult).then_inc(vz_ready, 1)

            @block.vector
            def _(dve):
                own = Chain(dve, dve_own)
                own.link(nc.vector.memset(keep[:, :], 1.0))
                own.link(nc.vector.memset(keep[:, 0:1], 0.0))
                own.link(nc.vector.memset(prompt(keep)[:, :, 0:1], 0.0))
                own.link(nc.vector.memset(sample(keep)[:, :, 0:1], 0.0))
                dve.wait_ge(soft_ready, 1)
                own.link(nc.vector.scalar_tensor_tensor(z[:, :], z[:, :], 0.0, soft[:, :], ALU.min, ALU.subtract))
                own.link(nc.vector.tensor_tensor_scan(cum[:, :], keep[:, :], z[:, :], 0.0, ALU.mult, ALU.add))
                nc.vector.tensor_tensor(prompt(rel), prompt(cum), over(prompt(cum)[:, :, 63:64], [P, NT, P]), ALU.subtract)
                nc.vector.tensor_tensor(sample(rel), sample(cum), over(sample(cum)[:, :, 7:8], [P, NSEQ, SLEN]), ALU.subtract)
                nc.vector.tensor_tensor(prompt(z), over(prompt(cum)[:, :, P - 1:P], [P, NT, P]), prompt(cum), ALU.subtract)
                nc.vector.tensor_tensor(z[:, 0:META], over(cum[:, META - 1:META], [P, META]), cum[:, 0:META], ALU.subtract)
                nc.vector.tensor_tensor(sample(z), over(sample(cum)[:, :, SLEN - 1:SLEN], [P, NSEQ, SLEN]), sample(cum),
                                        ALU.subtract).then_inc(rel_ready, 1)
                dve.wait_ge(exps_ready, 4)
                own.link(nc.vector.scalar_tensor_tensor(e_mid[:, META:ALL], AQ[:, META:ALL], DKA ** -0.5, e_mid[:, META:ALL],
                                                        ALU.mult, ALU.mult))

                own_n = own.k

                def operands(t, u, sampled=False):
                    nc.vector.tensor_tensor(ke[:, u, :], tile(AK, t), tile(e_neg, t), ALU.mult)
                    nc.vector.tensor_tensor(kd[:, u, :], tile(AK, t), tile(e_last, t), ALU.mult)
                    nc.vector.tensor_tensor(qbd[:, :, :], over(tile(e_mid, t).unsqueeze(1), [P, HA, P]),
                                            over(cols(m, "headA").unsqueeze(2), [P, HA, P]), ALU.mult)
                    if sampled:
                        out = bass.AP(qz, 0, [[NSEQ * P, P], [P + SLEN, NSEQ], [1, SLEN]])
                        i0, i1 = sample(AQ), sample(e_cum)
                    else:
                        out, i0, i1 = qc[:, u, :], tile(AQ, t), tile(e_cum, t)
                    nc.vector.scalar_tensor_tensor(out, i0, DKA ** -0.5, i1, ALU.mult, ALU.mult).then_inc(oper_ready, 1)

                nc.vector.tensor_tensor(kd[:, 0, 0:META], AK[:, 0:META], e_last[:, 0:META], ALU.mult).then_inc(oper_ready, 1)
                dve.wait_ge(upd_ready, 1)
                nc.vector.tensor_tensor(S[:, :], pS[:, 0:256], cols(m, "bdA"), ALU.mult).then_inc(state_ready, 1)
                with dve.Fori(0, NT // 2) as r:
                    for u in range(2):
                        t = 2 * r + u
                        operands(t, u)
                        dve.wait_ge(att_ready, t + 1)
                        nc.vector.tensor_tensor(attm[:, u, :, :], pA[:, :].rearrange("p (h t) -> p h t", h=HA),
                                                over(cols(m, "causal").unsqueeze(1), [P, HA, P]),
                                                ALU.mult).then_inc(attm_ready, 1)
                        dve.wait_ge(upd_ready, t + 2)
                        nc.vector.tensor_tensor(upd[:, :], pS[:, 0:256], cols(m, "bdA"), ALU.mult).then_inc(sample_upd, 1)
                        dve.wait_ge(sample_upd, t + 1)
                        dve.wait_ge(o_ready, t + 1)
                        nc.vector.scalar_tensor_tensor(S[:, :], S[:, :], e_cum[:, ds(META + t * P + (P - 1), 1)], upd[:, :],
                                                       ALU.mult, ALU.add).then_inc(state_ready, 1)
                dve.wait_ge(zeroed, 1)
                dve.wait_ge(s0_in, 16)
                operands(NT, 0, sampled=True)
                dve.wait_ge(att_ready, NT + 1)
                nc.vector.tensor_tensor(attm[:, 0, :, :], pA[:, :].rearrange("p (h t) -> p h t", h=HA),
                                        over(cols(m, "blocked").unsqueeze(1), [P, HA, P]), ALU.mult).then_inc(attm_ready, 1)
                dve.wait_ge(o_ready, NT + 1)
                dve.wait_ge(upd_ready, NT + 2)
                
                own = Chain(dve, dve_own, own_n)
                for i in range(NSEQ):
                    own.link(nc.vector.tensor_tensor(upd[:, :], pz[i // 2][:, 256 * (i % 2):256 * (i % 2) + 256],
                                                      cols(m, "bdA"), ALU.mult))
                    ins = nc.vector.scalar_tensor_tensor(S0[:, i, :], S0[:, i, :],
                                                         e_cum[:, PROMPT + SLEN * i + SLEN - 1:PROMPT + SLEN * i + SLEN],
                                                         upd[:, :], ALU.mult, ALU.add)
                    if i < NSEQ - 1:
                        own.link(ins)
                ins.then_inc(state_done, 1)

            @block.scalar
            def _(act):
                own = Chain(act, act_own)
                act.wait_ge(par_in, 32)
                for c, (a, b) in enumerate(spans):
                    act.wait_ge(z_ready, c + 1)
                    own.link(nc.scalar.activation(z[:, a:b], pz[c][:, 0:b - a], ACT.Identity, bias=bg[:, 0:1]))
                log_sigmoid_act(nc, act, own, soft[:, :], z[:, :]).then_inc(soft_ready, 1)
                act.wait_ge(rel_ready, 1)
                tau = 1.0 / 16.0
                nc.scalar.activation(e_mid[:, META:ALL], rel[:, META:ALL], ACT.Exp, scale=tau).then_inc(exps_ready, 1)
                nc.scalar.activation(e_neg[:, META:ALL], rel[:, META:ALL], ACT.Exp, scale=-tau).then_inc(exps_ready, 1)
                nc.scalar.activation(e_cum[:, :], cum[:, :], ACT.Exp, scale=tau).then_inc(exps_ready, 1)
                nc.scalar.activation(e_last[:, :], z[:, :], ACT.Exp, scale=tau).then_inc(exps_ready, 1)

                def copies(t, u, rows=P):
                    act.wait_ge(kdT_ready, t + 1)
                    nc.scalar.copy(kdT[0:rows, u, :], pK[0:rows, 0:P]).then_inc(kdT_copied, 1)

                copies(0, 0, META)
                with act.Fori(0, NT // 2) as r:
                    for u in range(2):
                        t = 2 * r + u
                        copies(t + 1, u)
                        act.wait_ge(o_ready, t + 1)
                        nc.scalar.copy(m.o[:, t, :], pO[:, 0:256]).then_inc(o_copied, 1)
                copies(NT + 1, 0)
                act.wait_ge(o_ready, NT + 1)
                nc.scalar.copy(m.o[:, NT, :], pO[:, 0:256]).then_inc(o_copied, 1)

            @block.tensor
            def _(pe):
                pe.wait_ge(par_in, 32)
                for c, (a, b) in enumerate(spans):
                    nc.tensor.matmul(pz[c][:, 0:b - a], wg[:, :], m.fm[0:RANK, F_MISC, a:b]).then_inc(z_ready, 1)

                def attend(t, u, first=False):
                    pe.wait_ge(oper_ready, t + 2)
                    if not first:
                        pe.wait_ge(attm_ready, t)
                    nc.tensor.matmul(pA[:, :], ke[:, u, :], qbd[:, :, :].rearrange("p h t -> p (h t)")).then_inc(att_ready, 1)
                    pe.wait_ge(kdT_copied, t + 1)
                    nc.tensor.transpose(pK[:, 0:P], kd[:, u, :], cols(m, "ident")).then_inc(kdT_ready, 1)

                def update(t, u):
                    pe.wait_ge(kdT_copied, t + 2)
                    pe.wait_ge(state_ready, t + 1)
                    nc.tensor.matmul(pS[:, 0:256], kdT[:, u, :], m.tm[:, t, AV:AV + 256]).then_inc(upd_ready, 1)

                def heads(t, u):
                    pe.wait_ge(attm_ready, t + 1)
                    for h in range(HA):
                        mm = nc.tensor.matmul(pO[:, DVA * h:DVA * h + DVA], attm[:, u, h, :],
                                              m.tm[:, t, AV + DVA * h:AV + DVA * h + DVA], start=False, stop=h == HA - 1,
                                              skip_group_check=True)
                    mm.then_inc(o_ready, 1)

                pe.wait_ge(oper_ready, 1)
                nc.tensor.transpose(pK[0:META, 0:P], kd[:, 0, 0:META], cols(m, "ident")).then_inc(kdT_ready, 1)
                pe.wait_ge(kdT_copied, 1)
                nc.tensor.matmul(pS[:, 0:256], kdT[0:META, 0, :], m.tm[0:META, MT, AV:AV + 256]).then_inc(upd_ready, 1)

                def prompt_tile(t, u, first=False):
                    attend(t, u, first)
                    pe.wait_ge(state_ready, t + 1)
                    if not first:
                        pe.wait_ge(o_copied, t)
                    nc.tensor.matmul(pO[:, 0:256], qc[:, u, :], S[:, :], start=True, stop=False, skip_group_check=True)
                    heads(t, u)
                    update(t, u)
                prompt_tile(0, 0, True)
                prompt_tile(1, 1)
                with pe.Fori(1, NT // 2) as r:
                    for u in range(2):
                        prompt_tile(2 * r + u, u)
                attend(NT, 0)
                pe.wait_ge(s0_in, 16)
                pe.wait_ge(o_copied, NT)
                for i in range(NSEQ):
                    nc.tensor.matmul(pO[:, 0:256], qz[:, i, :], S0[:, i, :], start=i == 0, stop=False, skip_group_check=True)
                heads(NT, 0)
                pe.wait_ge(kdT_copied, NT + 2)
                pe.wait_ge(vz_ready, 1)
                for j in range(NSEQ // 2):
                    mm = nc.tensor.matmul(pz[j][:, :], kdT[:, 0, :], vz[:, 2 * j:2 * j + 2, :].rearrange("p i c -> p (i c)"))
                mm.then_inc(upd_ready, 1)


def phase_head_norm(nc, m, d, tag, weight, gate, silu):
    with ExitStack() as ctx:
        sem = Semaphores(nc, tag)
        al = Bump(m, tag, m.HTO, m.CO)
        NH = TT * 4
        sq, sig = al("sq", [P, TT, 256]), al("sig", [P, TT, 256])
        g, mean, var = al("g", [P, 256]), al("mean", [P, NH]), al("var", [P, NH])
        g_in, dve_own, act_own = sem("g_in"), sem("dve_own"), sem("act_own")
        var_ready, rstd_ready, sig_ready = sem("var_ready"), sem("rstd_ready"), sem("sig_ready")
        oh = m.o[:, :, :].rearrange("p t (h v) -> p (t h) v", v=64)
        sh = sq[:, :, :].rearrange("p t (h v) -> p (t h) v", v=64)
        each = lambda ap: over(ap.unsqueeze(2), [P, NH, 64])
        r = m.tm[:, 0:TT, gate:gate + 256]
        ctx.enter_context(sem)
        with nc.Block() as block:
            @block.sync
            def _(sp):
                sp.dma_start(g[:, :], d[weight].partition_broadcast(P)).then_inc(g_in, 16)

            @block.vector
            def _(dve):
                own = Chain(dve, dve_own)
                own.link(nc.vector.tensor_reduce(mean[:, :], oh, AX.X, ALU.add))
                own.link(nc.vector.tensor_scalar(mean[:, :], mean[:, :], 1.0 / 64, None, ALU.mult))
                own.link(nc.vector.tensor_tensor(oh, oh, each(mean[:, :]), ALU.subtract))
                own.link(nc.vector.tensor_tensor(sh, oh, oh, ALU.mult))
                own.link(nc.vector.tensor_reduce(var[:, :], sh, AX.X, ALU.add))
                nc.vector.tensor_scalar(var[:, :], var[:, :], 1.0 / 64, EPS, ALU.mult, ALU.add).then_inc(var_ready, 1)
                dve.wait_ge(rstd_ready, 1)
                own.link(nc.vector.tensor_tensor(oh, oh, each(var[:, :]), ALU.mult))
                dve.wait_ge(g_in, 16)
                own.link(nc.vector.tensor_tensor(m.o[:, :, :], m.o[:, :, :], over(g[:, :].unsqueeze(1), [P, TT, 256]), ALU.mult))
                dve.wait_ge(sig_ready, 1)
                if silu:
                    own.link(nc.vector.tensor_tensor(m.o[:, :, :], m.o[:, :, :], r, ALU.mult))
                own.link(nc.vector.tensor_tensor(r, m.o[:, :, :], sig[:, :, :], ALU.mult))

            @block.scalar
            def _(act):
                own = Chain(act, act_own)
                own.link(nc.scalar.activation(sig[:, :, :], r, ACT.Exp, scale=-1.0))
                own.link(nc.scalar.activation(sig[:, :, :], sig[:, :, :], ACT.Ln, bias=1.0))
                nc.scalar.activation(sig[:, :, :], sig[:, :, :], ACT.Exp, scale=-1.0).then_inc(sig_ready, 1)
                act.wait_ge(var_ready, 1)
                own.link(nc.scalar.activation(var[:, :], var[:, :], ACT.Ln))
                nc.scalar.activation(var[:, :], var[:, :], ACT.Exp, scale=-0.5).then_inc(rstd_ready, 1)


def phase_norm_gla(nc, m, d):
    phase_head_norm(nc, m, d, "p4n_", "g_gla_norm", AR, True)


def phase_norm_mlstm(nc, m, d):
    phase_head_norm(nc, m, d, "p5n_", "g_mlstm_norm", BO, False)


def phase_mlstm(nc, m, d):
    with ExitStack() as ctx:
        sem = Semaphores(nc, "p5_")
        nlast, mlast = m.at("p5_nlast", [P, 2, NSEQ], m.HTO + 7 * ALL * 4 + 3264), m.at("p5_mlast", [P, NSEQ + 1], m.HTO + 7 * ALL * 4 + 3328)
        VE = DVA + 1
        al = Bump(m, "p5_", m.HTO, m.CO)
        t1, t2, cum, M, gates, keep, drop = (al(n, [P, ALL]) for n in ("t1", "t2", "cum", "M", "gates", "keep", "drop"))
        gtm = al("gtm", [P, TT + 1, 4, HB])
        slf, slb = al("slf", [P, 17]), al("slb", [P, 2, 17])
        m0, bfg = al("m0", [P, NSEQ]), al("bfg", [P, 1])
        C0 = Bump(m, "p5_", m.FMO, m.FMO + F_AQ * ALL * 4)("C0", [P, 2, NSEQ, 2 * VE])
        al = Bump(m, "p5_", m.SCR, m.END - TT * 1024 - BIAS_BYTES)
        vx = al("vx", [P, TT + 1, HB, VE])
        vz, qz = al("vz", [P, NSEQ, HB * VE]), al("qz", [P, 2, NSEQ, P])
        al = Bump(m, "p5_", m.FMO + F_AQ * ALL * 4, m.FMO + F_BQ * ALL * 4)
        kr, qr, qbd = al("kr", [P, 2, P]), al("qr", [P, 2, P]), al("qbd", [P, 2, 2, P])
        W, kw = al("W", [P, HB, P]), al("kw", [P, 256])
        tot, C = al("tot", [P, HB, VE]), al("C", [P, 2, 2 * VE])
        upd, den = m.at("p5_upd", [P, 2, 2 * VE], m.HTO + 7 * ALL * 4 + 2048), m.at("p5_den", [P, HB], m.HTO + 7 * ALL * 4 + 3200)
        assert m.HTO + 7 * ALL * 4 + 3400 <= m.CO
        pA, pM, pK, pI, pN, pC, pX, pY = (ctx.enter_context(nc.psum_tensor("p5_" + n, [P, 512], F32)) for n in "AMKINCXY")
        (par_in, c0_in, out, dve_own, act_own, raw_ready, soft_ready, arg_ready, gates_ready, turned, gtm_ready,
         sl_ready, slb_ready, oper_ready, prod_ready, d_ready, w_ready, masked, pm_ready, kw_ready, inter_ready,
         h_ready, num_ready, upd_ready, state_ready, zeroed, vz_ready, kT_ready, m_ready) = (sem(n) for n in (
            "par_in c0_in out dve_own act_own raw_ready soft_ready arg_ready gates_ready turned gtm_ready sl_ready "
            "slb_ready oper_ready prod_ready d_ready w_ready masked pm_ready kw_ready inter_ready h_ready num_ready "
            "upd_ready state_ready zeroed vz_ready kT_ready m_ready").split())
        prompt = lambda ap: ap[:, META:PROMPT].rearrange("p (j t) -> p j t", t=P)
        sample = lambda ap: ap[:, PROMPT:ALL].rearrange("p (i t) -> p i t", t=SLEN)
        H = lambda ap: ap[0:HB, :]
        span = lambda t: ds(META + t * P, P)
        banks = (pA, pM, pK)
        STEPS = 12
        pair_bank = lambda i, p: (pA, pM, pK, pC, pX, pY)[(2 * i + p) // 3][:, 2 * VE * ((2 * i + p) % 3):2 * VE * ((2 * i + p) % 3 + 1)]

        ctx.enter_context(sem)
        with nc.Block() as block:
            @block.sync
            def _(sp):
                sp.dma_start(m0[0:HB, :], d["m0"]).then_inc(par_in, 16)
                sp.dma_start(bfg[ROW_F:ROW_F + HB, :], d["b_forget"]).then_inc(par_in, 16)
                sp.dma_start(C0[:, :, :, :], d["mlstm_bd"]).then_inc(c0_in, 16)
                sp.wait_ge(m_ready, 1)
                sp.dma_start(d["p_m"], mlast[0:HB, NSEQ:NSEQ + 1]).then_inc(out, 16)
                sp.dma_start(d["s_m"], mlast[0:HB, 0:NSEQ]).then_inc(out, 16)
                sp.wait_ge(state_ready, NT + 1)
                for h in range(HB):
                    rows = slice(64 * (h % 2), 64 * (h % 2) + 64)
                    c = VE * (h % 2)
                    sp.dma_start(d["p_c"][h, :, :], C[rows, h // 2, c:c + 64]).then_inc(out, 16)
                    sp.dma_start(d["p_n"][h:h + 1, :].rearrange("a k -> k a"), C[rows, h // 2, c + 64:c + 65]).then_inc(out, 16)
                sp.wait_ge(state_ready, NT + 2)
                for h in range(HB):
                    rows = slice(64 * (h % 2), 64 * (h % 2) + 64)
                    c = VE * (h % 2)
                    sp.dma_start(d["s_c"][h, :, :, :], C0[rows, h // 2, :, c:c + 64]).then_inc(out, 16)
                    sp.dma_start(d["s_n"][h, :, :], nlast[rows, h // 2, :]).then_inc(out, 16)
                sp.wait_ge(out, 16 * (2 + 4 * HB))

            @block.gpsimd
            def _(pool):
                nc.gpsimd.memset(qz[:, :, :, :], 0.0).then_inc(zeroed, 1)
                nc.gpsimd.memset(vx[:, :, :, :], 1.0).then_inc(zeroed, 1)
                pool.wait_ge(zeroed, 2)
                nc.gpsimd.tensor_copy(vx[:, 0:TT, :, 0:DVA],
                                      m.tm[:, 0:TT, BV:BV + 256].rearrange("p t (h v) -> p t h v", v=DVA)).then_inc(zeroed, 1)
                nc.gpsimd.tensor_copy(vx[0:META, MT, :, 0:DVA],
                                      m.tm[0:META, MT, BV:BV + 256].rearrange("p (h v) -> p h v", v=DVA)).then_inc(zeroed, 1)
                pool.wait_ge(zeroed, 4)
                nc.gpsimd.tensor_tensor(vz[:, :, :], over(vx[:, SAMPLE, :, :].rearrange("p h v -> p (h v)").unsqueeze(1),
                                                          [P, NSEQ, HB * VE]),
                                        over(cols(m, "seqmask").unsqueeze(2), [P, NSEQ, HB * VE]),
                                        ALU.mult).then_inc(vz_ready, 1)

                def mask(t, which):
                    pool.wait_ge(w_ready, t + 1)
                    nc.gpsimd.tensor_tensor(W[:, :, :], W[:, :, :], over(cols(m, which).unsqueeze(1), [P, HB, P]),
                                            ALU.mult).then_inc(masked, 1)
                with pool.Fori(0, NT) as t:
                    mask(t, "causal")
                mask(NT, "blocked")

            @block.vector
            def _(dve):
                own = Chain(dve, dve_own)
                own.link(nc.vector.memset(gates[:, :], 0.0))
                own.link(nc.vector.memset(H(keep), 1.0))
                own.link(nc.vector.memset(sample(keep)[0:HB, :, 0:1], 0.0))
                own.link(nc.vector.memset(H(drop), 0.0))
                nc.vector.memset(sample(drop)[0:HB, :, 0:1], NEG).then_inc(raw_ready, 1)
                dve.wait_ge(soft_ready, 1)
                own.link(nc.vector.scalar_tensor_tensor(H(t1), H(t1), 0.0, H(t2), ALU.min, ALU.subtract))
                own.link(nc.vector.tensor_tensor_scan(H(cum), H(keep), H(t1), 0.0, ALU.mult, ALU.add))
                own.link(nc.vector.tensor_tensor(H(gates), H(gates), H(cum), ALU.subtract))
                own.link(nc.vector.tensor_copy(H(t2), H(gates)))
                own.link(nc.vector.tensor_scalar(t2[0:HB, 0:1], t2[0:HB, 0:1], 0.0, None, ALU.max))
                dve.wait_ge(par_in, 32)
                own.link(nc.vector.tensor_tensor(sample(t2)[0:HB, :, 0], sample(t2)[0:HB, :, 0], m0[0:HB, :], ALU.max))
                own.link(nc.vector.tensor_tensor_scan(H(M), H(drop), H(t2), NEG, ALU.add, ALU.max))
                own.link(nc.vector.tensor_tensor(t1[0:HB, 0:META], gates[0:HB, 0:META], over(M[0:HB, META - 1:META], [HB, META]),
                                                 ALU.subtract))
                own.link(nc.vector.tensor_tensor(prompt(t1)[0:HB], prompt(gates)[0:HB],
                                                 over(prompt(M)[0:HB, :, P - 1:P], [HB, NT, P]), ALU.subtract))
                own.link(nc.vector.tensor_tensor(sample(t1)[0:HB], sample(gates)[0:HB],
                                                 over(sample(M)[0:HB, :, SLEN - 1:SLEN], [HB, NSEQ, SLEN]), ALU.subtract))
                own.link(nc.vector.tensor_scalar(keep[0:HB, 0:META], M[0:HB, 0:META], -1.0, None, ALU.mult))
                before = M[0:HB, META - 1:META - 1 + SEQ].rearrange("p (j t) -> p j t", t=P)[:, :, 0:1]
                own.link(nc.vector.tensor_tensor(prompt(keep)[0:HB], over(before, [HB, NT, P]), prompt(M)[0:HB], ALU.subtract))
                own.link(nc.vector.tensor_tensor(sample(keep)[0:HB], over(m0[0:HB, :].unsqueeze(2), [HB, NSEQ, SLEN]),
                                                 sample(M)[0:HB], ALU.subtract))
                own.link(nc.vector.tensor_copy(slf[0:HB, 0:1], keep[0:HB, META - 1:META]))
                own.link(nc.vector.tensor_copy(slf[0:HB, 1:9], prompt(keep)[0:HB, :, P - 1]))
                own.link(nc.vector.tensor_copy(slf[0:HB, 9:17], sample(keep)[0:HB, :, SLEN - 1]))
                own.link(nc.vector.tensor_tensor(H(t2), H(M), H(cum), ALU.add))
                nc.vector.tensor_copy(mlast[0:HB, NSEQ:NSEQ + 1], t2[0:HB, PROMPT - 1:PROMPT]).then_inc(arg_ready, 1)
                nc.vector.tensor_copy(mlast[0:HB, 0:NSEQ], sample(t2)[0:HB, :, SLEN - 1]).then_inc(m_ready, 1)
                for g in range(3):
                    dve.wait_ge(turned, g + 1)
                    n = min(4, TT + 1 - 4 * g)
                    src = banks[g][:, :].rearrange("p (t k c) -> p t k c", t=4, k=4)
                    nfull = min(n, TT - 4 * g)
                    own.link(nc.vector.tensor_copy(gtm[:, 4 * g:4 * g + nfull, :, :], src[:, 0:nfull, :, 0:HB]))
                own.link(nc.vector.tensor_copy(gtm[0:META, MT, :, :], src[0:META, 1, :, 0:HB]))
                dve.wait_ge(sl_ready, 1)
                nc.vector.tensor_copy(slb[:, :, :], pX[:, 0:34].rearrange("p (a b) -> p a b", a=2)).then_inc(gtm_ready, 1)
                dve.wait_ge(gtm_ready, 1)

                head = lambda ap: over(ap.unsqueeze(2), [ap.shape[0], HB, 64])
                heads4 = lambda ap: ap.rearrange("p (h v) -> p h v", v=64)
                bd = over(cols(m, "bdB").unsqueeze(1), [P, 2, 2 * VE])
                kwt = kw[:, :]

                nc.vector.tensor_copy(kr[:, :, 0:META], m.fm[:, F_BK:F_BK + 2, 0:META]).then_inc(oper_ready, 1)
                dve.wait_ge(kT_ready, 1)
                nc.vector.tensor_tensor(heads4(kw[0:META, :]), heads4(pK[0:META, 0:256]), head(gtm[0:META, MT, 1, :]),
                                        ALU.mult).then_inc(kw_ready, 1)
                dve.wait_ge(upd_ready, 1)
                nc.vector.tensor_tensor(C[:, :, :], pC[:, 0:4 * VE].rearrange("p (a b) -> p a b", a=2), bd,
                                        ALU.mult).then_inc(state_ready, 1)

                def tile(t, own, sampled):
                    sl = span(t)
                    own.link(nc.vector.tensor_copy(kr[:, :, :], m.fm[:, F_BK:F_BK + 2, sl]))
                    if sampled:
                        for p in range(2):
                            own.link(nc.vector.tensor_copy(bass.AP(qz, p * NSEQ * P, [[2 * NSEQ * P, P], [P + SLEN, NSEQ], [1, SLEN]]),
                                                           sample(m.fm[:, F_BQ + p, :])))
                    else:
                        own.link(nc.vector.tensor_copy(qr[:, :, :], m.fm[:, F_BQ:F_BQ + 2, sl]))
                    for p in range(2):
                        ins = nc.vector.tensor_tensor(qbd[:, p, :, :], over(m.fm[:, F_BQ + p, sl].unsqueeze(1), [P, 2, P]),
                                                      over(cols(m, "headB").unsqueeze(2), [P, 2, P]), ALU.mult)
                        if p == 0:
                            own.link(ins)
                    ins.then_inc(oper_ready, 1)
                    dve.wait_ge(prod_ready, t + 1)
                    own.link(nc.vector.tensor_tensor(W[:, :, :], over(gtm[:, t, 0, :].unsqueeze(2), [P, HB, P]),
                                                     pM[:, :].rearrange("p (h t) -> p h t", h=HB), ALU.subtract))
                    nc.vector.tensor_scalar(W[:, :, :], W[:, :, :], 0.0, None, ALU.min).then_inc(d_ready, 1)
                    dve.wait_ge(kT_ready, t + 2)
                    nc.vector.tensor_tensor(heads4(kwt), heads4(pK[:, 0:256]), head(gtm[:, t, 1, :]), ALU.mult).then_inc(kw_ready, 1)
                    dve.wait_ge(masked, t + 1)
                    nc.vector.tensor_tensor(W[:, :, :], W[:, :, :], pA[:, :].rearrange("p (h t) -> p h t", h=HB),
                                            ALU.mult).then_inc(pm_ready, 1)
                    dve.wait_ge(inter_ready, t + 1)
                    own.link(nc.vector.tensor_tensor(tot[:, :, :], pI[:, 0:4 * VE].rearrange("p (h v) -> p h v", v=VE),
                                                     over(gtm[:, t, 2, :].unsqueeze(2), [P, HB, VE]), ALU.mult))
                    dve.wait_ge(num_ready, t + 1)
                    own.link(nc.vector.tensor_tensor(tot[:, :, :], tot[:, :, :], pN[:, 0:4 * VE].rearrange("p (h v) -> p h v", v=VE),
                                                     ALU.add))
                    own.link(nc.vector.scalar_tensor_tensor(den[:, :], tot[:, :, DVA], -1.0, tot[:, :, DVA], ALU.mult, ALU.max))
                    own.link(nc.vector.tensor_tensor(den[:, :], den[:, :], gtm[:, t, 3, :], ALU.max))
                    own.link(nc.vector.reciprocal(den[:, :], den[:, :]))
                    own.link(nc.vector.tensor_tensor(heads4(m.o[:, t, :]), tot[:, :, 0:DVA], head(den[:, :]), ALU.mult))
                    if sampled:
                        nc.vector.tensor_copy(upd[:, 0, 0:1], den[:, 0:1]).then_inc(h_ready, 1)
                    dve.wait_ge(upd_ready, t + 2)
                first = own.k
                with dve.Fori(0, NT) as t:
                    own = Chain(dve, dve_own, first + STEPS * t)
                    tile(t, own, False)
                    own.link(nc.vector.tensor_tensor(upd[:, :, :], pC[:, 0:4 * VE].rearrange("p (a b) -> p a b", a=2), bd, ALU.mult))
                    own.link(nc.vector.scalar_tensor_tensor(C[:, 0, :], C[:, 0, :], slb[:, 0, ds(t + 1, 1)], upd[:, 0, :],
                                                            ALU.mult, ALU.add))
                    nc.vector.scalar_tensor_tensor(C[:, 1, :], C[:, 1, :], slb[:, 1, ds(t + 1, 1)], upd[:, 1, :],
                                                   ALU.mult, ALU.add).then_inc(state_ready, 1)
                    dve.wait_ge(state_ready, t + 2)
                    own.steps(STEPS)
                own = Chain(dve, dve_own, first + STEPS * NT)
                dve.wait_ge(zeroed, 4)
                tile(NT, own, True)
                dve.wait_ge(c0_in, 16)
                cell = over(cols(m, "bdB"), [P, 2 * VE])
                for i in range(NSEQ):
                    for p in range(2):
                        n = 2 * i + p
                        own.link(nc.vector.tensor_tensor(upd[:, p, :], pair_bank(i, p), cell, ALU.mult))
                        own.link(nc.vector.scalar_tensor_tensor(C0[:, p, i, :], C0[:, p, i, :], slb[:, p, 9 + i:10 + i], upd[:, p, :],
                                                                ALU.mult, ALU.add))
                own.link(nc.vector.tensor_copy(nlast[0:64, :, :], C0[0:64, :, :, DVA]))
                nc.vector.tensor_copy(nlast[64:P, :, :], C0[64:P, :, :, 2 * VE - 1]).then_inc(state_ready, 1)

            @block.scalar
            def _(act):
                own = Chain(act, act_own)
                act.wait_ge(raw_ready, 1)
                act.wait_ge(par_in, 32)
                own.link(nc.scalar.activation(H(t1), m.fm[ROW_F:ROW_F + HB, F_MISC, :], ACT.Identity, bias=bfg[ROW_F:ROW_F + HB, :]))
                own.link(nc.scalar.copy(H(gates), m.fm[ROW_I:ROW_I + HB, F_MISC, :]))
                log_sigmoid_act(nc, act, own, H(t2), H(t1)).then_inc(soft_ready, 1)
                act.wait_ge(arg_ready, 1)
                nc.scalar.activation(gates[32:32 + HB, :], H(t1), ACT.Exp).then_inc(gates_ready, 1)
                nc.scalar.activation(gates[64:64 + HB, :], H(keep), ACT.Exp).then_inc(gates_ready, 1)
                nc.scalar.activation(gates[96:96 + HB, :], H(t2), ACT.Exp, scale=-1.0).then_inc(gates_ready, 1)
                nc.scalar.activation(slf[0:HB, :], slf[0:HB, :], ACT.Exp).then_inc(gates_ready, 1)
                with act.Fori(0, TT) as t:
                    act.wait_ge(d_ready, t + 1)
                    nc.scalar.activation(W[:, :, :], W[:, :, :], ACT.Exp).then_inc(w_ready, 1)

            @block.tensor
            def _(pe):
                pe.wait_ge(gates_ready, 4)
                for g in range(3):
                    for t in range(4 * g, min(4 * g + 4, TT)):
                        mm = nc.tensor.transpose(banks[g][:, P * (t % 4):P * (t % 4) + P], gates[:, META + t * P:META + t * P + P],
                                                 cols(m, "ident"))
                    if g == 2:
                        mm = nc.tensor.transpose(banks[g][0:META, P:2 * P], gates[:, 0:META], cols(m, "ident"))
                    mm.then_inc(turned, 1)
                for p in range(2):
                    mm = nc.tensor.matmul(pX[:, 17 * p:17 * p + 17], cols(m, "selB")[0:HB, P * p:P * p + P], slf[0:HB, :])
                mm.then_inc(sl_ready, 1)

                def keys(t, rows=P):
                    for p in range(2):
                        mm = nc.tensor.transpose(pK[0:rows, P * p:P * p + P], kr[:, p, 0:rows], cols(m, "ident"))
                    mm.then_inc(kT_ready, 1)

                pe.wait_ge(gtm_ready, 1)
                pe.wait_ge(oper_ready, 1)
                keys(-1, META)
                pe.wait_ge(kw_ready, 1)
                pe.wait_ge(zeroed, 4)
                for p in range(2):
                    mm = nc.tensor.matmul(pC[:, 2 * VE * p:2 * VE * (p + 1)], kw[0:META, P * p:P * p + P],
                                          vx[0:META, MT, 2 * p:2 * p + 2, :].rearrange("p h v -> p (h v)"))
                mm.then_inc(upd_ready, 1)

                def scores(t):
                    pe.wait_ge(oper_ready, t + 2)
                    pe.wait_ge(state_ready, t + 1)
                    for h in range(HB):
                        nc.tensor.matmul(pM[:, P * h:P * h + P], cols(m, "selM")[0:HB, P * h:P * h + P], M[0:HB, span(t)])
                    for p in range(2):
                        mm = nc.tensor.matmul(pA[:, 256 * p:256 * p + 256], kr[:, p, :],
                                              qbd[:, p, :, :].rearrange("p h t -> p (h t)"))
                    mm.then_inc(prod_ready, 1)
                    keys(t)

                def numerators(t):
                    pe.wait_ge(pm_ready, t + 1)
                    for h in range(HB):
                        mm = nc.tensor.matmul(pN[:, VE * h:VE * h + VE], W[:, h, :], vx[:, t, h, :])
                    mm.then_inc(num_ready, 1)

                with pe.Fori(0, NT) as t:
                    scores(t)
                    for p in range(2):
                        mm = nc.tensor.matmul(pI[:, 2 * VE * p:2 * VE * (p + 1)], qr[:, p, :], C[:, p, :])
                    mm.then_inc(inter_ready, 1)
                    pe.wait_ge(kw_ready, t + 2)
                    numerators(t)
                    for p in range(2):
                        mm = nc.tensor.matmul(pC[:, 2 * VE * p:2 * VE * (p + 1)], kw[:, P * p:P * p + P],
                                              vx[:, t, 2 * p:2 * p + 2, :].rearrange("p h v -> p (h v)"))
                    mm.then_inc(upd_ready, 1)
                scores(NT)
                pe.wait_ge(c0_in, 16)
                for p in range(2):
                    for i in range(NSEQ):
                        mm = nc.tensor.matmul(pI[:, 2 * VE * p:2 * VE * (p + 1)], qz[:, p, i, :], C0[:, p, i, :],
                                              start=i == 0, stop=i == NSEQ - 1)
                mm.then_inc(inter_ready, 1)
                numerators(NT)
                pe.wait_ge(kw_ready, NT + 2)
                pe.wait_ge(vz_ready, 1)
                pe.wait_ge(h_ready, 1)
                for i in range(NSEQ):
                    for p in range(2):
                        mm = nc.tensor.matmul(pair_bank(i, p), kw[:, P * p:P * p + P], vz[:, i, 2 * VE * p:2 * VE * (p + 1)])
                mm.then_inc(upd_ready, 1)


def phase_dsa(nc, m, d):
    with ExitStack() as ctx:
        sem = Semaphores(nc, "p6_")
        GQ = HC // KVC
        al = Bump(m, "p6_", m.HTO, m.CO)
        qz = al("qz", [P, 4, NSEQ, P])
        kC, vC = al("kC", [P, NSEQ, P]), al("vC", [P, NSEQ, P])
        al = Bump(m, "p6_", m.SCR, m.END - TT * 1024 - BIAS_BYTES)
        logit = al("logit", [P, 2, PROMPT])
        pT = al("pT", [P, 2, NT + 1, P])
        pmax, nmax, total, rden = (al(n, s) for n, s in (("pmax", [P, 2, 4]), ("nmax", [P, 2]),
                                                               ("total", [P, 2, HC]), ("rden", [P, HC])))
        pTz = m.at("p6_pTz", [P, NSEQ, P], m.FMO + F_AQ * ALL * 4)
        pL = [ctx.enter_context(nc.psum_tensor(f"p6_L{i}", [P, 512], F32)) for i in range(4)]
        pP = [ctx.enter_context(nc.psum_tensor(f"p6_P{i}", [P, 4, P], F32)) for i in range(2)]
        pO = [ctx.enter_context(nc.psum_tensor(f"p6_O{i}", [P, 512], F32)) for i in range(2)]

        (caches_in, zeroed, qz_ready, dve_own, logit_ready,
         masked, nmax_ready, exp_ready, turned, pT_copied, o_ready, o_used, act_own) = (sem(n) for n in (
            "caches_in zeroed qz_ready dve_own logit_ready "
            "masked nmax_ready exp_ready turned pT_copied o_ready o_used act_own").split())
        kv_rows = lambda h: slice(64 * (h // GQ), 64 * (h // GQ) + 64)

        heads = [(t, h) for t in range(TT) for h in range(HC)]
        logits = [(t, h, s) for t, h in heads for s in range(len(key_spans(t)))]
        n_logits = {(t, h): sum(1 for x in logits if x[:2] <= (t, h)) for t, h in heads}

        def blocks(t):
            return [(META + P * j, P) for j in range(t + 1)] + [(0, META)] if t < NT else [(0, P), (P, P)]
        groups = [(n, g) for n, (t, h) in enumerate(heads) for g in range(-(-len(blocks(t)) // 4))]

        ctx.enter_context(sem)
        with nc.Block() as block:
            @block.sync
            def _(sp):
                sp.dma_start(kC[:, :, :], d["kT_cache"]).then_inc(caches_in, 16)
                sp.dma_start(vC[:, :, :], d["v_cache"]).then_inc(caches_in, 16)
                sp.wait_ge(caches_in, 32)

            @block.gpsimd
            def _(pool):
                nc.gpsimd.memset(pTz[:, :, :], 0.0).then_inc(zeroed, 1)
                nc.gpsimd.memset(qz[:, :, :, :], 0.0).then_inc(zeroed, 1)
                pool.wait_ge(zeroed, 2)
                own = lambda ap: ap[:, PROMPT:ALL].rearrange("p (i t) -> p i t", t=SLEN)
                for c in range(4):
                    nc.gpsimd.tensor_copy(bass.AP(qz, c * NSEQ * P, [[4 * NSEQ * P, P], [P + SLEN, NSEQ], [1, SLEN]]),
                                          own(m.fm[:, F_CQ + c, :])).then_inc(qz_ready, 1)

            def finish(dve, own, t):
                dve.wait_ge(o_ready, (t + 1) * HC)
                own.link(nc.vector.reciprocal(rden[:, :], total[:, t % 2, :]))
                for c, first in ((AV, 0), (BV, GQ)):
                    ins = nc.vector.tensor_tensor(m.tm[:, t, c:c + 256].rearrange("p (h v) -> p h v", v=64),
                                                  pO[t % 2][:, 64 * first:64 * first + 256].rearrange("p (h v) -> p h v", v=64),
                                                  over(rden[:, first:first + GQ].unsqueeze(2), [P, GQ, 64]), ALU.mult)
                    ins.then_inc(o_used, 1)
                dve.wait_ge(o_used, 2 * t + 2)

            @block.vector
            def _(dve):
                own = Chain(dve, dve_own)
                n_log = 0
                for t in range(TT):
                    for h in range(HC):
                        g = t * HC + h
                        if g >= 2:
                            dve.wait_ge(exp_ready, g - 1)
                            dve.wait_ge(turned, sum(1 for x in groups if x[0] <= g - 2))
                        ks = key_spans(t)
                        for s, (a, b) in enumerate(ks):
                            dve.wait_ge(logit_ready, n_log + 1)
                            nc.vector.tensor_tensor_reduce(logit[:, g % 2, a:b], pL[n_log % 4][:, 0:b - a],
                                                           m.bias[:, KEY_AT[t] + a:KEY_AT[t] + b], 1.0,
                                                           -3e38, ALU.add, ALU.max, pmax[:, g % 2, s:s + 1]).then_inc(masked, 1)
                            n_log += 1
                        dve.wait_ge(masked, n_log)
                        if len(ks) > 1:
                            own.link(nc.vector.tensor_reduce(pmax[:, g % 2, 3:4], pmax[:, g % 2, 0:len(ks)], AX.X, ALU.max))
                            top_col = 3
                        else:
                            top_col = 0
                        nc.vector.tensor_scalar(nmax[:, g % 2:g % 2 + 1], pmax[:, g % 2, top_col:top_col + 1], -DHC ** -0.5, None,
                                                ALU.mult).then_inc(nmax_ready, 1)
                        if h == 1 and t > 0:
                            finish(dve, own, t - 1)
                finish(dve, own, TT - 1)

            @block.scalar
            def _(act):
                def exponent(g):
                    t, h = heads[g]
                    act.wait_ge(nmax_ready, g + 1)
                    if t >= 2 and h == 0:
                        act.wait_ge(o_used, 2 * (t - 2) + 2)
                    nc.scalar.activation(logit[:, g % 2, 0:NK[t]], logit[:, g % 2, 0:NK[t]], ACT.Exp, scale=DHC ** -0.5,
                                         bias=nmax[:, g % 2:g % 2 + 1], accum_out=total[:, t % 2, h:h + 1]).then_inc(exp_ready, 1)

                n_turned = 0

                def copies(g):
                    nonlocal n_turned
                    t, h = heads[g]
                    bl = blocks(t)
                    for k in range(-(-len(bl) // 4)):
                        act.wait_ge(turned, n_turned + 1)
                        if g >= 2:
                            act.wait_ge(o_ready, g - 1)
                        part = bl[4 * k:4 * k + 4]
                        bank = pP[n_turned % 2]
                        full = [x for x in part if x[1] == P]
                        if t == NT:
                            act.wait_ge(zeroed, 2)
                            if g > NT * HC:
                                act.wait_ge(o_ready, g)
                            nc.scalar.copy(bass.AP(pTz, 0, [[NSEQ * P, P], [P + SLEN, NSEQ], [1, SLEN]]),
                                           bank[:, 0, :].rearrange("p (i t) -> p i t", t=SLEN)).then_inc(act_own, 1)
                            nc.scalar.copy(pT[:, g % 2, 0, :], bank[:, 1, :]).then_inc(pT_copied, 1)
                        else:
                            if full:
                                ins = nc.scalar.copy(pT[:, g % 2, 4 * k:4 * k + len(full), :], bank[:, 0:len(full), :])
                            if len(full) < len(part):
                                if full:
                                    ins.then_inc(act_own, 1)
                                ins = nc.scalar.copy(pT[0:META, g % 2, 4 * k + len(full), :], bank[0:META, len(full), :])
                            ins.then_inc(pT_copied, 1)
                        n_turned += 1
                for g in range(len(heads)):
                    t, h = heads[g]
                    exponent(g)
                    if g:
                        copies(g - 1)
                copies(len(heads) - 1)

            @block.tensor
            def _(pe):
                n_log = 0

                def logit_products(g):
                    nonlocal n_log
                    t, h = heads[g]
                    if g == NT * HC:
                        pe.wait_ge(caches_in, 32)
                        pe.wait_ge(qz_ready, 4)
                    q = m.fm[kv_rows(h), F_CQ + h % GQ, q_cols(t)]
                    for a, b in key_spans(t):
                        if n_log >= 4:
                            pe.wait_ge(masked, n_log - 3)
                        bank = pL[n_log % 4]
                        if t < NT:
                            mm = nc.tensor.matmul(bank[:, 0:b - a], q, m.fm[kv_rows(h), F_CK, a:b])
                        else:
                            for i in range(NSEQ):
                                nc.tensor.matmul(bank[:, 0:P], qz[kv_rows(h), h % GQ, i, :], kC[kv_rows(h), i, :],
                                                 start=i == 0, stop=i == NSEQ - 1)
                            mm = nc.tensor.matmul(bank[:, P:SK], q, m.fm[kv_rows(h), F_CK, PROMPT:ALL])
                        mm.then_inc(logit_ready, 1)
                        n_log += 1

                n_turned = 0

                def turn(g):
                    nonlocal n_turned
                    t, h = heads[g]
                    bl = blocks(t)
                    pe.wait_ge(exp_ready, g + 1)
                    for k in range(-(-len(bl) // 4)):
                        if n_turned >= 2:
                            pe.wait_ge(pT_copied, n_turned - 1)
                        for j, (a, n) in enumerate(bl[4 * k:4 * k + 4]):
                            mm = nc.tensor.transpose(pP[n_turned % 2][0:n, j, :], logit[:, g % 2, a:a + n], cols(m, "ident"))
                        mm.then_inc(turned, 1)
                        n_turned += 1

                def values(g):
                    t, h = heads[g]
                    bl = blocks(t)
                    pe.wait_ge(pT_copied, sum(1 for x in groups if x[0] <= g))
                    if h == 0 and t >= 2:
                        pe.wait_ge(o_used, 2 * t - 2)
                    out = pO[t % 2][:, 64 * h:64 * h + 64]
                    c = CV + 64 * (h // GQ)
                    if t == NT:
                        pe.wait_ge(act_own, sum(1 for tt, hh in heads[:NT * HC] if len(blocks(tt)) % 4 != 1) + h + 1)
                        for i in range(NSEQ):
                            nc.tensor.matmul(out, pTz[:, i, :], vC[:, i, c - CV:c - CV + 64], start=i == 0, stop=False)
                        mm = nc.tensor.matmul(out, pT[:, g % 2, 0, :], m.tm[:, SAMPLE, c:c + 64], start=False, stop=True)
                    else:
                        for j, (a, n) in enumerate(bl):
                            src = m.tm[0:n, j if n == P else MT, c:c + 64]
                            mm = nc.tensor.matmul(out, pT[0:n, g % 2, j, :], src, start=j == 0, stop=j == len(bl) - 1)
                    mm.then_inc(o_ready, 1)

                for g in range(len(heads)):
                    t, h = heads[g]
                    logit_products(g)
                    if g:
                        turn(g - 1)
                    if g > 1:
                        values(g - 2)
                turn(len(heads) - 1)
                values(len(heads) - 2)
                values(len(heads) - 1)


def phase_out(nc, m, d):
    with ExitStack() as ctx:
        sem = Semaphores(nc, "p7_")
        al = Bump(m, "p7_", m.FMO, m.CO)
        w, wr, gb = al("w_out", [P, KD, D]), al("w_router", [P, KD, NE]), al("gb", [P, 2, D])
        h0, pre, h1 = (al(n, [P, 3, D]) for n in ("h0", "pre", "h1"))
        al = Bump(m, "p7_", m.SCR, m.END)
        yT, hT = al("yT", [P, 2, KD, P]), al("h1T", [P, 2, KD, P])
        stats, mv = al("stats", [P, 3, 2, 6]), al("mv", [P, 3, 4])
        m.rl = m.at("router_logits", [P, TT, NE], m.END - 1024)
        pT, pH = ctx.enter_context(nc.psum_tensor("p7_T", [P, KD, P], F32)), ctx.enter_context(nc.psum_tensor("p7_H", [P, KD, P], F32))
        pY, pR = ctx.enter_context(nc.psum_tensor("p7_Y", [P, 2, 512], F32)), ctx.enter_context(nc.psum_tensor("p7_R", [P, 512], F32))
        (w_in, dve_own, act_own, pool_own, y_turned, yT_copied, mixed, pre_ready, var_ready, rstd_ready, xn_ready,
         h1_ready, h1_turned, h1T_copied, routed, r_copied) = (sem(n) for n in (
            "w_in dve_own act_own pool_own y_turned yT_copied mixed pre_ready var_ready rstd_ready xn_ready "
            "h1_ready h1_turned h1T_copied routed r_copied").split())
        h0_in, h1_out = [sem(f"h0_in{u}") for u in range(3)], [sem(f"h1_out{u}") for u in range(3)]

        ctx.enter_context(sem)
        with nc.Block() as block:
            @block.sync
            def _(sp):
                for k in range(KD):
                    sp.dma_start(w[:, k, :], d["w_out"][:, k, :]).then_inc(w_in, 16)
                sp.dma_start(wr[:, :, :], d["w_router"]).then_inc(w_in, 16)
                sp.dma_start(gb[:, :, :], d["ln1_gb"].partition_broadcast(P)).then_inc(w_in, 16)
                for t in range(3):
                    sp.dma_start(h0[:, t, :], m.h0_dram[t * P:(t + 1) * P, :]).then_inc(h0_in[t], 16)
                for t in range(TT):
                    u = t % 3
                    if t + 3 < TT:
                        sp.wait_ge(pre_ready, t + 1)
                        sp.dma_start(h0[:, u, :], m.h0_dram[(t + 3) * P:(t + 4) * P, :]).then_inc(h0_in[u], 16)
                    sp.wait_ge(h1_ready, t + 1)
                    sp.dma_start(m.h1_dram[t * P:(t + 1) * P, :], h1[:, u, :]).then_inc(h1_out[u], 16)
                for u in range(3):
                    sp.wait_ge(h1_out[u], 16 * (TT // 3))

            @block.gpsimd
            def _(pool):
                own = Chain(pool, pool_own)
                pool.wait_ge(w_in, 16 * (KD + 2))
                for t in range(TT):
                    u = t % 3
                    pool.wait_ge(xn_ready, t + 1)
                    own.link(nc.gpsimd.tensor_tensor(h1[:, u, :], h1[:, u, :], gb[:, 0, :], ALU.mult))
                    nc.gpsimd.tensor_tensor(h1[:, u, :], h1[:, u, :], gb[:, 1, :], ALU.add).then_inc(h1_ready, 1)

            @block.vector
            def _(dve):
                own = Chain(dve, dve_own)

                def logits(t):
                    dve.wait_ge(routed, t + 1)
                    nc.vector.tensor_copy(m.rl[:, t, :], pR[:, 0:NE]).then_inc(r_copied, 1)
                for t in range(TT):
                    u = t % 3
                    dve.wait_ge(h0_in[u], 16 * (t // 3) + 16)
                    dve.wait_ge(mixed, t + 1)
                    nc.vector.scalar_tensor_tensor(pre[:, u, :], h0[:, u, :], ALPHA, pY[:, :, :].rearrange("p a b -> p (a b)"),
                                                   ALU.mult, ALU.add).then_inc(pre_ready, 1)
                    dve.wait_ge(pre_ready, t + 1)
                    own.link(nc.vector.bn_stats(stats[:, u, 0, :], pre[:, u, 0:512]))
                    own.link(nc.vector.bn_stats(stats[:, u, 1, :], pre[:, u, 512:1024]))
                    own.link(nc.vector.bn_aggr(mv[:, u, 0:2], stats[:, u, :, :]))
                    nc.vector.tensor_scalar(mv[:, u, 3:4], mv[:, u, 1:2], EPS, None, ALU.add).then_inc(var_ready, 1)
                    if t:
                        logits(t - 1)
                    dve.wait_ge(rstd_ready, t + 1)
                    if t >= 3:
                        dve.wait_ge(h1_out[u], 16 * (t // 3))
                        dve.wait_ge(h1_turned, t - 2)
                    nc.vector.tensor_scalar(h1[:, u, :], pre[:, u, :], mv[:, u, 0:1], mv[:, u, 3:4],
                                            ALU.subtract, ALU.mult).then_inc(xn_ready, 1)
                logits(TT - 1)

            @block.scalar
            def _(act):
                own = Chain(act, act_own)

                def y_copy(t):
                    act.wait_ge(y_turned, t + 1)
                    if t >= 2:
                        act.wait_ge(mixed, t - 1)
                    for b in range(2):
                        nc.scalar.copy(yT[:, t % 2, 4 * b:4 * b + 4, :], pT[:, 4 * b:4 * b + 4, :]).then_inc(yT_copied, 1)

                def h_copy(t):
                    act.wait_ge(h1_turned, t + 1)
                    if t >= 2:
                        act.wait_ge(routed, t - 1)
                    for b in range(2):
                        nc.scalar.copy(hT[:, t % 2, 4 * b:4 * b + 4, :], pH[:, 4 * b:4 * b + 4, :]).then_inc(h1T_copied, 1)
                y_copy(0)
                for t in range(TT):
                    u = t % 3
                    if t + 1 < TT:
                        y_copy(t + 1)
                    if t:
                        h_copy(t - 1)
                    act.wait_ge(var_ready, t + 1)
                    own.link(nc.scalar.activation(mv[:, u, 3:4], mv[:, u, 3:4], ACT.Ln))
                    nc.scalar.activation(mv[:, u, 3:4], mv[:, u, 3:4], ACT.Exp, scale=-0.5).then_inc(rstd_ready, 1)
                h_copy(TT - 1)

            @block.tensor
            def _(pe):
                def turn(t):
                    if t:
                        pe.wait_ge(yT_copied, 2 * t)
                    for k in range(KD):
                        mm = nc.tensor.transpose(pT[:, k, :], m.tm[:, t, k * P:(k + 1) * P], cols(m, "ident"))
                    mm.then_inc(y_turned, 1)

                def mix(t):
                    pe.wait_ge(yT_copied, 2 * t + 2)
                    if t:
                        pe.wait_ge(pre_ready, t)
                    for b in range(2):
                        for k in range(KD):
                            mm = nc.tensor.matmul(pY[:, b, :], yT[:, t % 2, k, :], w[:, k, 512 * b:512 * b + 512],
                                                  start=k == 0, stop=k == KD - 1)
                    mm.then_inc(mixed, 1)

                def turn_h1(t):
                    pe.wait_ge(h1_ready, t + 1)
                    if t:
                        pe.wait_ge(h1T_copied, 2 * t)
                    for k in range(KD):
                        mm = nc.tensor.transpose(pH[:, k, :], h1[:, t % 3, k * P:(k + 1) * P], cols(m, "ident"))
                    mm.then_inc(h1_turned, 1)

                def route(t):
                    pe.wait_ge(h1T_copied, 2 * t + 2)
                    if t:
                        pe.wait_ge(r_copied, t)
                    for k in range(KD):
                        mm = nc.tensor.matmul(pR[:, 0:NE], hT[:, t % 2, k, :], wr[:, k, :], start=k == 0, stop=k == KD - 1)
                    mm.then_inc(routed, 1)
                turn(0)
                pe.wait_ge(w_in, 16 * (KD + 2))
                for t in range(TT):
                    if t + 1 < TT:
                        turn(t + 1)
                    if t >= 2:
                        route(t - 2)
                    mix(t)
                    if t:
                        turn_h1(t - 1)
                route(TT - 2)
                turn_h1(TT - 1)
                route(TT - 1)


RING = 4
EARLY = 3
SLOTS = (2 * TOK + NE * (P - 1)) // P


def phase_route(nc, m, d):
    with ExitStack() as ctx:
        sem = Semaphores(nc, "p8_")
        al = Bump(m, "p8_", m.SCR, m.END - 1024)
        T16 = lambda n: al(n, [P, TT, NE])
        s, sb, e1, e2, both, tmp, pos = (T16(n) for n in ("s", "sb", "e1", "e2", "both", "tmp", "pos"))
        br = al("b_router", [P, NE])
        hi, lo = al("hi", [P, TT, NG, 2]), al("lo", [P, TT, NG, 2])
        gs, gm, g1t = al("gs", [P, TT, NG]), al("gm", [P, TT, NG]), al("g1t", [P, TT, NG])
        idx, w1, w2, tot = al("idx", [P, TT]), al("w1", [P, TT]), al("w2", [P, TT]), al("tot", [P, TT])
        ones = al("ones", [P, P])
        before, count = al("before", [P, TT, NE]), al("count", [P, NE])
        ge, ntile, cum, start = al("ge", [P, NE, 9]), al("ntile", [P, NE]), al("cum", [P, NE]), al("start", [P, NE])
        tge, eidf = al("tge", [P, SLOTS, NE]), al("eidf", [P, SLOTS])
        slotf, past = al("slotf", [P, 2, TT]), al("past", [P, SLOTS])
        less = al("less", [P, SLOTS])
        rows = al("rows", [P, 2, TT, 2], I32)
        fill = al("fill", [P, SLOTS * 2], I32)
        m.slot = m.at("slot", [P, 2, TT], m.TMO, U32)
        m.eid = m.at("eid", [P, SLOTS], m.TMO + 128, I32)
        m.wslot = m.at("wslot", [P, SLOTS], m.TMO + 640, I32)
        m.ends = m.at("ends", [P, NE], m.TMO + 800, I32)
        weights = Bump(m, "p9_", m.TMO + 1024, m.CO)
        m.wgu, m.wd = weights("wgu", [P, RING, KD, 2 * DE]), weights("wd", [P, RING, 2, D])
        m.MOE_O = weights.o
        m.table = m.at("table", [P, SLOTS, 2], m.TMO + 320, I32)
        p1 = ctx.enter_context(nc.psum_tensor("p8_1", [P, 512], F32))
        p2 = ctx.enter_context(nc.psum_tensor("p8_2", [P, 512], F32))
        w_first, own_s, b_in, exp_in, exp_out, both_ready, ranked, table_ready, filled, scattered, table_in = (sem(n) for n in (
            "w_first own b_in exp_in exp_out both_ready ranked table_ready filled scattered table_in").split())
        flat = lambda ap: ap.rearrange("p t e -> p (t e)")

        ctx.enter_context(sem)
        with nc.Block() as block:
            @block.sync
            def _(sp):
                sp.dma_start(br[:, :], d["b_router"].partition_broadcast(P)).then_inc(b_in, 16)
                for e in range(EARLY):
                    sp.dma_start(m.wgu[:, e, :, :], d["w_gu"][e, :, :, :]).then_inc(w_first, 16)
                    sp.dma_start(m.wd[:, e, :, :], d["w_down"][e, :, :, :]).then_inc(w_first, 16)
                sp.wait_ge(filled, 1)
                sp.dma_start(m.table_dram.rearrange("(i p) c -> p i c", p=P), fill[:, :].rearrange("p (i c) -> p i c", c=2)).then_inc(filled, 16)
                sp.wait_ge(scattered, 16 * 2 * TT)
                sp.dma_start(m.table[:, :, :], m.table_dram.rearrange("(i p) c -> p i c", p=P)).then_inc(table_in, 16)
                sp.wait_ge(table_in, 16)
                sp.wait_ge(w_first, 32 * EARLY)

            @block.gpsimd
            def _(pool):
                nc.gpsimd.memset(fill[:, :], 0).then_inc(filled, 1)
                pool.wait_ge(filled, 17)
                pool.wait_ge(table_ready, 1)
                for k in range(2):
                    for t in range(TT):
                        pool.indirect_dma_start(m.table_dram[:, :], bass.IndirectOffsetOnAxis(m.slot[:, k, t:t + 1], 0),
                                                rows[:, k, t, :], None).then_inc(scattered, 16)

            @block.scalar
            def _(act):
                act.wait_ge(exp_in, 1)
                nc.scalar.activation(s[:, :, :], m.rl[:, :, :], ACT.Exp, scale=-1.0).then_inc(exp_out, 1)

            @block.tensor
            def _(pe):
                pe.wait_ge(both_ready, 1)
                nc.tensor.matmul(p1[:, 0:TT * NE], cols(m, "tri"), flat(both[:, :, :]))
                nc.tensor.matmul(p2[:, 0:TT * NE], ones[:, :], flat(both[:, :, :])).then_inc(ranked, 1)

            @block.vector
            def _(dve):
                own = Chain(dve, own_s)
                V = nc.vector
                L = own.link
                L(V.memset(ones[:, :], 1.0))
                V.memset(before[:, 0, :], 0.0).then_inc(exp_in, 1)
                dve.wait_ge(exp_in, 1)
                dve.wait_ge(exp_out, 1)
                L(V.tensor_scalar(s[:, :, :], s[:, :, :], 1.0, None, ALU.add))
                L(V.reciprocal(s[:, :, :], s[:, :, :]))
                dve.wait_ge(b_in, 16)
                L(V.tensor_tensor(sb[:, :, :], s[:, :, :], over(br[:, :].unsqueeze(1), [P, TT, NE]), ALU.add))
                q = sb[:, :, :].rearrange("p t (g a b) -> p (t g) a b", g=NG, a=2)
                hv, lv = hi[:, :, :, :].rearrange("p t g a -> p (t g) a"), lo[:, :, :, :].rearrange("p t g a -> p (t g) a")
                gv, tv = gs[:, :, :].rearrange("p t g -> p (t g)"), g1t[:, :, :].rearrange("p t g -> p (t g)")
                L(V.tensor_tensor(hv, q[:, :, :, 0], q[:, :, :, 1], ALU.max))
                L(V.tensor_tensor(lv, q[:, :, :, 0], q[:, :, :, 1], ALU.min))
                L(V.tensor_tensor(gv, hv[:, :, 0], hv[:, :, 1], ALU.max))
                L(V.tensor_tensor(tv, hv[:, :, 0], hv[:, :, 1], ALU.min))
                L(V.tensor_tensor(lv[:, :, 0], lv[:, :, 0], lv[:, :, 1], ALU.max))
                L(V.tensor_tensor(tv, tv, lv[:, :, 0], ALU.max))
                L(V.tensor_tensor(gv, gv, tv, ALU.add))

                def first_max(out, val, n):
                    iota = over(cols(m, "iota16")[:, 0:n].unsqueeze(1), [P, TT, n])
                    L(V.tensor_reduce(idx[:, :], val, AX.X, ALU.max))
                    L(V.tensor_tensor(out, val, over(idx[:, :].unsqueeze(2), [P, TT, n]), ALU.is_equal))
                    L(V.scalar_tensor_tensor(out, out, -100.0, iota, ALU.mult, ALU.add))
                    L(V.tensor_reduce(idx[:, :], out, AX.X, ALU.min))
                    L(V.tensor_tensor(out, out, over(idx[:, :].unsqueeze(2), [P, TT, n]), ALU.is_equal))
                first_max(gm[:, :, :], gs[:, :, :], NG)
                L(V.tensor_scalar(gm[:, :, :], gm[:, :, :], -NEG, NEG, ALU.mult, ALU.add))
                L(V.tensor_tensor(sb[:, :, :].rearrange("p t (g e) -> p (t g) e", g=NG), sb[:, :, :].rearrange("p t (g e) -> p (t g) e", g=NG),
                                  over(gm[:, :, :].rearrange("p t g -> p (t g)").unsqueeze(2), [P, TT * NG, EG]), ALU.add))
                first_max(e1[:, :, :], sb[:, :, :], NE)
                L(V.scalar_tensor_tensor(sb[:, :, :], e1[:, :, :], -1e35, sb[:, :, :], ALU.mult, ALU.add))
                first_max(e2[:, :, :], sb[:, :, :], NE)
                for e, wk in ((e1, w1), (e2, w2)):
                    L(V.tensor_tensor(tmp[:, :, :], e[:, :, :], s[:, :, :], ALU.mult))
                    L(V.tensor_reduce(wk[:, :], tmp[:, :, :], AX.X, ALU.add))
                L(V.tensor_tensor(tot[:, :], w1[:, :], w2[:, :], ALU.add))
                L(V.reciprocal(tot[:, :], tot[:, :]))
                gate = lambda k: rows[:, k, :, 1].bitcast(F32)
                L(V.tensor_tensor(gate(0), w1[:, :], tot[:, :], ALU.mult))
                L(V.tensor_tensor(gate(1), w2[:, :], tot[:, :], ALU.mult))
                for k in range(2):
                    L(V.tensor_copy(rows[:, k, :, 0], cols(m, "rowid")))
                V.tensor_tensor(both[:, :, :], e1[:, :, :], e2[:, :, :], ALU.add).then_inc(both_ready, 1)
                dve.wait_ge(ranked, 1)
                tot16 = p2[:, 0:TT * NE].rearrange("p (t e) -> p t e", e=NE)
                for t in range(1, TT):
                    L(V.tensor_tensor(before[:, t, :], before[:, t - 1, :], tot16[:, t - 1, :], ALU.add))
                L(V.tensor_tensor(count[:, :], before[:, TT - 1, :], tot16[:, TT - 1, :], ALU.add))
                L(V.tensor_tensor(ge[:, :, :], over(count[:, :].unsqueeze(2), [P, NE, 9]),
                                  over(cols(m, "tiles128").unsqueeze(1), [P, NE, 9]), ALU.is_gt))
                L(V.tensor_reduce(ntile[:, :], ge[:, :, :], AX.X, ALU.add))
                L(V.tensor_tensor_scan(cum[:, :], ones[:, 0:NE], ntile[:, :], 0.0, ALU.mult, ALU.add))
                L(V.tensor_tensor(start[:, :], cum[:, :], ntile[:, :], ALU.subtract))
                L(V.tensor_tensor(pos[:, :, :], p1[:, 0:TT * NE].rearrange("p (t e) -> p t e", e=NE), before[:, :, :], ALU.add))
                L(V.scalar_tensor_tensor(pos[:, :, :], over(start[:, :].unsqueeze(1), [P, TT, NE]), float(P), pos[:, :, :],
                                         ALU.mult, ALU.add))
                for k, e in enumerate((e1, e2)):
                    L(V.tensor_tensor(tmp[:, :, :], e[:, :, :], pos[:, :, :], ALU.mult))
                    L(V.tensor_reduce(slotf[:, k, :], tmp[:, :, :], AX.X, ALU.add))
                L(V.tensor_tensor(tge[:, :, :], over(cum[:, :].unsqueeze(1), [P, SLOTS, NE]),
                                  over(cols(m, "slotid").unsqueeze(2), [P, SLOTS, NE]), ALU.is_le))
                L(V.tensor_reduce(eidf[:, :], tge[:, :, :], AX.X, ALU.add))
                L(V.tensor_scalar(eidf[:, :], eidf[:, :], float(NE - 1), None, ALU.min))
                L(V.tensor_copy(m.eid[:, :], eidf[:, :]))
                L(V.tensor_copy(m.ends[:, :], cum[:, :]))
                for c in range(RING, NE, RING):
                    L(V.tensor_scalar(past[:, :], eidf[:, :], float(c), -float(RING), ALU.is_ge, ALU.mult))
                    if c == RING:
                        L(V.tensor_copy(less[:, :], past[:, :]))
                    else:
                        L(V.tensor_tensor(less[:, :], less[:, :], past[:, :], ALU.add))
                L(V.tensor_tensor(eidf[:, :], eidf[:, :], less[:, :], ALU.add))
                L(V.tensor_copy(m.wslot[:, :], eidf[:, :]))
                V.tensor_copy(m.slot[:, :, :], slotf[:, :, :]).then_inc(table_ready, 1)


def phase_moe(nc, m, d):
    with ExitStack() as ctx:
        sem = Semaphores(nc, "p9_")
        al = Bump(m, "p9_", m.MOE_O, m.CO)
        wgu, wd = m.wgu, m.wd
        x, xT, ys = al("x", [P, 3, D]), al("xT", [P, 3, KD, P]), al("ys", [P, 3, D])
        al = Bump(m, "p9_", m.SCR, m.END)
        he, sg, heT = al("he", [P, 3, DE]), al("sg", [P, 3, DE]), al("heT", [P, 3, 2, P])
        entry, gate = al("entry", [P, 3, 2], I32), al("gate", [P, 3, 1], I32)
        pT = ctx.enter_context(nc.psum_tensor("p9_T", [P, KD, P], F32))
        pG = [ctx.enter_context(nc.psum_tensor(f"p9_G{i}", [P, 512], F32)) for i in range(3)]
        pH = ctx.enter_context(nc.psum_tensor("p9_H", [P, 2, P], F32))
        pY = ctx.enter_context(nc.psum_tensor("p9_Y", [P, 2, 512], F32))
        (w_in, gather_held, gate_ready, entry_ready, turned, xT_copied, gu_ready, silu_ready, he_ready, h_turned, heT_ready, y_ready, ys_ready, held) = (
            sem(n) for n in "w_in gather_held gate_ready entry_ready turned xT_copied gu_ready silu_ready he_ready h_turned heT_ready y_ready ys_ready held".split())
        x_in, ys_out = ([sem(f"{n}{u}") for u in range(3)] for n in ("x_in", "ys_out"))
        R = SLOTS // 3
        assert SLOTS == 3 * R

        def turns(eng, step):
            for u in range(3):
                step(0, u, False)
            with eng.Fori(1, R) as r:
                for u in range(3):
                    step(r, u, True)

        ctx.enter_context(sem)
        with nc.Block() as block:
            @block.sync
            def _(sp):
                def load(e, u):
                    sp.dma_start(wgu[:, u, :, :], d["w_gu"][ds(e, 1), :, :, :].rearrange("a p k n -> p (a k) n")).then_inc(w_in, 16)
                    sp.dma_start(wd[:, u, :, :], d["w_down"][ds(e, 1), :, :, :].rearrange("a p k n -> p (a k) n")).then_inc(w_in, 16)
                    sp.wait_ge(w_in, 32 * e + 32)
                    sp.sem_inc(held, 1)

                sp.sem_inc(w_in, 32 * EARLY)
                for e in range(EARLY, RING):
                    load(e, e)
                with sp.Fori(1, NE // RING) as r:
                    for u in range(RING):
                        last = sp.value_load(m.ends[0:1, ds(RING * r + (u - RING), 1)], min_val=0, max_val=SLOTS)
                        sp.wait_ge(y_ready, last)
                        sp.sem_inc(held, 1)
                        load(RING * r + u, u)

            @block.gpsimd
            def _(pool):
                def step(r, u, later):
                    t = 3 * r + u
                    if later:
                        pool.wait_ge(turned, t - 2)
                    nc.gpsimd.tensor_copy(entry[:, u, :], m.table[:, t, :]).then_inc(entry_ready, 1)
                    pool.wait_ge(entry_ready, t + 1)
                    pool.sem_inc(gather_held, 1)
                    pool.indirect_dma_start(x[:, u, :], None, m.h1_dram[:, :],
                                            bass.IndirectOffsetOnAxis(entry[:, u, 0:1].bitcast(U32), 0)).then_inc(x_in[u], 16)
                turns(pool, step)

            @block.vector
            def _(dve):
                def step(r, u, later):
                    t = 3 * r + u
                    if later:
                        dve.wait_ge(he_ready, t - 2)
                    nc.vector.tensor_copy(gate[:, u, :], m.table[:, t, 1:2]).then_inc(gate_ready, 1)
                    dve.wait_ge(gate_ready, t + 1)
                    dve.wait_ge(silu_ready, t + 1)
                    if later:
                        dve.wait_ge(h_turned, t - 2)
                    nc.vector.scalar_tensor_tensor(he[:, u, :], sg[:, u, :], gate[:, u, :].bitcast(F32), pG[u][:, DE:2 * DE],
                                                   ALU.mult, ALU.mult).then_inc(he_ready, 1)
                    dve.wait_ge(h_turned, t + 1)
                    if later:
                        dve.wait_ge(y_ready, t - 2)
                    nc.vector.tensor_copy(heT[:, u, :, :], pH[:, :, :]).then_inc(heT_ready, 1)
                    dve.wait_ge(y_ready, t + 1)
                    if later:
                        dve.wait_ge(ys_out[u], 16 * r)
                    nc.vector.tensor_copy(ys[:, u, :], pY[:, :, :].rearrange("p a b -> p (a b)")).then_inc(ys_ready, 1)
                turns(dve, step)

            @block.scalar
            def _(act):
                def copy_x(r, u, later):
                    t = 3 * r + u
                    act.wait_ge(turned, t + 1)
                    if later:
                        act.wait_ge(gu_ready, t - 2)
                    for b in range(2):
                        nc.scalar.copy(xT[:, u, 4 * b:4 * b + 4, :], pT[:, 4 * b:4 * b + 4, :]).then_inc(xT_copied, 1)

                def step(r, u, later):
                    t = 3 * r + u
                    act.wait_ge(gu_ready, t + 1)
                    if later:
                        act.wait_ge(he_ready, t - 2)
                    nc.scalar.activation(sg[:, u, :], pG[u][:, 0:DE], ACT.Silu).then_inc(silu_ready, 1)

                def store(r, u):
                    t = 3 * r + u
                    act.wait_ge(ys_ready, t + 1)
                    act.dma_start(m.ys_dram[ds(t * P, P), :], ys[:, u, :]).then_inc(ys_out[u], 16)
                copy_x(0, 0, False)
                copy_x(0, 1, False)
                step(0, 0, False)
                copy_x(0, 2, False)
                step(0, 1, False)
                store(0, 0)
                copy_x(1, 0, True)
                step(0, 2, False)
                store(0, 1)
                with act.Fori(1, R - 1) as r:
                    for u in range(3):
                        if u < 2:
                            copy_x(r, u + 1, True)
                        else:
                            copy_x(r + 1, 0, True)
                        step(r, u, True)
                        if u:
                            store(r, u - 1)
                        else:
                            store(r - 1, 2)
                r = R - 1
                copy_x(r, 1, True)
                step(r, 0, True)
                store(r - 1, 2)
                copy_x(r, 2, True)
                step(r, 1, True)
                store(r, 0)
                step(r, 2, True)
                store(r, 1)
                store(r, 2)
                for u in range(3):
                    act.wait_ge(ys_out[u], 16 * R)

            @block.tensor
            def _(pe):
                def turn(r, u, later):
                    t = 3 * r + u
                    pe.wait_ge(x_in[u], 16 * r + 16)
                    if later or u:
                        pe.wait_ge(xT_copied, 2 * t)
                    for k in range(KD):
                        mm = nc.tensor.transpose(pT[:, k, :], x[:, u, k * P:(k + 1) * P], cols(m, "ident"))
                    mm.then_inc(turned, 1)

                def up(r, u, later):
                    t = 3 * r + u
                    e = pe.value_load(m.eid[0:1, ds(t, 1)], min_val=0, max_val=NE - 1)
                    slot = pe.value_load(m.wslot[0:1, ds(t, 1)], min_val=0, max_val=RING - 1)
                    pe.wait_ge(xT_copied, 2 * t + 2)
                    pe.wait_ge(w_in, 32 * e + 32)
                    if later:
                        pe.wait_ge(he_ready, t - 2)
                    for k in range(KD):
                        mm = nc.tensor.matmul(pG[u][:, :], xT[:, u, k, :], wgu[:, ds(slot, 1), k, :].rearrange("p a n -> p (a n)"),
                                              start=k == 0, stop=k == KD - 1)
                    mm.then_inc(gu_ready, 1)

                def down(r, u, later):
                    t = 3 * r + u
                    slot = pe.value_load(m.wslot[0:1, ds(t, 1)], min_val=0, max_val=RING - 1)
                    pe.wait_ge(he_ready, t + 1)
                    if later or u:
                        pe.wait_ge(heT_ready, t)
                    for k in range(2):
                        mm = nc.tensor.transpose(pH[:, k, :], he[:, u, k * P:(k + 1) * P], cols(m, "ident"))
                    mm.then_inc(h_turned, 1)
                    pe.wait_ge(heT_ready, t + 1)
                    if later or u:
                        pe.wait_ge(ys_ready, t)
                    for b in range(2):
                        for k in range(2):
                            mm = nc.tensor.matmul(pY[:, b, :], heT[:, u, k, :],
                                                  wd[:, ds(slot, 1), k, 512 * b:512 * b + 512].rearrange("p a n -> p (a n)"),
                                                  start=k == 0, stop=k == 1)
                    mm.then_inc(y_ready, 1)
                turn(0, 0, False)
                turn(0, 1, False)
                up(0, 0, False)
                turn(0, 2, False)
                up(0, 1, False)
                down(0, 0, False)
                turn(1, 0, True)
                up(0, 2, False)
                down(0, 1, False)
                with pe.Fori(1, R - 1) as r:
                    for u in range(3):
                        if u < 2:
                            turn(r, u + 1, True)
                        else:
                            turn(r + 1, 0, True)
                        up(r, u, True)
                        if u:
                            down(r, u - 1, True)
                        else:
                            down(r - 1, 2, True)
                r = R - 1
                turn(r, 1, True)
                up(r, 0, True)
                down(r - 1, 2, True)
                turn(r, 2, True)
                up(r, 1, True)
                down(r, 0, True)
                up(r, 2, True)
                down(r, 1, True)
                down(r, 2, True)


def phase_finish(nc, m, d):
    with ExitStack() as ctx:
        sem = Semaphores(nc, "pa_")
        al = Bump(m, "pa_", m.TMO + 1024, m.CO)
        gb = al("gb", [P, 2, D])
        a, b, h1, pre, y = (al(n, [P, 3, D]) for n in ("a", "b", "h1", "pre", "y"))
        entry = al("entry", [P, 3, 2], U32)
        stats, mv = al("stats", [P, 3, 2, 6]), al("mv", [P, 3, 4])
        (g_in, dve_own, act_own, pool_own, sum_ready, var_ready, rstd_ready, xn_ready, y_ready, entry_ready) = (sem(n) for n in (
            "g_in dve_own act_own pool_own sum_ready var_ready rstd_ready xn_ready y_ready entry_ready").split())
        ab_in, h1_in, y_out = ([sem(f"{n}{u}") for u in range(3)] for n in ("ab_in", "h1_in", "y_out"))
        ctx.enter_context(sem)
        with nc.Block() as block:
            @block.sync
            def _(sp):
                sp.dma_start(gb[:, :, :], d["ln2_gb"].partition_broadcast(P)).then_inc(g_in, 16)

                for t in range(3):
                    sp.dma_start(h1[:, t, :], m.h1_dram[t * P:(t + 1) * P, :]).then_inc(h1_in[t], 16)
                for t in range(TT):
                    if t + 3 < TT:
                        sp.wait_ge(sum_ready, t + 1)
                        sp.dma_start(h1[:, t % 3, :], m.h1_dram[(t + 3) * P:(t + 4) * P, :]).then_inc(h1_in[t % 3], 16)
                    sp.wait_ge(y_ready, t + 1)
                    sp.dma_start(d["y"][t * P:(t + 1) * P, :], y[:, t % 3, :]).then_inc(y_out[t % 3], 16)
                for u in range(3):
                    sp.wait_ge(y_out[u], 16 * (TT // 3))

            @block.gpsimd
            def _(pool):
                def gather(t, u):
                    pool.wait_ge(entry_ready, t + 1)
                    if t >= 3:
                        pool.wait_ge(sum_ready, t - 2)
                    for k, dst in ((0, a), (1, b)):
                        pool.indirect_dma_start(dst[:, u, :], None, m.ys_dram[:, :],
                                                bass.IndirectOffsetOnAxis(entry[:, u, k:k + 1], 0)).then_inc(ab_in[u], 16)
                own = Chain(pool, pool_own)
                for t in range(3):
                    gather(t, t)
                pool.wait_ge(g_in, 16)
                for t in range(TT):
                    pool.wait_ge(xn_ready, t + 1)
                    own.link(nc.gpsimd.tensor_tensor(y[:, t % 3, :], y[:, t % 3, :], gb[:, 0, :], ALU.mult))
                    nc.gpsimd.tensor_tensor(y[:, t % 3, :], y[:, t % 3, :], gb[:, 1, :], ALU.add).then_inc(y_ready, 1)
                    if t + 3 < TT:
                        gather(t + 3, t % 3)

            @block.vector
            def _(dve):
                def entries(t, u):
                    if t >= 3:
                        dve.wait_ge(ab_in[u], 32 * (t // 3))
                    nc.vector.tensor_copy(entry[:, u, :], m.slot[:, :, t]).then_inc(entry_ready, 1)

                def total(t, u):
                    own = Chain(dve, dve_own, 3 * t)
                    dve.wait_ge(ab_in[u], 32 * (t // 3) + 32)
                    dve.wait_ge(h1_in[u], 16 * (t // 3) + 16)
                    own.link(nc.vector.tensor_tensor(a[:, u, :], a[:, u, :], b[:, u, :], ALU.add))
                    if t >= 3:
                        dve.wait_ge(xn_ready, t - 2)
                    nc.vector.scalar_tensor_tensor(pre[:, u, :], h1[:, u, :], ALPHA, a[:, u, :],
                                                   ALU.mult, ALU.add).then_inc(sum_ready, 1)
                    dve.wait_ge(sum_ready, t + 1)
                    nc.vector.bn_stats(stats[:, u, 0, :], pre[:, u, 0:512])
                    own.link(nc.vector.bn_stats(stats[:, u, 1, :], pre[:, u, 512:1024]))
                    own.link(nc.vector.bn_aggr(mv[:, u, 0:2], stats[:, u, :, :]))
                    nc.vector.tensor_scalar(mv[:, u, 3:4], mv[:, u, 1:2], EPS, None, ALU.add).then_inc(var_ready, 1)

                def normal(t, u):
                    dve.wait_ge(rstd_ready, t + 1)
                    if t >= 3:
                        dve.wait_ge(y_out[u], 16 * (t // 3))
                    nc.vector.tensor_scalar(y[:, u, :], pre[:, u, :], mv[:, u, 0:1], mv[:, u, 3:4],
                                            ALU.subtract, ALU.mult).then_inc(xn_ready, 1)
                for t in range(3):
                    entries(t, t)
                for t in range(TT):
                    total(t, t % 3)
                    if t + 3 < TT:
                        entries(t + 3, t % 3)
                    if t:
                        normal(t - 1, (t - 1) % 3)
                normal(TT - 1, (TT - 1) % 3)

            @block.scalar
            def _(act):
                own = Chain(act, act_own)
                for t in range(TT):
                    act.wait_ge(var_ready, t + 1)
                    own.link(nc.scalar.activation(mv[:, t % 3, 3:4], mv[:, t % 3, 3:4], ACT.Ln))
                    nc.scalar.activation(mv[:, t % 3, 3:4], mv[:, t % 3, 3:4], ACT.Exp, scale=-0.5).then_inc(rstd_ready, 1)


class Shared:
    pass


def build(nc, d):
    m = Shared()
    base = (nc.sbuf_base + 63) // 64 * 64

    def at(name, shape, offset, dtype=F32):
        return nc.alloc_sbuf_tensor_at(name, shape, dtype, offset=base + offset)
    m.at = at
    m.TMO = 0
    m.FMO = m.TMO + (TT + 1) * TM * 4
    m.HTO = m.FMO + FM * ALL * 4
    m.CO = m.HTO + KD * ALL * 4
    m.SCR = m.CO + (NCONST * 4 + 63) // 64 * 64
    m.END = (nc.sbuf_usable_end - base) // 64 * 64
    m.tm = at("tm", [P, TT + 1, TM], m.TMO)
    m.fm = at("fm", [P, FM, ALL], m.FMO)
    m.hT = at("hT", [P, KD, ALL], m.HTO)
    m.const = at("const", [P, NCONST], m.CO)
    m.h0_dram = nc.dram_tensor("h0_rows", (TOK, D), F32, kind="Internal").ap()
    m.h1_dram = nc.dram_tensor("h1_rows", (TOK, D), F32, kind="Internal").ap()
    m.table_dram = nc.dram_tensor("slot_table", (SLOTS * P, 2), I32, kind="Internal").ap()
    m.ys_dram = nc.dram_tensor("expert_rows", (SLOTS * P, D), F32, kind="Internal").ap()
    for phase in PHASES:
        phase(nc, m, d)


OUTS = {
    "y": (TOK, D),
    "p_k": (PROMPT, 128), "p_v": (PROMPT, 128), "p_kidx": (PROMPT, DI),
    "p_gla": (HA, DKA, DVA), "p_c": (HB, DHB, DHB), "p_n": (HB, DHB), "p_m": (HB, 1), "p_conv": (4, P, 3),
    "s_k": (P, 128), "s_v": (P, 128), "s_kidx": (P, DI),
    "s_gla": (HA, DKA, NSEQ, DVA), "s_c": (HB, DHB, NSEQ, DHB), "s_n": (HB, DHB, NSEQ), "s_m": (HB, NSEQ),
    "s_conv": (4, P, NSEQ, 3),
}


def constants():
    p = np.arange(P)[:, None]
    c = lambda n: np.arange(n)[None, :]
    selM = np.zeros((P, 512), np.float32)
    selM[0:HB] = c(512) // P == np.arange(HB)[:, None]
    selB = np.zeros((P, 256), np.float32)
    selB[0:HB] = c(256) // DHB == np.arange(HB)[:, None]
    v = {
        "ident": p == c(P), "headA": p // DKA == c(HA), "bdA": p // DKA == c(256) // DVA,
        "causal": p <= c(P), "blocked": (p <= c(P)) & (p // SLEN == c(P) // SLEN),
        "seqmask": p // SLEN == c(NSEQ), "bdB": p // DHB == c(130) // 65, "headB": p // DHB == c(2),
        "otherseq": np.where(p // SLEN == c(P) // SLEN, 0.0, NEG), "tri": p < c(P),
        "iota16": c(NE) + 0 * p, "tiles128": P * c(9) + 0 * p, "rowid": p + P * c(TT), "slotid": c(33) + 0 * p, "selM": selM, "selB": selB,
    }
    return np.ascontiguousarray(np.concatenate([np.asarray(v[n], np.float32) for n in CONSTS], axis=1))


def lay_out(q):
    w, b = q["w_in"][0], q["b_in"][0]
    names = (('a_q', 128), ('a_k', 128), ('a_v', 256), ('a_g', 16), ('a_r', 256), ('b_qk', 512), ('b_v', 256),
             ('b_i', 4), ('b_f', 4), ('b_o', 256), ('c_q', 512), ('c_k', 128), ('c_v', 128), ('c_qi', 128),
             ('c_w', 4), ('c_ki', 32))
    s, at = {}, 0
    for n, k in names:
        s[n] = np.arange(at, at + k)
        at += k

    def pick(parts):
        return (np.concatenate([w[:, x] if not isinstance(x, int) else np.zeros((D, x), w.dtype) for x in parts], axis=1),
                np.concatenate([b[x] if not isinstance(x, int) else np.zeros((x,), b.dtype) for x in parts]))

    wt, bt = pick([s["a_v"], s["a_r"], s["b_v"], s["b_o"], s["c_v"], s["c_k"], s["c_ki"], s["c_w"], TM - CW - 4])
    cq = [np.concatenate([s["c_q"][64 * j:64 * j + 64], s["c_q"][64 * (j + 4):64 * (j + 4) + 64]]) for j in range(4)]
    wf, bf = pick([s["c_qi"]] + [s["c_ki"]] * HI + [s["a_q"], s["a_k"], s["b_qk"]] + cq
                  + [s["c_k"], s["a_g"], 16, s["b_i"], 28, s["b_f"], 60])
    o = {
        "consts": constants(),
        "x": np.concatenate([q["x_prompt"][0], q["x_sample"].reshape(P, D), q["meta_tokens"]]),
        "ln_in_gb": np.stack([q["ln_in_g"], q["ln_in_b"]]),
        "w_tm": wt.reshape(KD, P, TM).transpose(1, 0, 2), "b_tm": bt,
        "w_fm": wf.reshape(KD, P, FM, P).transpose(2, 1, 0, 3), "b_fm": bf.reshape(FM, P).T,
    }
    o.update(lay_out_rest(q))
    return {k: np.ascontiguousarray(v) for k, v in o.items()}


def kernel(**inputs):
    import concourse.bacc as bacc
    from concourse.bass_utils import run_bass_kernel_spmd

    q = {k: np.asarray(v) for k, v in inputs.items()}
    arrays = lay_out(q)
    nc = bacc.Bacc("TRN2", target_bir_lowering=False, num_devices=1)
    d = {k: nc.dram_tensor("in_" + k, v.shape, F32, kind="ExternalInput").ap() for k, v in arrays.items()}
    d.update({k: nc.dram_tensor("out_" + k, s, F32, kind="ExternalOutput").ap() for k, s in OUTS.items()})
    build(nc, d)
    r = run_bass_kernel_spmd(nc, [{"in_" + k: v for k, v in arrays.items()}], core_ids=[0]).results[0]
    g = {k: np.asarray(r["out_" + k]) for k in OUTS}
    rows = lambda n, *s: g[n].reshape(*s)
    return (
        g["y"][0:SEQ].reshape(1, SEQ, D), g["y"][SEQ:TOK].reshape(NSEQ, SLEN, D),
        rows("p_k", 1, 1, PROMPT, KVC, DHC), rows("p_v", 1, 1, PROMPT, KVC, DHC), rows("p_kidx", 1, 1, PROMPT, DI),
        g["p_gla"][None, None], g["p_c"].transpose(0, 2, 1)[None, None], g["p_n"][None, None],
        g["p_m"].reshape(1, 1, HB), g["p_conv"].transpose(2, 0, 1).reshape(1, 1, 3, 512),
        rows("s_k", 1, NSEQ, SLEN, KVC, DHC), rows("s_v", 1, NSEQ, SLEN, KVC, DHC), rows("s_kidx", 1, NSEQ, SLEN, DI),
        g["s_gla"].transpose(2, 0, 1, 3)[None], g["s_c"].transpose(2, 0, 3, 1)[None], g["s_n"].transpose(2, 0, 1)[None],
        g["s_m"].T[None], g["s_conv"].transpose(2, 3, 0, 1).reshape(1, NSEQ, 3, 512),
    )
def lay_out_rest(q):
    P, NSEQ = 128, 8
    cw, cb = q["conv_w"][0], q["conv_b"][0]
    bd = np.zeros((HA, DKA, NSEQ, HA, DVA), np.float32)
    for h in range(HA):
        bd[h, :, :, h, :] = q["state_gla"][0][:, h].transpose(1, 0, 2)
    cbd = np.zeros((2, 2, DHB, NSEQ, 2, DHB + 1), np.float32)
    for h in range(HB):
        cbd[h // 2, h % 2, :, :, h % 2, 0:DHB] = q["state_mlstm_c"][0][:, h].transpose(2, 0, 1)
        cbd[h // 2, h % 2, :, :, h % 2, DHB] = q["state_mlstm_n"][0][:, h].T
    wo = q["w_out"][0]
    wo = np.concatenate([wo[512:768], wo[0:256], wo[768:1024], wo[256:512]])
    e = lambda w, k: w.reshape(NE, k, P, -1).transpose(0, 2, 1, 3)
    return {
        "w_out": wo.reshape(KD, P, D).transpose(1, 0, 2), "ln1_gb": np.stack([q["ln1_g"][0], q["ln1_b"][0]]),
        "w_router": q["w_router"].reshape(KD, P, NE).transpose(1, 0, 2), "b_router": q["b_router"],
        "w_gu": e(np.concatenate([q["w_gate"][0], q["w_up"][0]], axis=2), KD), "w_down": e(q["w_down"][0], 2),
        "ln2_gb": np.stack([q["ln2_g"][0], q["ln2_b"][0]]),
        "kT_cache": q["cache_k"][0].transpose(2, 3, 0, 1).reshape(P, NSEQ, P),
        "kiT_cache": np.concatenate([q["cache_kidx"][0].transpose(2, 0, 1)] * HI),
        "v_cache": q["cache_v"][0].transpose(1, 0, 2, 3).reshape(P, NSEQ, P),
        "mlstm_bd": cbd.reshape(2, P, NSEQ, 2 * DHB + 2).transpose(1, 0, 2, 3), "m0": q["state_mlstm_m"][0].T,
        "b_forget": q["b_forget"][0].reshape(HB, 1), "g_gla_norm": q["g_gla_norm"][0], "g_mlstm_norm": q["g_mlstm_norm"][0],
        "conv_hist": q["state_conv"][0].reshape(NSEQ, 3, 4, P).transpose(3, 2, 0, 1),
        "conv_wb": np.concatenate([cw, cb[None]]).reshape(5, 4, P).transpose(2, 1, 0),
        "w_gla_gate": q["w_gla_gate"][0], "b_gla_gate": q["b_gla_gate"][0].reshape(P, 1),
        "gla_bd": bd.reshape(P, NSEQ, 256),
    }
PHASES = [phase_norm_in, phase_project, phase_conv, phase_gla, phase_norm_gla, phase_mlstm, phase_norm_mlstm, phase_dsa,
          phase_out, phase_route, phase_moe, phase_finish]
```

```python
from contextlib import ExitStack

import concourse.bass as bass
import numpy as np
from concourse import mybir

F32 = mybir.dt.float32
I32 = mybir.dt.int32
U32 = mybir.dt.uint32
BF16 = mybir.dt.bfloat16
ALU = mybir.AluOpType
ACT = mybir.ActivationFunctionType
AX = mybir.AxisListType
ds = bass.ds

P = 128
D = 1024
KD = D // P
SEQ, NSEQ, SLEN, META = 1024, 8, 16, 16
NT = SEQ // P
SAMPLE = NT
MT = NT + 1
TOK = SEQ + NSEQ * SLEN
TT = TOK // P
ALL = TOK + META
PROMPT = META + SEQ
PAST = 128
HA, DKA, DVA, RANK = 4, 32, 64, 16
HB, DHB = 4, 64
HC, KVC, DHC = 8, 2, 64
HI, DI = 4, 32
TOPK_P, TOPK_S = 256, (PAST + SLEN) // 4
NE, NG, EG, DE = 16, 4, 4, 256
EPS = 1e-5
ALPHA = 2 ** 0.25
NEG = -1e30
BIAS_BYTES = 10240
TAKEN = -3e38

AV, AR, BV, BO, CV, CW, CK, CI = 0, 256, 512, 768, 1024, 1152, 1160, 1288
TM, TG = 1320, 386
TP = 3 * TG
F_QI, F_KI, F_AQ, F_AK, F_BQ, F_BK, F_CQ, F_CK, F_MISC = 0, 1, 2, 3, 4, 6, 8, 12, 13
FM = 14
ROW_I, ROW_F = 32, 64

CONSTS = {}
_at = 0
for _name, _n in (("ident", P), ("headA", HA), ("bdA", 256), ("causal", P), ("blocked", P),
                  ("seqmask", NSEQ), ("bdB", 130), ("headB", 2), ("otherseq", P), ("tri", P),
                  ("iota16", NE), ("tiles128", 9), ("rowid", TT), ("slotid", 33), ("selM", 512), ("selB", 256)):
    CONSTS[_name] = (_at, _at + _n)
    _at += _n
NCONST = _at


class Chain:

    def __init__(self, eng, sem, base=0):
        self.eng, self.sem, self.base, self.k = eng, sem, base, 0

    def link(self, ins):
        self.k += 1
        ins.then_inc(self.sem, 1)
        self.eng.wait_ge(self.sem, self.base + self.k)

    def steps(self, n):
        assert self.k == n, (self.k, n)


class Semaphores:

    def __init__(self, nc, tag):
        self.nc, self.tag, self.made = nc, tag, []

    def __call__(self, name):
        self.made.append(self.nc.alloc_semaphore(self.tag + name))
        return self.made[-1]

    def __enter__(self):
        return self

    def __exit__(self, *error):
        if not any(error):
            self.nc.clear_and_free_semaphores(self.made)
            self.nc.all_engine_barrier()


def cols(m, name):
    a, b = CONSTS[name]
    return m.const[:, a:b]


class Bump:

    def __init__(self, m, tag, start, end):
        self.m, self.tag, self.o, self.end = m, tag, start, end

    def __call__(self, name, shape, dtype=F32):
        n = int(np.prod(shape[1:])) * 4
        at = self.o
        self.o = at + (n + 31) // 32 * 32
        assert self.o <= self.end, (self.tag, name, self.o - self.end)
        return self.m.at(self.tag + name, shape, at, dtype)


def over(ap, shape):
    return ap.broadcast_to(shape)


def phase_norm_in(nc, m, d):
    with ExitStack() as ctx:
        sem = Semaphores(nc, "p1_")
        al = Bump(m, "p1_", m.FMO + F_AQ * ALL * 4, m.HTO)
        m.wtm, m.btm = al("wtm", [P, KD, TP]), al("btm", [P, TP])
        m.own_o = al.o
        al = Bump(m, "p1_", m.SCR, m.END)
        m.wfm = al("wfm", [P, 2, KD, P])
        gb, x, h0 = al("gb", [P, 2, D]), al("x", [P, 3, D]), al("h0", [P, 3, D])
        stats, mv = al("stats", [P, 3, 2, 6]), al("mv", [P, 3, 4])
        pT = [ctx.enter_context(nc.psum_tensor(f"p1_T{i}", [P, 4, P], F32)) for i in range(2)]
        gb_in, consts_in, w_in = sem("gb_in"), sem("consts_in"), sem("w_in")
        x_in, h0_out = [sem(f"x_in{i}") for i in range(3)], [sem(f"h0_out{i}") for i in range(3)]
        dve_own, act_own, scaled = sem("dve_own"), sem("act_own"), sem("scaled")
        var_ready, rstd_ready, xn_ready, h0_ready = sem("var_ready"), sem("rstd_ready"), sem("xn_ready"), sem("h0_ready")
        turned, hT_copied = sem("turned"), sem("hT_copied")

        ctx.enter_context(sem)
        with nc.Block() as block:
            @block.sync
            def _(sp):
                for u in range(3):
                    sp.dma_start(x[:, u, :], d["x"][u * P:(u + 1) * P, :]).then_inc(x_in[u], 16)
                    if u == 0:
                        sp.dma_start(gb[:, :, :], d["ln_in_gb"].partition_broadcast(P)).then_inc(gb_in, 16)
                        sp.dma_start(m.const[:, :], d["consts"]).then_inc(consts_in, 16)
                for k in range(KD // 2):
                    sp.dma_start(m.wtm[:, k, :], d["w_tm"][:, k, :]).then_inc(w_in, 16)
                with sp.Fori(1, 3) as r:
                    for u in range(3):
                        sp.wait_ge(xn_ready, 3 * r + (u - 2))
                        sp.dma_start(x[:, u, :], d["x"][ds((3 * r + u) * P, P), :]).then_inc(x_in[u], 16)
                sp.wait_ge(xn_ready, 7)
                sp.dma_start(x[0:META, 0, :], d["x"][TOK:ALL, :]).then_inc(x_in[0], 16)
                for k in range(KD // 2, KD):
                    sp.dma_start(m.wtm[:, k, :], d["w_tm"][:, k, :]).then_inc(w_in, 16)
                sp.dma_start(m.btm[:, :], d["b_tm"].partition_broadcast(P)).then_inc(w_in, 16)
                for u in range(2):
                    sp.dma_start(m.wfm[:, u, :, :], d["w_fm"][u, :, :, :]).then_inc(w_in, 16)
                sp.wait_ge(w_in, 16 * (KD + 3))

            @block.gpsimd
            def _(pool):
                pool.wait_ge(gb_in, 16)

                def scale(r, u, rows=P):
                    t = 3 * r + u
                    pool.wait_ge(scaled, t + 1)
                    nc.gpsimd.tensor_tensor(h0[0:rows, u, :], h0[0:rows, u, :], gb[0:rows, 1, :],
                                            ALU.add).then_inc(h0_ready, 1)

                with pool.Fori(0, 3) as r:
                    for u in range(3):
                        scale(r, u)
                scale(3, 0, META)

            @block.vector
            def _(dve):
                def variance(r, u, rows=P):
                    t = 3 * r + u
                    own = Chain(dve, dve_own, 3 * t)
                    dve.wait_ge(x_in[u], 16 * (r + 1))
                    own.link(nc.vector.bn_stats(stats[0:rows, u, 0, :], x[0:rows, u, 0:512]))
                    own.link(nc.vector.bn_stats(stats[0:rows, u, 1, :], x[0:rows, u, 512:1024]))
                    nc.vector.tensor_copy(mv[0:rows, u, 3:4], stats[0:rows, u, 1, 0:1])
                    own.link(nc.vector.bn_aggr(mv[0:rows, u, 0:2], stats[0:rows, u, :, :]))
                    nc.vector.tensor_scalar(mv[0:rows, u, 2:3], mv[0:rows, u, 1:2], EPS, None,
                                            ALU.add).then_inc(var_ready, 1)

                def normal(r, u, rows=P, fresh=False):
                    t = 3 * r + u
                    dve.wait_ge(rstd_ready, t + 1)
                    if not fresh:
                        dve.wait_ge(h0_out[u], 16 * r)
                        dve.wait_ge(turned, 2 * t - 4)
                    nc.vector.tensor_scalar(h0[0:rows, u, :], x[0:rows, u, :], mv[0:rows, u, 0:1], mv[0:rows, u, 3:4],
                                            ALU.subtract, ALU.mult).then_inc(xn_ready, 1)
                    dve.wait_ge(xn_ready, t + 1)
                    nc.vector.tensor_tensor(h0[0:rows, u, :], h0[0:rows, u, :], gb[0:rows, 0, :], ALU.mult).then_inc(scaled, 1)
                dve.wait_ge(gb_in, 16)
                variance(0, 0)
                for u in range(3):
                    if u < 2:
                        variance(0, u + 1)
                    normal(0, u, fresh=True)
                with dve.Fori(1, 3) as r:
                    for u in range(3):
                        variance(r, u)
                        normal(r, u)
                variance(3, 0, META)
                normal(3, 0, META)

            @block.scalar
            def _(act):
                def rstd(r, u, rows=P):
                    t = 3 * r + u
                    own = Chain(act, act_own, t)
                    act.wait_ge(var_ready, t + 1)
                    own.link(nc.scalar.activation(mv[0:rows, u, 3:4], mv[0:rows, u, 2:3], ACT.Ln))
                    nc.scalar.activation(mv[0:rows, u, 3:4], mv[0:rows, u, 3:4], ACT.Exp, scale=-0.5).then_inc(rstd_ready, 1)

                def copy(r, u, rows=P):
                    t = 3 * r + u
                    dst = m.hT[:, :, ds(META + t * P, P)] if rows == P else m.hT[:, :, 0:META]
                    act.wait_ge(h0_ready, t + 1)
                    if rows == P:
                        act.dma_start(m.h0_dram[ds(t * P, P), :], h0[:, u, :]).then_inc(h0_out[u], 16)
                    for b in range(2):
                        act.wait_ge(turned, 2 * t + b + 1)
                        nc.scalar.copy(dst[:, 4 * b:4 * b + 4, :], pT[b][:, :, 0:rows]).then_inc(hT_copied, 1)

                rstd(0, 0)
                for u in range(1, 3):
                    rstd(0, u)
                    copy(0, u - 1)
                with act.Fori(1, 3) as r:
                    for u in range(3):
                        rstd(r, u)
                        if u:
                            copy(r, u - 1)
                        else:
                            copy(r - 1, 2)
                rstd(3, 0, META)
                copy(2, 2)
                copy(3, 0, META)
                for u in range(3):
                    act.wait_ge(h0_out[u], 48)

            @block.tensor
            def _(pe):
                pe.wait_ge(consts_in, 16)

                def turn(r, u, rows=P):
                    t = 3 * r + u
                    pe.wait_ge(h0_ready, t + 1)
                    for b in range(2):
                        if not isinstance(r, int) or r or u:
                            pe.wait_ge(hT_copied, 2 * t - 1 + b)
                        for k in range(4):
                            mm = nc.tensor.transpose(pT[b][:, k, 0:rows], h0[0:rows, u, (4 * b + k) * P:(4 * b + k + 1) * P],
                                                     cols(m, "ident")[0:rows, 0:rows])
                        mm.then_inc(turned, 1)
                for u in range(3):
                    turn(0, u)
                with pe.Fori(1, 3) as r:
                    for u in range(3):
                        turn(r, u)
                turn(3, 0, META)


SK = 2 * P
NK = [META + P * (t + 1) for t in range(NT)] + [SK]
KEY_AT = [sum(NK[:t]) for t in range(TT + 1)]
LATE = (NT - 2, NT - 1)
LEFT = [NT - 1] * (TOPK_P // 8)
EXTRA = 4
SCORE_AT = [sum(NK[s] for s in range(t) if (s in LATE) == (t in LATE)) for t in range(TT)] + [
    sum(NK[t] for t in range(TT) if t not in LATE) + EXTRA]


def spans_of(n):
    parts = -(-n // 512)
    width = -(-n // parts // 16) * 16
    return [(a, min(a + width, n)) for a in range(0, n, width)]


def key_spans(t):
    return spans_of(NK[t]) if t < NT else [(0, SK)]


def q_cols(t):
    return slice(META + P * t, META + P * t + P)


def score_of(m, score, t, a, b):
    buf = m.late_score if t in LATE else score
    return buf[:, SCORE_AT[t] + a:SCORE_AT[t] + b]


def key_bias(nc, own, m, t, taken):
    N, at = NK[t], KEY_AT[t]
    if taken is None:
        own.link(nc.vector.memset(m.bias[:, at:at + N], 0.0))
    else:
        own.link(nc.vector.tensor_scalar(m.bias[:, at:at + N], taken, TAKEN, NEG, ALU.not_equal, ALU.mult))
    if t < NT:
        own.link(nc.vector.memset(m.bias[0:64, at + N - 64:at + N], NEG))
    else:
        own.link(nc.vector.tensor_tensor(m.bias[:, at + P:at + N], m.bias[:, at + P:at + N], cols(m, "otherseq"), ALU.add))


def phase_project(nc, m, d):
    with ExitStack() as ctx:
        sem = Semaphores(nc, "p2_")
        m.bias = m.at("key_bias", [P, KEY_AT[TT]], m.END - TT * 1024 - BIAS_BYTES, BF16)
        al = Bump(m, "p2_", m.SCR, m.END - TT * 1024 - BIAS_BYTES)
        al.o += 2 * KD * P * 4
        w, score = m.wfm, al("score", [P, SCORE_AT[TT]])
        hist, up, wc = al("hist", [P, 4, NSEQ, 3]), al("up", [P, NSEQ, SLEN + 3]), al("wc", [P, 4, 5])
        last_p, last_s = al("last_p", [P, 4, 3]), al("last_s", [P, 4, NSEQ, 3])
        both = Bump(m, "p2_", al.o, al.o + 8192)
        relu = al("relu", [P, 4, 512])
        acc, part = both("acc", [P, ALL]), both("part", [P, PROMPT // 2 + P])
        al = Bump(m, "p2_", m.END - TT * 1024, m.END)
        m.late_score = al("late_score", [P, sum(NK[t] for t in LATE)])
        bfm, top = al("bfm", [P, FM]), al("top", [P, 8])
        al = Bump(m, "p2_", m.own_o, m.HTO)
        qiz, kiC = al("qiz", [P, NSEQ, P]), al("kiC", [P, NSEQ, P])
        ps = [ctx.enter_context(nc.psum_tensor(f"p2_{i}", [P, 512], F32)) for i in range(6)]
        w_in = [sem("w_in0"), sem("w_in1")]
        (b_in, rows_out, kiC_in, fm_ready, fm_copied, tm_ready, tm_copied, bias_added, zeroed, qiz_ready,
         raw_ready, relu_ready, relu_used, dve_own, round_own, conv_in, pool_own, acc_ready, silu_ready, keys_scaled, conv_out, rows_ready, rows_copied) = (sem(n) for n in (
            "b_in rows_out kiC_in fm_ready fm_copied tm_ready tm_copied bias_added zeroed qiz_ready "
            "raw_ready relu_ready relu_used dve_own round_own conv_in pool_own acc_ready silu_ready keys_scaled conv_out rows_ready rows_copied").split())
        spans = [(0, 512), (512, 1024), (1024, ALL)]
        i_rows = lambda h: slice(DI * h, DI * h + DI)
        n_relu = HI * sum(len(key_spans(t)) for t in range(TT))
        others = [(t, g) for t in range(TT + 1) for g in range(2)]
        order = []
        for t in range(TT):
            fill = {1: 4, 2: 6, 3: 8}.get(t, 0)
            order += [("tokens", t, 2), ("scores", t, 0)] + [("tokens", *x) for x in others[:fill]]
            others = others[fill:]
        order += [("tokens", MT, 2)] + [("tokens", *x) for x in others]
        groups = [(t, g) for kind, t, g in order if kind == "tokens"]
        uses = [("features", i) for i in range(6)]
        for kind, t, g in order:
            for i in range(HI * len(key_spans(t)) if kind == "scores" else 1):
                uses.append((kind, sum(1 for x in uses if x[0] == kind)))
        bank = {x: ps[i % 6] for i, x in enumerate(uses)}
        rows_of = lambda t: META if t == MT else P
        ctx.enter_context(sem)
        with nc.Block() as block:
            @block.sync
            def _(sp):
                sp.dma_start(bfm[:, :], d["b_fm"]).then_inc(b_in, 16)
                sp.dma_start(kiC[:, :, :], d["kiT_cache"]).then_inc(kiC_in, 16)
                sp.dma_start(hist[:, :, :, :], d["conv_hist"]).then_inc(conv_in, 16)
                sp.dma_start(wc[:, :, :], d["conv_wb"]).then_inc(conv_in, 16)
                with sp.Fori(1, FM // 2) as r:
                    for u in range(2):
                        sp.wait_ge(fm_ready, 6 * r + (3 * u - 3))
                        sp.dma_start(w[:, u, :, :], d["w_fm"][2 * r + u, :, :, :]).then_inc(w_in[u], 16)
                sp.wait_ge(acc_ready, 4)
                sp.dma_start(d["p_conv"].rearrange("c p j -> p c j"), last_p[:, :, :]).then_inc(conv_out, 16)
                sp.dma_start(d["s_conv"].rearrange("c p i j -> p c i j"), last_s[:, :, :, :]).then_inc(conv_out, 16)
                sp.wait_ge(conv_out, 32)
                sp.wait_ge(bias_added, len(groups))
                sp.wait_ge(rows_copied, TT + 1)
                n = 0
                for name, c, width in (("k", CK, 128), ("v", CV, 128), ("kidx", CI, DI)):
                    out = d["p_" + name]
                    sp.dma_start(out[0:META, :], m.tm[0:META, MT, c:c + width]).then_inc(rows_out, 16)
                    sp.dma_start(out[META:PROMPT, :].rearrange("(j p) c -> p j c", p=P),
                                   m.tm[:, 0:NT, c:c + width]).then_inc(rows_out, 16)
                    sp.dma_start(d["s_" + name], m.tm[:, SAMPLE, c:c + width]).then_inc(rows_out, 16)
                    n += 3
                sp.wait_ge(rows_out, 16 * n)

            @block.gpsimd
            def _(pool):
                nc.gpsimd.memset(qiz[:, :, :], 0.0).then_inc(zeroed, 1)
                pool.wait_ge(zeroed, 1)
                pool.wait_ge(fm_copied, 3)
                nc.gpsimd.tensor_copy(bass.AP(qiz, 0, [[NSEQ * P, P], [P + SLEN, NSEQ], [1, SLEN]]),
                                      m.fm[:, F_QI, PROMPT:ALL].rearrange("p (i t) -> p i t", t=SLEN)).then_inc(qiz_ready, 1)
                for n, (t, g) in enumerate(groups):
                    rows, c = rows_of(t), slice(g * TG, (g + 1) * TG)
                    pool.wait_ge(tm_copied, n + 1)
                    nc.gpsimd.tensor_tensor(m.tm[0:rows, t, c], m.tm[0:rows, t, c], m.btm[0:rows, c], ALU.add).then_inc(bias_added, 1)
                pool.wait_ge(conv_in, 32)
                pool.wait_ge(relu_used, n_relu)
                own = Chain(pool, pool_own)
                g = nc.gpsimd
                for c in range(4):
                    pool.wait_ge(fm_copied, 3 * (F_BQ + c) + 3)
                    if c:
                        pool.wait_ge(silu_ready, c)
                    u = m.fm[:, F_BQ + c, :]
                    us = u[:, PROMPT:ALL].rearrange("p (i t) -> p i t", i=NSEQ)
                    accs = acc[:, PROMPT:ALL].rearrange("p (i t) -> p i t", i=NSEQ)
                    tap = lambda j: wc[:, c, j:j + 1]
                    g.tensor_copy(last_p[:, c, :], u[:, PROMPT - 3:PROMPT])
                    g.tensor_copy(last_s[:, c, :, :], us[:, :, SLEN - 3:SLEN])
                    g.tensor_copy(up[:, :, 0:3], hist[:, c, :, :])
                    own.link(g.tensor_copy(up[:, :, 3:SLEN + 3], us))
                    g.tensor_scalar(acc[:, 0:PROMPT], u[:, 0:PROMPT], tap(3), tap(4), ALU.mult, ALU.add)
                    own.link(g.tensor_scalar(accs, up[:, :, 3:SLEN + 3], tap(3), tap(4), ALU.mult, ALU.add))
                    half = PROMPT // 2
                    parts = part[:, half:half + P].rearrange("p (i t) -> p i t", i=NSEQ)
                    for j in range(1, 4):
                        for x, y in ((j, half), (half, PROMPT)):
                            own.link(g.tensor_scalar(part[:, 0:y - x], u[:, x - j:y - j], tap(3 - j), None, ALU.mult))
                            own.link(g.tensor_tensor(acc[:, x:y], acc[:, x:y], part[:, 0:y - x], ALU.add))
                        own.link(g.tensor_scalar(parts, up[:, :, 3 - j:SLEN + 3 - j], tap(3 - j), None, ALU.mult))
                        ins = g.tensor_tensor(accs, accs, parts, ALU.add)
                        if j < 3:
                            own.link(ins)
                    ins.then_inc(acc_ready, 1)
                for c in range(2):
                    pool.wait_ge(silu_ready, 3 + c)
                    g.tensor_scalar(m.fm[:, F_BK + c, :], m.fm[:, F_BK + c, :], DHB ** -0.5, None, ALU.mult).then_inc(keys_scaled, 1)

            @block.tensor
            def _(pe):
                def tile(r, u, free):
                    if not isinstance(r, int) or r:
                        pe.wait_ge(w_in[u], 16 * r)
                    for c, (a, b) in enumerate(spans):
                        free(c)
                        for k in range(KD):
                            mm = nc.tensor.matmul(ps[3 * u + c][:, 0:b - a], w[:, u, k, :], m.hT[:, k, a:b],
                                                  start=k == 0, stop=k == KD - 1)
                        mm.then_inc(fm_ready, 1)
                tile(0, 0, lambda c: None)
                tile(0, 1, lambda c: None)

                def token_tile(n):
                    t, g = groups[n]
                    rows = rows_of(t)
                    for k in range(KD):
                        stream = m.hT[:, k, q_cols(t)] if rows == P else m.hT[:, k, 0:META]
                        mm = nc.tensor.matmul(bank["tokens", n][0:rows, 0:TG], stream, m.wtm[:, k, g * TG:(g + 1) * TG],
                                              start=k == 0, stop=k == KD - 1)
                    mm.then_inc(tm_ready, 1)

                def free(i):
                    kind, n = uses[i - 6]
                    pe.wait_ge({"features": fm_copied, "tokens": tm_copied, "scores": relu_ready}[kind], n + 1)
                i, n_raw, n_tm = 6, 0, 0
                for kind, t, g in order:
                    if kind == "tokens":
                        free(i)
                        token_tile(n_tm)
                        n_tm += 1
                        i += 1
                        continue
                    if t == 0:
                        pe.wait_ge(fm_copied, 6)
                    if t == NT:
                        pe.wait_ge(kiC_in, 16)
                        pe.wait_ge(qiz_ready, 1)
                    for a, b in key_spans(t):
                        for h in range(HI):
                            free(i)
                            out = bank["scores", n_raw]
                            if t < NT:
                                mm = nc.tensor.matmul(out[:, 0:b - a], m.fm[i_rows(h), F_QI, q_cols(t)], m.fm[i_rows(h), F_KI, a:b])
                            else:
                                for j in range(NSEQ):
                                    nc.tensor.matmul(out[:, 0:P], qiz[i_rows(h), j, :], kiC[i_rows(h), j, :],
                                                     start=j == 0, stop=j == NSEQ - 1)
                                mm = nc.tensor.matmul(out[:, P:SK], m.fm[i_rows(h), F_QI, q_cols(t)],
                                                      m.fm[i_rows(h), F_KI, PROMPT:ALL])
                            mm.then_inc(raw_ready, 1)
                            n_raw += 1
                            i += 1
                pe.wait_ge(relu_ready, n_raw)
                for u in range(2):
                    tile(1, u, lambda c: free(6 + max(j for j in range(len(uses)) if j % 6 == 3 * u + c)))
                with pe.Fori(2, FM // 2) as r:
                    for u in range(2):
                        tile(r, u, lambda c: pe.wait_ge(fm_copied, 6 * r + (3 * u + c - 5)))
                pe.wait_ge(fm_copied, 3 * FM)
                for t in range(TT + 1):
                    if t >= 6:
                        pe.wait_ge(rows_copied, t - 5)
                    rows, stream = (P, q_cols(t)) if t < MT else (META, slice(0, META))
                    nc.tensor.transpose(ps[t % 6][0:rows, 0:P], m.fm[:, F_CK, stream], cols(m, "ident"))
                    nc.tensor.transpose(ps[t % 6][0:rows, P:P + DI], m.fm[0:DI, F_KI, stream],
                                        cols(m, "ident")[0:DI, 0:DI]).then_inc(rows_ready, 1)

            @block.scalar
            def _(act):
                act.wait_ge(b_in, 16)

                def feature_tile(r, u):
                    for c, (a, b) in enumerate(spans):
                        act.wait_ge(fm_ready, 6 * r + (3 * u + c + 1))
                        nc.scalar.activation(m.fm[:, 2 * r + u, a:b], ps[3 * u + c][:, 0:b - a], ACT.Identity,
                                             bias=bfm[:, ds(2 * r + u, 1)]).then_inc(fm_copied, 1)
                for u in range(2):
                    feature_tile(0, u)

                def token_copy(n):
                    t, g = groups[n]
                    act.wait_ge(tm_ready, n + 1)
                    nc.scalar.copy(m.tm[0:rows_of(t), t, g * TG:(g + 1) * TG], bank["tokens", n][0:rows_of(t), 0:TG]).then_inc(tm_copied, 1)
                n_raw = n_tm = 0
                for kind, t, g in order:
                    if kind == "tokens":
                        token_copy(n_tm)
                        n_tm += 1
                        continue
                    for a, b in key_spans(t):
                        for h in range(HI):
                            act.wait_ge(raw_ready, n_raw + 1)
                            if n_raw >= 4:
                                act.wait_ge(relu_used, n_raw - 3)
                            nc.scalar.activation(relu[:, n_raw % 4, 0:b - a], bank["scores", n_raw][:, 0:b - a], ACT.Relu,
                                                 scale=DI ** -0.5 * HI ** -0.5).then_inc(relu_ready, 1)
                            n_raw += 1
                act.wait_ge(bias_added, len(groups))
                nc.scalar.activation(m.tm[:, 0:TT, AR:AR + 256], m.tm[:, 0:TT, AR:AR + 256], ACT.Silu)
                nc.scalar.activation(m.tm[:, 0:TT, BO:BO + 256], m.tm[:, 0:TT, BO:BO + 256], ACT.Sigmoid)
                with act.Fori(1, F_BK // 2) as r:
                    for u in range(2):
                        feature_tile(r, u)
                for c in range(4):
                    for u in range(2):
                        feature_tile(F_BK // 2 + c, u)
                    act.wait_ge(acc_ready, c + 1)
                    nc.scalar.activation(m.fm[:, F_BQ + c, :], acc[:, :], ACT.Silu).then_inc(silu_ready, 1)
                for t in range(TT + 1):
                    act.wait_ge(rows_ready, t + 1)
                    nc.scalar.copy(m.tm[0:rows_of(t), t, CK:CK + P + DI], ps[t % 6][0:rows_of(t), 0:P + DI]).then_inc(rows_copied, 1)

            @block.vector
            def _(dve):
                own = Chain(dve, dve_own)
                n_raw = 0

                def scores(t):
                    nonlocal n_raw
                    dve.wait_ge(bias_added, groups.index((t, 2)) + 1)
                    for a, b in key_spans(t):
                        for h in range(HI):
                            n_raw += 1
                            dve.wait_ge(relu_ready, n_raw)
                            r, out = relu[:, (n_raw - 1) % 4, 0:b - a], score_of(m, score, t, a, b)
                            if h == 0:
                                ins = nc.vector.tensor_scalar(out, r, m.tm[:, t, CW + h:CW + h + 1], None, ALU.mult)
                            else:
                                ins = nc.vector.scalar_tensor_tensor(out, r, m.tm[:, t, CW + h:CW + h + 1], out, ALU.mult, ALU.add)
                            ins.then_inc(relu_used, 1)
                            dve.wait_ge(relu_used, n_raw)
                    if t < NT:
                        own.link(nc.vector.memset(score_of(m, score, t, NK[t] - 64, NK[t])[0:64], NEG))
                    else:
                        own.link(nc.vector.memset(score[:, SCORE_AT[NT] + SK:SCORE_AT[TT]], 3e38))
                        new = score_of(m, score, NT, P, SK)
                        own.link(nc.vector.tensor_tensor(new, new, cols(m, "otherseq"), ALU.add))

                def top_keys(t):
                    N, n = NK[t], (TOPK_P if t < NT else TOPK_S + EXTRA) // 8
                    n -= LEFT.count(t)
                    if n == 0:
                        return
                    if N <= TOPK_P and t < NT:
                        key_bias(nc, own, m, t, None)
                        return
                    src = score_of(m, score, t, 0, N if t < NT else N + EXTRA)

                    def a_round(k):
                        nc.vector.max(top[:, :], src).then_inc(round_own, 1)
                        dve.wait_ge(round_own, 2 * k + 1)
                        nc.vector.match_replace(src, top[:, :], src, TAKEN).then_inc(round_own, 1)
                        dve.wait_ge(round_own, 2 * k + 2)
                    if n > 8:
                        assert n % 8 == 0
                        with dve.Fori(0, n // 8) as r:
                            for k in range(8):
                                a_round(k)
                            nc.vector.sem_clear(round_own)
                    else:
                        for k in range(n):
                            a_round(k)
                        nc.vector.sem_clear(round_own)
                    if t not in LEFT:
                        key_bias(nc, own, m, t, src[:, 0:N])
                for t in range(4):
                    scores(t)
                    top_keys(t)
                for t in range(4, TT):
                    scores(t)
                for t in range(4, TT):
                    top_keys(t)


def log_sigmoid_act(nc, act, own, out, z):
    own.link(nc.scalar.activation(out, z, ACT.Abs))
    own.link(nc.scalar.activation(out, out, ACT.Exp, scale=-1.0))
    return nc.scalar.activation(out, out, ACT.Ln, bias=1.0)


def phase_gla(nc, m, d):
    with ExitStack() as ctx:
        sem = Semaphores(nc, "p4_")
        al = Bump(m, "p4_", m.HTO, m.CO)
        e_mid, e_neg, e_cum, e_last = (al(n, [P, ALL]) for n in ("e_mid", "e_neg", "e_cum", "e_last"))
        z, soft, cum = al("z", [P, ALL]), al("soft", [P, ALL]), al("cum", [P, ALL])
        keep = al("keep", [P, ALL])
        rel = soft
        al = Bump(m, "p4_", m.SCR, m.END - TT * 1024 - BIAS_BYTES)
        wg, bg = al("wg", [RANK, P]), al("bg", [P, 1])
        ke, qc, kd = (al(n, [P, 2, P]) for n in ("ke", "qc", "kd"))
        qbd, attm = al("qbd", [P, 2, HA, P]), al("attm", [P, 2, HA, P])
        kdT, S, upd = al("kdT", [P, 2, P]), al("S", [P, 256]), al("upd", [P, 256])
        S0 = Bump(m, "p4_", m.FMO, m.FMO + F_AQ * ALL * 4)("S0", [P, NSEQ, 256])
        qz, vz = al("qz", [P, NSEQ, P]), al("vz", [P, NSEQ, 256])
        pz = [ctx.enter_context(nc.psum_tensor(f"p4_z{i}", [P, 512], F32)) for i in range(4)]
        pA0, pK0, pO, pS = (ctx.enter_context(nc.psum_tensor("p4_" + n, [P, 512], F32)) for n in "AKOS")
        pA, pK = (pA0, pz[0]), (pK0, pz[1])

        par_in, s0_in, out = sem("par_in"), sem("s0_in"), sem("out")
        z_ready, soft_ready, cum_ready, exps_ready = sem("z_ready"), sem("soft_ready"), sem("cum_ready"), sem("exps_ready")
        dve_own, act_own, pool_own = sem("dve_own"), sem("act_own"), sem("pool_own")
        zb_ready, rel_ready = sem("zb_ready"), sem("rel_ready")
        oper_ready, att_ready, attm_ready, kdT_ready, kdT_copied = (sem(n) for n in (
            "oper_ready", "att_ready", "attm_ready", "kdT_ready", "kdT_copied"))
        o_ready, o_copied, upd_ready, state_ready = sem("o_ready"), sem("o_copied"), sem("upd_ready"), sem("state_ready")
        zeroed, state_done, vz_ready, inter_ready = sem("zeroed"), sem("state_done"), sem("vz_ready"), sem("inter_ready")
        spans = [(0, 512), (512, 1024), (1024, ALL)]
        tile = lambda ap, t: ap[:, q_cols(t)]
        prompt = lambda ap: ap[:, META:PROMPT].rearrange("p (j t) -> p j t", t=P)
        sample = lambda ap: ap[:, PROMPT:ALL].rearrange("p (i t) -> p i t", t=SLEN)
        AQ, AK = m.fm[:, F_AQ, :], m.fm[:, F_AK, :]

        ctx.enter_context(sem)
        with nc.Block() as block:
            @block.sync
            def _(sp):
                sp.dma_start(wg[:, :], d["w_gla_gate"]).then_inc(par_in, 16)
                sp.dma_start(bg[:, :], d["b_gla_gate"]).then_inc(par_in, 16)
                sp.dma_start(S0[:, :, :], d["gla_bd"]).then_inc(s0_in, 16)
                sp.wait_ge(state_ready, 9)
                for h in range(HA):
                    sp.dma_start(d["p_gla"][h, :, :], S[DKA * h:DKA * h + DKA, DVA * h:DVA * h + DVA]).then_inc(out, 16)
                sp.wait_ge(state_done, 1)
                for h in range(HA):
                    sp.dma_start(d["s_gla"][h, :, :, :],
                                 S0[DKA * h:DKA * h + DKA, :, DVA * h:DVA * h + DVA]).then_inc(out, 16)
                sp.wait_ge(out, 16 * 2 * HA)

            @block.gpsimd
            def _(pool):
                nc.gpsimd.memset(qz[:, :, :], 0.0).then_inc(zeroed, 1)
                nc.gpsimd.tensor_tensor(vz[:, :, :], over(m.tm[:, SAMPLE, AV:AV + 256].unsqueeze(1), [P, NSEQ, 256]),
                                        over(cols(m, "seqmask").unsqueeze(2), [P, NSEQ, 256]),
                                        ALU.mult).then_inc(vz_ready, 1)

            @block.vector
            def _(dve):
                own = Chain(dve, dve_own)
                own.link(nc.vector.memset(keep[:, :], 1.0))
                own.link(nc.vector.memset(keep[:, 0:1], 0.0))
                own.link(nc.vector.memset(prompt(keep)[:, :, 0:1], 0.0))
                own.link(nc.vector.memset(sample(keep)[:, :, 0:1], 0.0))
                dve.wait_ge(soft_ready, 1)
                own.link(nc.vector.scalar_tensor_tensor(z[:, :], z[:, :], 0.0, soft[:, :], ALU.min, ALU.subtract))
                own.link(nc.vector.tensor_tensor_scan(cum[:, :], keep[:, :], z[:, :], 0.0, ALU.mult, ALU.add))
                nc.vector.tensor_tensor(prompt(rel), prompt(cum), over(prompt(cum)[:, :, 63:64], [P, NT, P]), ALU.subtract)
                nc.vector.tensor_tensor(sample(rel), sample(cum), over(sample(cum)[:, :, 7:8], [P, NSEQ, SLEN]), ALU.subtract)
                nc.vector.tensor_tensor(prompt(z), over(prompt(cum)[:, :, P - 1:P], [P, NT, P]), prompt(cum), ALU.subtract)
                nc.vector.tensor_tensor(z[:, 0:META], over(cum[:, META - 1:META], [P, META]), cum[:, 0:META], ALU.subtract)
                nc.vector.tensor_tensor(sample(z), over(sample(cum)[:, :, SLEN - 1:SLEN], [P, NSEQ, SLEN]), sample(cum),
                                        ALU.subtract).then_inc(rel_ready, 1)
                dve.wait_ge(exps_ready, 4)
                own.link(nc.vector.scalar_tensor_tensor(e_mid[:, META:ALL], AQ[:, META:ALL], DKA ** -0.5, e_mid[:, META:ALL],
                                                        ALU.mult, ALU.mult))

                def operands(t):
                    u = t % 2
                    nc.vector.tensor_tensor(ke[:, u, :], tile(AK, t), tile(e_neg, t), ALU.mult)
                    nc.vector.tensor_tensor(kd[:, u, :], tile(AK, t), tile(e_last, t), ALU.mult)
                    nc.vector.tensor_tensor(qbd[:, u, :, :], over(tile(e_mid, t).unsqueeze(1), [P, HA, P]),
                                            over(cols(m, "headA").unsqueeze(2), [P, HA, P]), ALU.mult)
                    if t == NT:
                        dve.wait_ge(zeroed, 1)
                        out = bass.AP(qz, 0, [[NSEQ * P, P], [P + SLEN, NSEQ], [1, SLEN]])
                        i0, i1 = sample(AQ), sample(e_cum)
                    else:
                        out, i0, i1 = qc[:, u, :], tile(AQ, t), tile(e_cum, t)
                    nc.vector.scalar_tensor_tensor(out, i0, DKA ** -0.5, i1, ALU.mult, ALU.mult).then_inc(oper_ready, 1)

                def masked_scores(t):
                    dve.wait_ge(att_ready, t + 1)
                    mask = cols(m, "causal" if t < NT else "blocked")
                    nc.vector.tensor_tensor(attm[:, t % 2, :, :], pA[t % 2][:, :].rearrange("p (h t) -> p h t", h=HA),
                                            over(mask.unsqueeze(1), [P, HA, P]), ALU.mult).then_inc(attm_ready, 1)

                def state(t):
                    dve.wait_ge(upd_ready, t + 2)
                    own.link(nc.vector.tensor_tensor(upd[:, :], pS[:, 0:256], cols(m, "bdA"), ALU.mult))
                    dve.wait_ge(inter_ready, t + 1)
                    end = META + P * t + P - 1
                    nc.vector.scalar_tensor_tensor(S[:, :], S[:, :], e_cum[:, end:end + 1], upd[:, :],
                                                   ALU.mult, ALU.add).then_inc(state_ready, 1)
                    dve.wait_ge(state_ready, t + 2)

                nc.vector.tensor_tensor(kd[:, 1, 0:META], AK[:, 0:META], e_last[:, 0:META], ALU.mult).then_inc(oper_ready, 1)
                operands(0)
                dve.wait_ge(upd_ready, 1)
                nc.vector.tensor_tensor(S[:, :], pS[:, 0:256], cols(m, "bdA"), ALU.mult).then_inc(state_ready, 1)
                dve.wait_ge(state_ready, 1)
                masked_scores(0)
                for t in range(TT):
                    if t + 1 < TT:
                        if t:
                            dve.wait_ge(o_ready, t)
                        dve.wait_ge(kdT_ready, t + 1)
                        operands(t + 1)
                    if t < NT:
                        state(t)
                    if t + 1 < TT:
                        masked_scores(t + 1)
                dve.wait_ge(s0_in, 16)
                dve.wait_ge(o_ready, NT + 1)
                dve.wait_ge(upd_ready, NT + 2)
                for i in range(NSEQ):
                    own.link(nc.vector.tensor_tensor(upd[:, :], pz[i // 2][:, 256 * (i % 2):256 * (i % 2) + 256],
                                                      cols(m, "bdA"), ALU.mult))
                    ins = nc.vector.scalar_tensor_tensor(S0[:, i, :], S0[:, i, :],
                                                         e_cum[:, PROMPT + SLEN * i + SLEN - 1:PROMPT + SLEN * i + SLEN],
                                                         upd[:, :], ALU.mult, ALU.add)
                    if i < NSEQ - 1:
                        own.link(ins)
                ins.then_inc(state_done, 1)

            @block.scalar
            def _(act):
                own = Chain(act, act_own)
                act.wait_ge(par_in, 32)
                for c, (a, b) in enumerate(spans):
                    act.wait_ge(z_ready, c + 1)
                    own.link(nc.scalar.activation(z[:, a:b], pz[c][:, 0:b - a], ACT.Identity, bias=bg[:, 0:1]))
                log_sigmoid_act(nc, act, own, soft[:, :], z[:, :]).then_inc(soft_ready, 1)
                act.wait_ge(rel_ready, 1)
                tau = 1.0 / 16.0
                nc.scalar.activation(e_mid[:, META:ALL], rel[:, META:ALL], ACT.Exp, scale=tau).then_inc(exps_ready, 1)
                nc.scalar.activation(e_neg[:, META:ALL], rel[:, META:ALL], ACT.Exp, scale=-tau).then_inc(exps_ready, 1)
                nc.scalar.activation(e_cum[:, :], cum[:, :], ACT.Exp, scale=tau).then_inc(exps_ready, 1)
                nc.scalar.activation(e_last[:, :], z[:, :], ACT.Exp, scale=tau).then_inc(exps_ready, 1)

                def copies(n, rows=P):
                    act.wait_ge(kdT_ready, n + 1)
                    if n >= 2:
                        act.wait_ge(upd_ready, n - 1)
                    u = (n + 1) % 2
                    nc.scalar.copy(kdT[0:rows, u, :], pK[u][0:rows, 0:P]).then_inc(kdT_copied, 1)

                copies(0, META)
                copies(1)
                for t in range(TT):
                    if t + 2 <= TT:
                        copies(t + 2)
                    act.wait_ge(o_ready, t + 1)
                    act.wait_ge(upd_ready, t + 2)
                    if t == NT:
                        act.wait_ge(vz_ready, 1)
                    nc.scalar.copy(m.tm[:, t, AV:AV + 256], pO[:, 0:256]).then_inc(o_copied, 1)

            @block.tensor
            def _(pe):
                pe.wait_ge(par_in, 32)
                for c, (a, b) in enumerate(spans):
                    nc.tensor.matmul(pz[c][:, 0:b - a], wg[:, :], m.fm[0:RANK, F_MISC, a:b]).then_inc(z_ready, 1)

                def scores(t):
                    pe.wait_ge(oper_ready, t + 2)
                    if t >= 2:
                        pe.wait_ge(attm_ready, t - 1)
                    nc.tensor.matmul(pA[t % 2][:, :], ke[:, t % 2, :],
                                     qbd[:, t % 2, :, :].rearrange("p h t -> p (h t)")).then_inc(att_ready, 1)

                def keys(t):
                    if t >= 1:
                        pe.wait_ge(kdT_copied, t)
                    nc.tensor.transpose(pK[t % 2][:, 0:P], kd[:, t % 2, :], cols(m, "ident")).then_inc(kdT_ready, 1)

                def heads(t):
                    pe.wait_ge(attm_ready, t + 1)
                    for h in range(HA):
                        mm = nc.tensor.matmul(pO[:, DVA * h:DVA * h + DVA], attm[:, t % 2, h, :],
                                              m.tm[:, t, AV + DVA * h:AV + DVA * h + DVA], start=False, stop=h == HA - 1,
                                              skip_group_check=True)
                    mm.then_inc(o_ready, 1)

                pe.wait_ge(soft_ready, 1)
                pe.wait_ge(oper_ready, 1)
                nc.tensor.transpose(pK[1][0:META, 0:P], kd[:, 1, 0:META], cols(m, "ident")).then_inc(kdT_ready, 1)
                scores(0)
                keys(0)
                pe.wait_ge(kdT_copied, 1)
                nc.tensor.matmul(pS[:, 0:256], kdT[0:META, 1, :], m.tm[0:META, MT, AV:AV + 256]).then_inc(upd_ready, 1)
                for t in range(TT):
                    pe.wait_ge(state_ready, t + 1)
                    if t:
                        pe.wait_ge(o_copied, t)
                    if t < NT:
                        nc.tensor.matmul(pO[:, 0:256], qc[:, t % 2, :], S[:, :], start=True, stop=False,
                                         skip_group_check=True).then_inc(inter_ready, 1)
                        pe.wait_ge(kdT_copied, t + 2)
                        nc.tensor.matmul(pS[:, 0:256], kdT[:, t % 2, :], m.tm[:, t, AV:AV + 256]).then_inc(upd_ready, 1)
                        scores(t + 1)
                    else:
                        pe.wait_ge(s0_in, 16)
                        for i in range(NSEQ):
                            nc.tensor.matmul(pO[:, 0:256], qz[:, i, :], S0[:, i, :], start=i == 0, stop=False, skip_group_check=True)
                    heads(t)
                    if t < NT:
                        keys(t + 1)
                pe.wait_ge(kdT_copied, NT + 2)
                pe.wait_ge(vz_ready, 1)
                for j in range(NSEQ // 2):
                    mm = nc.tensor.matmul(pz[j][:, :], kdT[:, NT % 2, :], vz[:, 2 * j:2 * j + 2, :].rearrange("p i c -> p (i c)"))
                mm.then_inc(upd_ready, 1)


def phase_mlstm(nc, m, d):
    with ExitStack() as ctx:
        sem = Semaphores(nc, "p5_")
        nlast, mlast = m.at("p5_nlast", [P, 2, NSEQ], m.HTO + 7 * ALL * 4 + 3264), m.at("p5_mlast", [P, NSEQ + 1], m.HTO + 7 * ALL * 4 + 3328)
        VE = DVA + 1
        al = Bump(m, "p5_", m.HTO, m.CO)
        t1, t2, cum, M, gates, keep, drop = (al(n, [P, ALL]) for n in ("t1", "t2", "cum", "M", "gates", "keep", "drop"))
        gtm = al("gtm", [P, TT + 1, 4, HB])
        slf, slb = al("slf", [P, 17]), al("slb", [P, 2, 17])
        m0, bfg = al("m0", [P, NSEQ]), al("bfg", [P, 1])
        C0 = Bump(m, "p5_", m.FMO, m.FMO + F_AQ * ALL * 4)("C0", [P, 2, NSEQ, 2 * VE])
        al = Bump(m, "p5_", m.SCR, m.END - TT * 1024 - BIAS_BYTES)
        vx = al("vx", [P, TT + 1, HB, VE])
        vz, qz = al("vz", [P, NSEQ, HB * VE]), al("qz", [P, 2, NSEQ, P])
        kw, tot = al("kw", [P, 2, 256]), al("tot", [P, HB, VE])
        al = Bump(m, "p5_", m.FMO + F_AQ * ALL * 4, m.FMO + F_BQ * ALL * 4)
        qbd, W, C = al("qbd", [P, 2, 2, 2, P]), al("W", [P, 2, HB, P]), al("C", [P, 2, 2 * VE])
        upd, den = m.at("p5_upd", [P, 2, 2 * VE], m.HTO + 7 * ALL * 4 + 2048), m.at("p5_den", [P, HB], m.HTO + 7 * ALL * 4 + 3200)
        assert m.HTO + 7 * ALL * 4 + 3400 <= m.CO
        pA, pM, pK, pI, pN, pC, pX, pY = (ctx.enter_context(nc.psum_tensor("p5_" + n, [P, 512], F32)) for n in "AMKINCXY")
        (par_in, c0_in, out, dve_own, act_own, raw_ready, soft_ready, arg_ready, gates_ready, turned, gtm_ready,
         sl_ready, slb_ready, oper_ready, prod_ready, d_ready, w_ready, masked, pm_ready, kw_ready, inter_ready,
         num_ready, upd_ready, state_ready, zeroed, vz_ready, kT_ready, m_ready) = (sem(n) for n in (
            "par_in c0_in out dve_own act_own raw_ready soft_ready arg_ready gates_ready turned gtm_ready sl_ready "
            "slb_ready oper_ready prod_ready d_ready w_ready masked pm_ready kw_ready inter_ready num_ready "
            "upd_ready state_ready zeroed vz_ready kT_ready m_ready").split())
        prompt = lambda ap: ap[:, META:PROMPT].rearrange("p (j t) -> p j t", t=P)
        sample = lambda ap: ap[:, PROMPT:ALL].rearrange("p (i t) -> p i t", t=SLEN)
        H = lambda ap: ap[0:HB, :]
        span = lambda t: slice(META + t * P, META + t * P + P)
        banks = (pA, pM, pK)
        pM2, pA2 = (pM, pY), (pA, pX)
        pair_bank = lambda i, p: (pA, pM, pK, pC, pX, pY)[(2 * i + p) // 3][:, 2 * VE * ((2 * i + p) % 3):2 * VE * ((2 * i + p) % 3 + 1)]

        ctx.enter_context(sem)
        with nc.Block() as block:
            @block.sync
            def _(sp):
                sp.dma_start(m0[0:HB, :], d["m0"]).then_inc(par_in, 16)
                sp.dma_start(bfg[ROW_F:ROW_F + HB, :], d["b_forget"]).then_inc(par_in, 16)
                sp.dma_start(C0[:, :, :, :], d["mlstm_bd"]).then_inc(c0_in, 16)
                sp.wait_ge(m_ready, 1)
                sp.dma_start(d["p_m"], mlast[0:HB, NSEQ:NSEQ + 1]).then_inc(out, 16)
                sp.dma_start(d["s_m"], mlast[0:HB, 0:NSEQ]).then_inc(out, 16)
                sp.wait_ge(state_ready, NT + 1)
                for h in range(HB):
                    rows = slice(64 * (h % 2), 64 * (h % 2) + 64)
                    c = VE * (h % 2)
                    sp.dma_start(d["p_c"][h, :, :], C[rows, h // 2, c:c + 64]).then_inc(out, 16)
                    sp.dma_start(d["p_n"][h:h + 1, :].rearrange("a k -> k a"), C[rows, h // 2, c + 64:c + 65]).then_inc(out, 16)
                sp.wait_ge(state_ready, NT + 2)
                for h in range(HB):
                    rows = slice(64 * (h % 2), 64 * (h % 2) + 64)
                    c = VE * (h % 2)
                    sp.dma_start(d["s_c"][h, :, :, :], C0[rows, h // 2, :, c:c + 64]).then_inc(out, 16)
                    sp.dma_start(d["s_n"][h, :, :], nlast[rows, h // 2, :]).then_inc(out, 16)
                sp.wait_ge(out, 16 * (2 + 4 * HB))

            @block.gpsimd
            def _(pool):
                nc.gpsimd.memset(qz[:, :, :, :], 0.0).then_inc(zeroed, 1)
                nc.gpsimd.memset(vx[:, :, :, :], 1.0).then_inc(zeroed, 1)
                pool.wait_ge(zeroed, 2)
                nc.gpsimd.tensor_copy(vx[:, 0:TT, :, 0:DVA],
                                      m.tm[:, 0:TT, BV:BV + 256].rearrange("p t (h v) -> p t h v", v=DVA)).then_inc(zeroed, 1)
                nc.gpsimd.tensor_copy(vx[0:META, MT, :, 0:DVA],
                                      m.tm[0:META, MT, BV:BV + 256].rearrange("p (h v) -> p h v", v=DVA)).then_inc(zeroed, 1)
                pool.wait_ge(zeroed, 4)
                nc.gpsimd.tensor_tensor(vz[:, :, :], over(vx[:, SAMPLE, :, :].rearrange("p h v -> p (h v)").unsqueeze(1),
                                                          [P, NSEQ, HB * VE]),
                                        over(cols(m, "seqmask").unsqueeze(2), [P, NSEQ, HB * VE]),
                                        ALU.mult).then_inc(vz_ready, 1)

                def mask(t, which):
                    pool.wait_ge(w_ready, t + 1)
                    nc.gpsimd.tensor_tensor(W[:, t % 2, :, :], W[:, t % 2, :, :], over(cols(m, which).unsqueeze(1), [P, HB, P]),
                                            ALU.mult).then_inc(masked, 1)
                for t in range(TT):
                    mask(t, "causal" if t < NT else "blocked")

            @block.vector
            def _(dve):
                own = Chain(dve, dve_own)
                own.link(nc.vector.memset(gates[:, :], 0.0))
                own.link(nc.vector.memset(H(keep), 1.0))
                own.link(nc.vector.memset(sample(keep)[0:HB, :, 0:1], 0.0))
                own.link(nc.vector.memset(H(drop), 0.0))
                nc.vector.memset(sample(drop)[0:HB, :, 0:1], NEG).then_inc(raw_ready, 1)
                dve.wait_ge(soft_ready, 1)
                own.link(nc.vector.scalar_tensor_tensor(H(t1), H(t1), 0.0, H(t2), ALU.min, ALU.subtract))
                own.link(nc.vector.tensor_tensor_scan(H(cum), H(keep), H(t1), 0.0, ALU.mult, ALU.add))
                own.link(nc.vector.tensor_tensor(H(gates), H(gates), H(cum), ALU.subtract))
                own.link(nc.vector.tensor_copy(H(t2), H(gates)))
                own.link(nc.vector.tensor_scalar(t2[0:HB, 0:1], t2[0:HB, 0:1], 0.0, None, ALU.max))
                dve.wait_ge(par_in, 32)
                own.link(nc.vector.tensor_tensor(sample(t2)[0:HB, :, 0], sample(t2)[0:HB, :, 0], m0[0:HB, :], ALU.max))
                own.link(nc.vector.tensor_tensor_scan(H(M), H(drop), H(t2), NEG, ALU.add, ALU.max))
                own.link(nc.vector.tensor_tensor(t1[0:HB, 0:META], gates[0:HB, 0:META], over(M[0:HB, META - 1:META], [HB, META]),
                                                 ALU.subtract))
                own.link(nc.vector.tensor_tensor(prompt(t1)[0:HB], prompt(gates)[0:HB],
                                                 over(prompt(M)[0:HB, :, P - 1:P], [HB, NT, P]), ALU.subtract))
                own.link(nc.vector.tensor_tensor(sample(t1)[0:HB], sample(gates)[0:HB],
                                                 over(sample(M)[0:HB, :, SLEN - 1:SLEN], [HB, NSEQ, SLEN]), ALU.subtract))
                own.link(nc.vector.tensor_scalar(keep[0:HB, 0:META], M[0:HB, 0:META], -1.0, None, ALU.mult))
                before = M[0:HB, META - 1:META - 1 + SEQ].rearrange("p (j t) -> p j t", t=P)[:, :, 0:1]
                own.link(nc.vector.tensor_tensor(prompt(keep)[0:HB], over(before, [HB, NT, P]), prompt(M)[0:HB], ALU.subtract))
                own.link(nc.vector.tensor_tensor(sample(keep)[0:HB], over(m0[0:HB, :].unsqueeze(2), [HB, NSEQ, SLEN]),
                                                 sample(M)[0:HB], ALU.subtract))
                own.link(nc.vector.tensor_copy(slf[0:HB, 0:1], keep[0:HB, META - 1:META]))
                own.link(nc.vector.tensor_copy(slf[0:HB, 1:9], prompt(keep)[0:HB, :, P - 1]))
                own.link(nc.vector.tensor_copy(slf[0:HB, 9:17], sample(keep)[0:HB, :, SLEN - 1]))
                own.link(nc.vector.tensor_tensor(H(t2), H(M), H(cum), ALU.add))
                nc.vector.tensor_copy(mlast[0:HB, NSEQ:NSEQ + 1], t2[0:HB, PROMPT - 1:PROMPT]).then_inc(arg_ready, 1)
                nc.vector.tensor_copy(mlast[0:HB, 0:NSEQ], sample(t2)[0:HB, :, SLEN - 1]).then_inc(m_ready, 1)
                for g in range(3):
                    dve.wait_ge(turned, g + 1)
                    n = min(4, TT + 1 - 4 * g)
                    src = banks[g][:, :].rearrange("p (t k c) -> p t k c", t=4, k=4)
                    nfull = min(n, TT - 4 * g)
                    own.link(nc.vector.tensor_copy(gtm[:, 4 * g:4 * g + nfull, :, :], src[:, 0:nfull, :, 0:HB]))
                own.link(nc.vector.tensor_copy(gtm[0:META, MT, :, :], src[0:META, 1, :, 0:HB]))
                dve.wait_ge(sl_ready, 1)
                nc.vector.tensor_copy(slb[:, :, :], pX[:, 0:34].rearrange("p (a b) -> p a b", a=2)).then_inc(gtm_ready, 1)
                dve.wait_ge(gtm_ready, 1)

                head = lambda ap: over(ap.unsqueeze(2), [ap.shape[0], HB, 64])
                heads4 = lambda ap: ap.rearrange("p (h v) -> p h v", v=64)
                bd = over(cols(m, "bdB").unsqueeze(1), [P, 2, 2 * VE])

                dve.wait_ge(kT_ready, 1)
                nc.vector.tensor_tensor(heads4(kw[0:META, 1, :]), heads4(pK[0:META, 0:256]), head(gtm[0:META, MT, 1, :]),
                                        ALU.mult).then_inc(kw_ready, 1)
                dve.wait_ge(upd_ready, 1)
                nc.vector.tensor_tensor(C[:, :, :], pC[:, 0:4 * VE].rearrange("p (a b) -> p a b", a=2), bd,
                                        ALU.mult).then_inc(state_ready, 1)

                def operands(t):
                    if t == NT:
                        for p in range(2):
                            nc.vector.tensor_copy(bass.AP(qz, p * NSEQ * P, [[2 * NSEQ * P, P], [P + SLEN, NSEQ], [1, SLEN]]),
                                                  sample(m.fm[:, F_BQ + p, :]))
                    for p in range(2):
                        ins = nc.vector.tensor_tensor(qbd[:, t % 2, p, :, :], over(m.fm[:, F_BQ + p, span(t)].unsqueeze(1), [P, 2, P]),
                                                      over(cols(m, "headB").unsqueeze(2), [P, 2, P]), ALU.mult)
                    ins.then_inc(oper_ready, 1)

                def exponents(t):
                    dve.wait_ge(prod_ready, t + 1)
                    Wt = W[:, t % 2, :, :]
                    own.link(nc.vector.tensor_tensor(Wt, over(gtm[:, t, 0, :].unsqueeze(2), [P, HB, P]),
                                                     pM2[t % 2][:, :].rearrange("p (h t) -> p h t", h=HB), ALU.subtract))
                    nc.vector.tensor_scalar(Wt, Wt, 0.0, None, ALU.min).then_inc(d_ready, 1)

                def weighted_keys(t):
                    dve.wait_ge(kT_ready, t + 2)
                    nc.vector.tensor_tensor(heads4(kw[:, t % 2, :]), heads4(pK[:, 0:256]), head(gtm[:, t, 1, :]),
                                            ALU.mult).then_inc(kw_ready, 1)

                def weighted_scores(t):
                    dve.wait_ge(masked, t + 1)
                    Wt = W[:, t % 2, :, :]
                    nc.vector.tensor_tensor(Wt, Wt, pA2[t % 2][:, :].rearrange("p (h t) -> p h t", h=HB), ALU.mult).then_inc(pm_ready, 1)

                def totals(t):
                    dve.wait_ge(inter_ready, t + 1)
                    own.link(nc.vector.tensor_tensor(tot[:, :, :], pI[:, 0:4 * VE].rearrange("p (h v) -> p h v", v=VE),
                                                     over(gtm[:, t, 2, :].unsqueeze(2), [P, HB, VE]), ALU.mult))
                    dve.wait_ge(num_ready, t + 1)
                    own.link(nc.vector.tensor_tensor(tot[:, :, :], tot[:, :, :], pN[:, 0:4 * VE].rearrange("p (h v) -> p h v", v=VE),
                                                     ALU.add))

                def state(t):
                    dve.wait_ge(upd_ready, t + 2)
                    own.link(nc.vector.tensor_tensor(upd[:, :, :], pC[:, 0:4 * VE].rearrange("p (a b) -> p a b", a=2), bd, ALU.mult))
                    nc.vector.scalar_tensor_tensor(C[:, 0, :], C[:, 0, :], slb[:, 0, t + 1:t + 2], upd[:, 0, :], ALU.mult, ALU.add)
                    nc.vector.scalar_tensor_tensor(C[:, 1, :], C[:, 1, :], slb[:, 1, t + 1:t + 2], upd[:, 1, :],
                                                   ALU.mult, ALU.add).then_inc(state_ready, 1)
                    dve.wait_ge(state_ready, t + 2)

                def output(t):
                    own.link(nc.vector.scalar_tensor_tensor(den[:, :], tot[:, :, DVA], -1.0, tot[:, :, DVA], ALU.mult, ALU.max))
                    own.link(nc.vector.tensor_tensor(den[:, :], den[:, :], gtm[:, t, 3, :], ALU.max))
                    own.link(nc.vector.reciprocal(den[:, :], den[:, :]))
                    own.link(nc.vector.tensor_tensor(heads4(m.tm[:, t, BV:BV + 256]), tot[:, :, 0:DVA], head(den[:, :]), ALU.mult))

                dve.wait_ge(zeroed, 4)
                operands(0)
                exponents(0)
                weighted_keys(0)
                weighted_scores(0)
                for t in range(TT):
                    if t + 1 < TT:
                        operands(t + 1)
                    totals(t)
                    if t + 1 < TT:
                        exponents(t + 1)
                    if t < NT:
                        state(t)
                    if t + 1 < TT:
                        weighted_keys(t + 1)
                    output(t)
                    if t + 1 < TT:
                        weighted_scores(t + 1)
                dve.wait_ge(upd_ready, NT + 2)
                dve.wait_ge(c0_in, 16)
                cell = over(cols(m, "bdB"), [P, 2 * VE])
                for i in range(NSEQ):
                    for p in range(2):
                        n = 2 * i + p
                        own.link(nc.vector.tensor_tensor(upd[:, p, :], pair_bank(i, p), cell, ALU.mult))
                        own.link(nc.vector.scalar_tensor_tensor(C0[:, p, i, :], C0[:, p, i, :], slb[:, p, 9 + i:10 + i], upd[:, p, :],
                                                                ALU.mult, ALU.add))
                own.link(nc.vector.tensor_copy(nlast[0:64, :, :], C0[0:64, :, :, DVA]))
                nc.vector.tensor_copy(nlast[64:P, :, :], C0[64:P, :, :, 2 * VE - 1]).then_inc(state_ready, 1)

            @block.scalar
            def _(act):
                own = Chain(act, act_own)
                act.wait_ge(raw_ready, 1)
                act.wait_ge(par_in, 32)
                own.link(nc.scalar.activation(H(t1), m.fm[ROW_F:ROW_F + HB, F_MISC, :], ACT.Identity, bias=bfg[ROW_F:ROW_F + HB, :]))
                own.link(nc.scalar.copy(H(gates), m.fm[ROW_I:ROW_I + HB, F_MISC, :]))
                log_sigmoid_act(nc, act, own, H(t2), H(t1)).then_inc(soft_ready, 1)
                act.wait_ge(arg_ready, 1)
                nc.scalar.activation(gates[32:32 + HB, :], H(t1), ACT.Exp).then_inc(gates_ready, 1)
                nc.scalar.activation(gates[64:64 + HB, :], H(keep), ACT.Exp).then_inc(gates_ready, 1)
                nc.scalar.activation(gates[96:96 + HB, :], H(t2), ACT.Exp, scale=-1.0).then_inc(gates_ready, 1)
                nc.scalar.activation(slf[0:HB, :], slf[0:HB, :], ACT.Exp).then_inc(gates_ready, 1)
                for t in range(TT):
                    act.wait_ge(d_ready, t + 1)
                    nc.scalar.activation(W[:, t % 2, :, :], W[:, t % 2, :, :], ACT.Exp).then_inc(w_ready, 1)

            @block.tensor
            def _(pe):
                pe.wait_ge(gates_ready, 4)
                for g in range(3):
                    for t in range(4 * g, min(4 * g + 4, TT)):
                        mm = nc.tensor.transpose(banks[g][:, P * (t % 4):P * (t % 4) + P], gates[:, META + t * P:META + t * P + P],
                                                 cols(m, "ident"))
                    if g == 2:
                        mm = nc.tensor.transpose(banks[g][0:META, P:2 * P], gates[:, 0:META], cols(m, "ident"))
                    mm.then_inc(turned, 1)
                for p in range(2):
                    mm = nc.tensor.matmul(pX[:, 17 * p:17 * p + 17], cols(m, "selB")[0:HB, P * p:P * p + P], slf[0:HB, :])
                mm.then_inc(sl_ready, 1)

                def keys(t):
                    rows, src = (P, span(t)) if t >= 0 else (META, slice(0, META))
                    if t >= 0:
                        pe.wait_ge(kw_ready, t + 1)
                    for p in range(2):
                        mm = nc.tensor.transpose(pK[0:rows, P * p:P * p + P], m.fm[:, F_BK + p, src], cols(m, "ident"))
                    mm.then_inc(kT_ready, 1)

                pe.wait_ge(gtm_ready, 1)
                keys(-1)
                pe.wait_ge(kw_ready, 1)
                pe.wait_ge(zeroed, 4)
                for p in range(2):
                    mm = nc.tensor.matmul(pC[:, 2 * VE * p:2 * VE * (p + 1)], kw[0:META, 1, P * p:P * p + P],
                                          vx[0:META, MT, 2 * p:2 * p + 2, :].rearrange("p h v -> p (h v)"))
                mm.then_inc(upd_ready, 1)

                def scores(t):
                    pe.wait_ge(oper_ready, t + 1)
                    if t >= 2:
                        pe.wait_ge(pm_ready, t - 1)
                    for h in range(HB):
                        nc.tensor.matmul(pM2[t % 2][:, P * h:P * h + P], cols(m, "selM")[0:HB, P * h:P * h + P], M[0:HB, span(t)])
                    for p in range(2):
                        mm = nc.tensor.matmul(pA2[t % 2][:, 256 * p:256 * p + 256], m.fm[:, F_BK + p, span(t)],
                                              qbd[:, t % 2, p, :, :].rearrange("p h t -> p (h t)"))
                    mm.then_inc(prod_ready, 1)

                def from_state(t):
                    pe.wait_ge(state_ready, t + 1)
                    for p in range(2):
                        if t < NT:
                            mm = nc.tensor.matmul(pI[:, 2 * VE * p:2 * VE * (p + 1)], m.fm[:, F_BQ + p, span(t)], C[:, p, :])
                        else:
                            for i in range(NSEQ):
                                mm = nc.tensor.matmul(pI[:, 2 * VE * p:2 * VE * (p + 1)], qz[:, p, i, :], C0[:, p, i, :],
                                                      start=i == 0, stop=i == NSEQ - 1)
                    mm.then_inc(inter_ready, 1)

                def numerators(t):
                    pe.wait_ge(pm_ready, t + 1)
                    for h in range(HB):
                        mm = nc.tensor.matmul(pN[:, VE * h:VE * h + VE], W[:, t % 2, h, :], vx[:, t, h, :])
                    mm.then_inc(num_ready, 1)

                scores(0)
                keys(0)
                for t in range(TT):
                    if t == NT:
                        pe.wait_ge(c0_in, 16)
                    from_state(t)
                    numerators(t)
                    if t + 1 < TT:
                        scores(t + 1)
                    pe.wait_ge(kw_ready, t + 2)
                    if t < NT:
                        for p in range(2):
                            mm = nc.tensor.matmul(pC[:, 2 * VE * p:2 * VE * (p + 1)], kw[:, t % 2, P * p:P * p + P],
                                                  vx[:, t, 2 * p:2 * p + 2, :].rearrange("p h v -> p (h v)"))
                        mm.then_inc(upd_ready, 1)
                        keys(t + 1)
                pe.wait_ge(vz_ready, 1)
                for i in range(NSEQ):
                    for p in range(2):
                        mm = nc.tensor.matmul(pair_bank(i, p), kw[:, NT % 2, P * p:P * p + P], vz[:, i, 2 * VE * p:2 * VE * (p + 1)])
                mm.then_inc(upd_ready, 1)


def phase_dsa(nc, m, d):
    with ExitStack() as ctx:
        sem = Semaphores(nc, "p6_")
        GQ = HC // KVC
        m.w_out0 = Bump(m, "p6_", m.FMO + F_AQ * ALL * 4, m.FMO + F_BQ * ALL * 4)("w_out0", [P, 2, D])
        al = Bump(m, "p6_", m.FMO + F_MISC * ALL * 4, m.CO)
        m.w_out2 = al("w_out2", [P, 4, D])
        qz = al("qz", [P, 4, NSEQ, P])
        kC, vC = al("kC", [P, NSEQ, P]), al("vC", [P, NSEQ, P])
        al = Bump(m, "p6_", m.SCR, m.END - TT * 1024 - BIAS_BYTES)
        logit = al("logit", [P, 3, PROMPT])
        pT = [al("pT0", [P, NT + 1, 2, P]), Bump(m, "p6_", m.FMO, m.FMO + F_AQ * ALL * 4)("pT1", [P, NT + 1, 2, P])]
        pmax, nmax, total, rden = (al(n, s) for n, s in (("pmax", [P, 2, 4]), ("nmax", [P, 2]),
                                                               ("total", [P, 3]), ("rden", [P, 3])))
        top, sq, g = al("top", [P, 8]), al("sq", [P, 2, 256]), al("g", [P, 2, 256])
        tree = al("tree", [P, 2, 4, 32])
        mean, var = al("mean", [P, TT, 2, 4]), al("var", [P, TT, 2, 4])
        cen = m.at("p6_cen", [P, TT, 2, 256], m.FMO + F_BQ * ALL * 4)
        pL = [ctx.enter_context(nc.psum_tensor(f"p6_L{i}", [P, 512], F32)) for i in range(4)]
        pP = [ctx.enter_context(nc.psum_tensor(f"p6_P{i}", [P, 4, P], F32)) for i in range(2)]
        pO = [ctx.enter_context(nc.psum_tensor(f"p6_O{i}", [P, 512], F32)) for i in range(2)]

        (w_in, g_in, norm_own, pool_own, centred, var_ready, rstd_ready, caches_in, zeroed, qz_ready, dve_own, logit_ready,
         masked, nmax_ready, exp_ready, turned, pT_copied, o_ready, o_used, rden_ready, normal_ready, full_copied) = (sem(n) for n in (
            "w_in g_in norm_own pool_own centred var_ready rstd_ready caches_in zeroed qz_ready dve_own logit_ready "
            "masked nmax_ready exp_ready turned pT_copied o_ready o_used rden_ready normal_ready full_copied").split())
        kv_rows = lambda h: slice(64 * (h // GQ), 64 * (h // GQ) + 64)

        heads = [(t, h) for t in range(TT) for h in range(HC)]
        logits = [(t, h, s) for t, h in heads for s in range(len(key_spans(t)))]
        n_logits = {(t, h): sum(1 for x in logits if x[:2] <= (t, h)) for t, h in heads}

        def blocks(t):
            return [(META + P * j, P) for j in range(t + 1)] + [(0, META)] if t < NT else [(0, P), (P, P)]
        groups = [(n, g) for n, (t, h) in enumerate(heads) for g in range(-(-len(blocks(t)) // 4))]

        ctx.enter_context(sem)
        with nc.Block() as block:
            @block.sync
            def _(sp):
                sp.dma_start(g[:, :, :], d["g_norms"].partition_broadcast(P)).then_inc(g_in, 16)
                sp.dma_start(kC[:, :, :], d["kT_cache"]).then_inc(caches_in, 16)
                sp.dma_start(vC[:, :, :], d["v_cache"]).then_inc(caches_in, 16)
                sp.dma_start(m.w_out0[:, :, :], d["w_out"][:, 0:2, :]).then_inc(w_in, 16)
                sp.dma_start(m.w_out2[:, :, :], d["w_out"][:, 2:6, :]).then_inc(w_in, 16)
                sp.wait_ge(caches_in, 32)
                sp.wait_ge(g_in, 16)
                sp.wait_ge(w_in, 32)

            @block.gpsimd
            def _(pool):
                chain = Chain(pool, pool_own)
                halves = lambda t: m.tm[:, t, 0:1024].rearrange("p (g a v) -> p g a v", g=2, a=2)
                heads4 = lambda ap: ap.rearrange("p g (h v) -> p g h v", v=64)
                each = lambda ap: over(ap.unsqueeze(3), [P, 2, 4, 64])

                def head_sums(out, src):
                    n = 32
                    while n:
                        dst = tree[:, :, :, 0:n] if n > 1 else out.unsqueeze(3)
                        chain.link(nc.gpsimd.tensor_tensor(dst, src[:, :, :, 0:n], src[:, :, :, n:2 * n], ALU.add))
                        src, n = tree, n // 2
                for t in range(TT):
                    o = heads4(halves(t)[:, :, 0, :])
                    head_sums(mean[:, t, :, :], o)
                    chain.link(nc.gpsimd.tensor_scalar(mean[:, t, :, :], mean[:, t, :, :], 1.0 / 64, None, ALU.mult))
                    nc.gpsimd.tensor_tensor(heads4(cen[:, t, :, :]), o, each(mean[:, t, :, :]), ALU.subtract).then_inc(centred, 1)
                    pool.wait_ge(centred, t + 1)
                    chain.link(nc.gpsimd.tensor_tensor(sq[:, :, :], cen[:, t, :, :], cen[:, t, :, :], ALU.mult))
                    head_sums(var[:, t, :, :], heads4(sq[:, :, :]))
                nc.gpsimd.tensor_scalar(var[:, :, :, :], var[:, :, :, :], 1.0 / 64, EPS, ALU.mult, ALU.add).then_inc(var_ready, 1)
                nc.gpsimd.memset(qz[:, :, :, :], 0.0).then_inc(zeroed, 1)
                pool.wait_ge(zeroed, 1)
                own = lambda ap: ap[:, PROMPT:ALL].rearrange("p (i t) -> p i t", t=SLEN)
                for c in range(4):
                    nc.gpsimd.tensor_copy(bass.AP(qz, c * NSEQ * P, [[4 * NSEQ * P, P], [P + SLEN, NSEQ], [1, SLEN]]),
                                          own(m.fm[:, F_CQ + c, :])).then_inc(qz_ready, 1)
                pool.wait_ge(g_in, 16)
                pool.wait_ge(rstd_ready, 1)
                for t in range(TT):
                    c4, gate = cen[:, t, :, :], halves(t)[:, :, 1, :]
                    chain.link(nc.gpsimd.tensor_tensor(heads4(c4), heads4(c4), each(var[:, t, :, :]), ALU.mult))
                    chain.link(nc.gpsimd.tensor_tensor(c4, c4, g[:, :, :], ALU.mult))
                    nc.gpsimd.tensor_tensor(gate, gate, c4, ALU.mult)

            @block.vector
            def _(dve):
                own = Chain(dve, dve_own)
                def reciprocal(g):
                    dve.wait_ge(exp_ready, g + 1)
                    nc.vector.reciprocal(rden[:, g % 3:g % 3 + 1], total[:, g % 3:g % 3 + 1]).then_inc(rden_ready, 1)

                def output(q):
                    t, j = q // 4, q % 4
                    dve.wait_ge(o_ready, q + 1)
                    dve.wait_ge(centred, t + 1)
                    c = (AV, BV)[j // 2] + P * (j % 2)
                    for i in range(2):
                        nc.vector.tensor_copy(m.tm[64 * i:64 * i + 64, t, c:c + P], pO[q % 2][0:64, P * i:P * i + P]).then_inc(o_used, 1)

                n_log = n_round = 0
                weight = [NK[t] for t in range(LATE[1]) for h in range(HC)]
                for t in range(TT):
                    for h in range(HC):
                        g = t * HC + h
                        while n_round < len(LEFT) and n_round * sum(weight) < len(LEFT) * sum(weight[:g + 1]):
                            late = LEFT[n_round]
                            src = score_of(m, None, late, 0, NK[late])
                            own.link(nc.vector.max(top[:, :], src))
                            own.link(nc.vector.match_replace(src, top[:, :], src, TAKEN))
                            n_round += 1
                            if late not in LEFT[n_round:]:
                                key_bias(nc, own, m, late, src)
                        if g >= 2:
                            dve.wait_ge(exp_ready, g - 1)
                        if g >= 3:
                            dve.wait_ge(turned, sum(1 for x in groups if x[0] <= g - 3))
                        ks = key_spans(t)
                        for s, (a, b) in enumerate(ks):
                            dve.wait_ge(logit_ready, n_log + 1)
                            nc.vector.tensor_tensor_reduce(logit[:, g % 3, a:b], pL[n_log % 4][:, 0:b - a],
                                                           m.bias[:, KEY_AT[t] + a:KEY_AT[t] + b], 1.0,
                                                           -3e38, ALU.add, ALU.max, pmax[:, g % 2, s:s + 1]).then_inc(masked, 1)
                            n_log += 1
                        dve.wait_ge(masked, n_log)
                        if len(ks) > 1:
                            own.link(nc.vector.tensor_reduce(pmax[:, g % 2, 3:4], pmax[:, g % 2, 0:len(ks)], AX.X, ALU.max))
                            top_col = 3
                        else:
                            top_col = 0
                        nc.vector.tensor_scalar(nmax[:, g % 2:g % 2 + 1], pmax[:, g % 2, top_col:top_col + 1], -DHC ** -0.5, None,
                                                ALU.mult).then_inc(nmax_ready, 1)
                        if g:
                            reciprocal(g - 1)
                        if g >= 5 and g % 2:
                            output((g - 5) // 2)
                reciprocal(len(heads) - 1)
                output(len(heads) // 2 - 2)
                output(len(heads) // 2 - 1)

            @block.scalar
            def _(act):
                own = Chain(act, norm_own)
                def exponent(g):
                    t, h = heads[g]
                    act.wait_ge(nmax_ready, g + 1)
                    if g >= 3:
                        act.wait_ge(rden_ready, g - 2)
                    nc.scalar.activation(logit[:, g % 3, 0:NK[t]], logit[:, g % 3, 0:NK[t]], ACT.Exp, scale=DHC ** -0.5,
                                         bias=nmax[:, g % 2:g % 2 + 1], accum_out=total[:, g % 3:g % 3 + 1]).then_inc(exp_ready, 1)

                def normalise(g):
                    t, h = heads[g]
                    act.wait_ge(rden_ready, g + 1)
                    act.wait_ge(exp_ready, g + 1)
                    nc.scalar.activation(logit[:, g % 3, 0:NK[t]], logit[:, g % 3, 0:NK[t]], ACT.Copy,
                                         scale=rden[:, g % 3:g % 3 + 1]).then_inc(normal_ready, 1)

                n_turned = 0

                def copies(g):
                    nonlocal n_turned
                    t, h = heads[g]
                    bl = blocks(t)
                    q = g // 2
                    if q >= 2:
                        act.wait_ge(o_ready, q - 1)
                    for k in range(-(-len(bl) // 4)):
                        act.wait_ge(turned, n_turned + 1)
                        part = bl[4 * k:4 * k + 4]
                        bank = pP[n_turned % 2]
                        full = [x for x in part if x[1] == P]
                        if full:
                            ins = nc.scalar.copy(pT[q % 2][:, 4 * k:4 * k + len(full), g % 2, :], bank[:, 0:len(full), :])
                        if len(full) < len(part):
                            if full:
                                ins.then_inc(full_copied, 1)
                            ins = nc.scalar.copy(pT[q % 2][0:META, 4 * k + len(full), g % 2, :], bank[0:META, len(full), :])
                        ins.then_inc(pT_copied, 1)
                        n_turned += 1
                for g in range(len(heads) + 2):
                    if g == 3 * HC:
                        act.wait_ge(var_ready, 1)
                        flat = var[:, :, :, :].rearrange("p t g h -> p (t g h)")
                        own.link(nc.scalar.activation(flat, flat, ACT.Ln))
                        nc.scalar.activation(flat, flat, ACT.Exp, scale=-0.5).then_inc(rstd_ready, 1)
                    if g < len(heads):
                        exponent(g)
                    if 1 <= g <= len(heads):
                        normalise(g - 1)
                    if g >= 2:
                        copies(g - 2)

            @block.tensor
            def _(pe):
                n_log = 0

                def logit_products(g):
                    nonlocal n_log
                    t, h = heads[g]
                    if g == NT * HC:
                        pe.wait_ge(caches_in, 32)
                        pe.wait_ge(qz_ready, 4)
                    q = m.fm[kv_rows(h), F_CQ + h % GQ, q_cols(t)]
                    for a, b in key_spans(t):
                        if n_log >= 4:
                            pe.wait_ge(masked, n_log - 3)
                        bank = pL[n_log % 4]
                        if t < NT:
                            mm = nc.tensor.matmul(bank[:, 0:b - a], q, m.fm[kv_rows(h), F_CK, a:b])
                        else:
                            for i in range(NSEQ):
                                nc.tensor.matmul(bank[:, 0:P], qz[kv_rows(h), h % GQ, i, :], kC[kv_rows(h), i, :],
                                                 start=i == 0, stop=i == NSEQ - 1)
                            mm = nc.tensor.matmul(bank[:, P:SK], q, m.fm[kv_rows(h), F_CK, PROMPT:ALL])
                        mm.then_inc(logit_ready, 1)
                        n_log += 1

                n_turned = 0

                def turn(g):
                    nonlocal n_turned
                    t, h = heads[g]
                    bl = blocks(t)
                    pe.wait_ge(normal_ready, g + 1)
                    for k in range(-(-len(bl) // 4)):
                        if n_turned >= 2:
                            pe.wait_ge(pT_copied, n_turned - 1)
                        for j, (a, n) in enumerate(bl[4 * k:4 * k + 4]):
                            mm = nc.tensor.transpose(pP[n_turned % 2][0:n, j, :], logit[:, g % 3, a:a + n], cols(m, "ident"))
                        mm.then_inc(turned, 1)
                        n_turned += 1

                def values(q):
                    g = 2 * q
                    t, h = heads[g]
                    bl = blocks(t)
                    pe.wait_ge(pT_copied, sum(1 for x in groups if x[0] <= g + 1))
                    if q >= 2:
                        pe.wait_ge(o_used, 2 * (q - 2) + 2)
                    out = pO[q % 2][0:64, 0:2 * P]
                    turned_p = pT[q % 2]
                    c = CV + 64 * (h // GQ)
                    if t == NT:
                        nc.tensor.matmul(out, m.tm[:, SAMPLE, c:c + 64], turned_p[:, 1, :, :].rearrange("p h t -> p (h t)"),
                                         start=True, stop=False, skip_group_check=True)
                        each = out.rearrange("p (h t) -> p h t", h=2)
                        for i in range(NSEQ):
                            own = slice(SLEN * i, SLEN * i + SLEN)
                            mm = nc.tensor.matmul(each[:, :, own], vC[:, i, c - CV:c - CV + 64], turned_p[:, 0, :, own],
                                                  start=False, stop=i == NSEQ - 1, skip_group_check=True)
                    else:
                        for j, (a, n) in enumerate(bl):
                            src = m.tm[0:n, j if n == P else MT, c:c + 64]
                            mm = nc.tensor.matmul(out, src, turned_p[0:n, j, :, :].rearrange("p h t -> p (h t)"),
                                                  start=j == 0, stop=j == len(bl) - 1)
                    mm.then_inc(o_ready, 1)

                for g in range(len(heads) + 3):
                    if g < len(heads):
                        logit_products(g)
                    if 2 <= g < len(heads) + 2:
                        turn(g - 2)
                    if g >= 4 and g % 2 == 0:
                        values(g // 2 - 2)


def phase_out(nc, m, d):
    with ExitStack() as ctx:
        sem = Semaphores(nc, "p7_")
        late = Bump(m, "p7_", m.FMO, m.FMO + F_AQ * ALL * 4)("w_late", [P, KD - 6, D])
        w = lambda k: (m.w_out0[:, k, :] if k < 2 else m.w_out2[:, k - 2, :] if k < 6 else late[:, k - 6, :])
        al = Bump(m, "p7_", m.FMO + F_BQ * ALL * 4, m.FMO + F_MISC * ALL * 4)
        wr = al("w_router", [P, KD, NE])
        h0, pre = (al(n, [P, 3, D]) for n in ("h0", "pre"))
        h1 = m.h1 = Bump(m, "p7_", m.SCR, m.END - 1024)("h1", [P, TT, D])
        al = Bump(m, "p7_", m.FMO + F_MISC * ALL * 4 + 4 * D * 4, m.CO)
        gb = al("gb", [P, 2, D])
        MAJOR = (2, 3, 6, 7)
        yT, hT = al("yT", [P, 2, 4, P]), al("h1T", [P, 2, KD, P])
        stats, mv = al("stats", [P, 3, 2, 6]), al("mv", [P, 3, 4])
        m.rl = m.at("router_logits", [P, TT, NE], m.END - 1024)
        pT, pH = ctx.enter_context(nc.psum_tensor("p7_T", [P, 4, P], F32)), ctx.enter_context(nc.psum_tensor("p7_H", [P, KD, P], F32))
        pY, pR = ctx.enter_context(nc.psum_tensor("p7_Y", [P, 2, 512], F32)), ctx.enter_context(nc.psum_tensor("p7_R", [P, 512], F32))
        (w_in, dve_own, act_own, pool_own, y_turned, yT_copied, mixed, pre_ready, var_ready, rstd_ready, xn_ready,
         h1_ready, h1_turned, h1T_copied, routed, r_copied) = (sem(n) for n in (
            "w_in dve_own act_own pool_own y_turned yT_copied mixed pre_ready var_ready rstd_ready xn_ready "
            "h1_ready h1_turned h1T_copied routed r_copied").split())
        h0_in, h1_out = [sem(f"h0_in{u}") for u in range(3)], sem("h1_out")

        ctx.enter_context(sem)
        with nc.Block() as block:
            @block.sync
            def _(sp):
                sp.dma_start(late[:, :, :], d["w_out"][:, 6:KD, :]).then_inc(w_in, 16)
                sp.dma_start(wr[:, :, :], d["w_router"]).then_inc(w_in, 16)
                sp.dma_start(gb[:, :, :], d["ln1_gb"].partition_broadcast(P)).then_inc(w_in, 16)
                for t in range(3):
                    sp.dma_start(h0[:, t, :], m.h0_dram[t * P:(t + 1) * P, :]).then_inc(h0_in[t], 16)
                for t in range(TT):
                    u = t % 3
                    if t + 3 < TT:
                        sp.wait_ge(pre_ready, t + 1)
                        sp.dma_start(h0[:, u, :], m.h0_dram[(t + 3) * P:(t + 4) * P, :]).then_inc(h0_in[u], 16)
                    sp.wait_ge(h1_ready, t + 1)
                    sp.dma_start(m.h1_dram[t * P:(t + 1) * P, :], h1[:, t, :]).then_inc(h1_out, 16)
                sp.wait_ge(h1_out, 16 * TT)

            @block.gpsimd
            def _(pool):
                own = Chain(pool, pool_own)
                pool.wait_ge(w_in, 48)
                for t in range(TT):
                    u = t % 3
                    pool.wait_ge(xn_ready, t + 1)
                    own.link(nc.gpsimd.tensor_tensor(h1[:, t, :], h1[:, t, :], gb[:, 0, :], ALU.mult))
                    nc.gpsimd.tensor_tensor(h1[:, t, :], h1[:, t, :], gb[:, 1, :], ALU.add).then_inc(h1_ready, 1)

            @block.vector
            def _(dve):
                own = Chain(dve, dve_own)

                def logits(t):
                    dve.wait_ge(routed, t + 1)
                    nc.vector.tensor_copy(m.rl[:, t, :], pR[:, 0:NE]).then_inc(r_copied, 1)
                for t in range(TT):
                    u = t % 3
                    dve.wait_ge(h0_in[u], 16 * (t // 3) + 16)
                    dve.wait_ge(mixed, t + 1)
                    nc.vector.scalar_tensor_tensor(pre[:, u, :], h0[:, u, :], ALPHA, pY[:, :, :].rearrange("p a b -> p (a b)"),
                                                   ALU.mult, ALU.add).then_inc(pre_ready, 1)
                    dve.wait_ge(pre_ready, t + 1)
                    own.link(nc.vector.bn_stats(stats[:, u, 0, :], pre[:, u, 0:512]))
                    own.link(nc.vector.bn_stats(stats[:, u, 1, :], pre[:, u, 512:1024]))
                    own.link(nc.vector.bn_aggr(mv[:, u, 0:2], stats[:, u, :, :]))
                    nc.vector.tensor_scalar(mv[:, u, 3:4], mv[:, u, 1:2], EPS, None, ALU.add).then_inc(var_ready, 1)
                    if t:
                        logits(t - 1)
                    dve.wait_ge(rstd_ready, t + 1)
                    nc.vector.tensor_scalar(h1[:, t, :], pre[:, u, :], mv[:, u, 0:1], mv[:, u, 3:4],
                                            ALU.subtract, ALU.mult).then_inc(xn_ready, 1)
                logits(TT - 1)

            @block.scalar
            def _(act):
                own = Chain(act, act_own)

                def y_copy(t):
                    act.wait_ge(y_turned, t + 1)
                    if t >= 2:
                        act.wait_ge(mixed, t - 1)
                    nc.scalar.copy(yT[:, t % 2, :, :], pT[:, :, :]).then_inc(yT_copied, 1)

                def h_copy(t):
                    act.wait_ge(h1_turned, t + 1)
                    if t >= 2:
                        act.wait_ge(routed, t - 1)
                    for b in range(2):
                        nc.scalar.copy(hT[:, t % 2, 4 * b:4 * b + 4, :], pH[:, 4 * b:4 * b + 4, :]).then_inc(h1T_copied, 1)
                y_copy(0)
                for t in range(TT):
                    u = t % 3
                    if t + 1 < TT:
                        y_copy(t + 1)
                    if t:
                        h_copy(t - 1)
                    act.wait_ge(var_ready, t + 1)
                    own.link(nc.scalar.activation(mv[:, u, 3:4], mv[:, u, 3:4], ACT.Ln))
                    nc.scalar.activation(mv[:, u, 3:4], mv[:, u, 3:4], ACT.Exp, scale=-0.5).then_inc(rstd_ready, 1)
                h_copy(TT - 1)

            @block.tensor
            def _(pe):
                def turn(t):
                    if t:
                        pe.wait_ge(yT_copied, t)
                    for i, k in enumerate(MAJOR):
                        mm = nc.tensor.transpose(pT[:, i, :], m.tm[:, t, k * P:(k + 1) * P], cols(m, "ident"))
                    mm.then_inc(y_turned, 1)

                def mix(t):
                    pe.wait_ge(yT_copied, t + 1)
                    if t:
                        pe.wait_ge(pre_ready, t)
                    for b in range(2):
                        for k in range(KD):
                            y = yT[:, t % 2, MAJOR.index(k), :] if k in MAJOR else m.tm[:, t, k * P:(k + 1) * P]
                            mm = nc.tensor.matmul(pY[:, b, :], y, w(k)[:, 512 * b:512 * b + 512],
                                                  start=k == 0, stop=k == KD - 1)
                    mm.then_inc(mixed, 1)

                def turn_h1(t):
                    pe.wait_ge(h1_ready, t + 1)
                    if t:
                        pe.wait_ge(h1T_copied, 2 * t)
                    for k in range(KD):
                        mm = nc.tensor.transpose(pH[:, k, :], h1[:, t, k * P:(k + 1) * P], cols(m, "ident"))
                    mm.then_inc(h1_turned, 1)

                def route(t):
                    pe.wait_ge(h1T_copied, 2 * t + 2)
                    if t:
                        pe.wait_ge(r_copied, t)
                    for k in range(KD):
                        mm = nc.tensor.matmul(pR[:, 0:NE], hT[:, t % 2, k, :], wr[:, k, :], start=k == 0, stop=k == KD - 1)
                    mm.then_inc(routed, 1)
                turn(0)
                pe.wait_ge(w_in, 48)
                for t in range(TT):
                    if t + 1 < TT:
                        turn(t + 1)
                    if t >= 2:
                        route(t - 2)
                    mix(t)
                    if t:
                        turn_h1(t - 1)
                route(TT - 2)
                turn_h1(TT - 1)
                route(TT - 1)


RING = 4
EARLY = 3
SLOTS = (2 * TOK + NE * (P - 1)) // P


def phase_route(nc, m, d):
    with ExitStack() as ctx:
        sem = Semaphores(nc, "p8_")
        al = Bump(m, "p8_", m.TMO + 1024 + RING * (KD * 2 * DE + 2 * D) * 4, m.CO)
        T16 = lambda n: al(n, [P, TT, NE])
        s, sb, e1, e2, both, tmp, pos = (T16(n) for n in ("s", "sb", "e1", "e2", "both", "tmp", "pos"))
        br = al("b_router", [P, NE])
        hi, lo = al("hi", [P, TT, NG, 2]), al("lo", [P, TT, NG, 2])
        gs, gm, g1t = al("gs", [P, TT, NG]), al("gm", [P, TT, NG]), al("g1t", [P, TT, NG])
        idx, w1, w2, tot = al("idx", [P, TT]), al("w1", [P, TT]), al("w2", [P, TT]), al("tot", [P, TT])
        ones = al("ones", [P, P])
        before, count = al("before", [P, TT, NE]), al("count", [P, NE])
        ge, ntile, cum, start = al("ge", [P, NE, 9]), al("ntile", [P, NE]), al("cum", [P, NE]), al("start", [P, NE])
        tge, eidf = al("tge", [P, SLOTS, NE]), al("eidf", [P, SLOTS])
        slotf, past = al("slotf", [P, 2, TT]), al("past", [P, SLOTS])
        less = al("less", [P, SLOTS])
        gate = al("gate", [P, 2, TT])
        lane, bound = al("lane", [P, P]), al("bound", [P, SLOTS])
        tile_of, lane_of = al("tile_of", [P, 2, TT]), al("lane_of", [P, 2, TT])
        past128, in_tile = al("past128", [P, 2, TT, SLOTS]), al("in_tile", [P, 2, TT, SLOTS])
        entry, in_lane = al("entry", [P, 2, TT, 2, SLOTS]), al("in_lane", [P, 2, TT, P])
        m.slot = m.at("slot", [P, 2, TT], m.TMO, U32)
        m.eid = m.at("eid", [P, SLOTS], m.TMO + 128, I32)
        m.wslot = m.at("wslot", [P, SLOTS], m.TMO + 640, I32)
        m.ends = m.at("ends", [P, NE], m.TMO + 800, I32)
        weights = Bump(m, "p9_", m.TMO + 1024, m.CO)
        m.wgu, m.wd = weights("wgu", [P, RING, KD, 2 * DE]), weights("wd", [P, RING, 2, D])
        m.MOE_O = weights.o
        m.token = m.at("token", [P, SLOTS], m.TMO + 320, I32)
        m.gate = m.at("gate_of_slot", [P, SLOTS], m.TMO + 480)
        p1 = ctx.enter_context(nc.psum_tensor("p8_1", [P, 512], F32))
        p2 = ctx.enter_context(nc.psum_tensor("p8_2", [P, 512], F32))
        p3 = ctx.enter_context(nc.psum_tensor("p8_3", [P, 512], F32))
        w_first, own_s, b_in, exp_in, exp_out, both_ready, ranked, lane_in, entries_ready, table_made = (sem(n) for n in (
            "w_first own b_in exp_in exp_out both_ready ranked lane_in entries_ready table_made").split())
        flat = lambda ap: ap.rearrange("p t e -> p (t e)")

        ctx.enter_context(sem)
        with nc.Block() as block:
            @block.sync
            def _(sp):
                sp.dma_start(br[:, :], d["b_router"].partition_broadcast(P)).then_inc(b_in, 16)
                sp.dma_start(lane[:, :], d["lane"]).then_inc(lane_in, 16)
                for e in range(EARLY):
                    sp.dma_start(m.wgu[:, e, :, :], d["w_gu"][e, :, :, :]).then_inc(w_first, 16)
                    sp.dma_start(m.wd[:, e, :, :], d["w_down"][e, :, :, :]).then_inc(w_first, 16)
                sp.wait_ge(w_first, 32 * EARLY)

            @block.scalar
            def _(act):
                act.wait_ge(exp_in, 1)
                nc.scalar.activation(s[:, :, :], m.rl[:, :, :], ACT.Exp, scale=-1.0).then_inc(exp_out, 1)

            @block.tensor
            def _(pe):
                pe.wait_ge(both_ready, 1)
                nc.tensor.matmul(p1[:, 0:TT * NE], cols(m, "tri"), flat(both[:, :, :]))
                nc.tensor.matmul(p2[:, 0:TT * NE], ones[:, :], flat(both[:, :, :])).then_inc(ranked, 1)
                pe.wait_ge(entries_ready, 1)
                for k in range(2):
                    for t in range(TT):
                        mm = nc.tensor.matmul(p3[:, 0:2 * SLOTS], in_lane[:, k, t, :], entry[:, k, t, :, :].rearrange("p a i -> p (a i)"),
                                              start=k + t == 0, stop=k * t == TT - 1)
                mm.then_inc(table_made, 1)

            @block.vector
            def _(dve):
                own = Chain(dve, own_s)
                V = nc.vector
                L = own.link
                L(V.memset(ones[:, :], 1.0))
                V.memset(before[:, 0, :], 0.0).then_inc(exp_in, 1)
                dve.wait_ge(exp_in, 1)
                dve.wait_ge(exp_out, 1)
                L(V.tensor_scalar(s[:, :, :], s[:, :, :], 1.0, None, ALU.add))
                L(V.reciprocal(s[:, :, :], s[:, :, :]))
                dve.wait_ge(b_in, 16)
                L(V.tensor_tensor(sb[:, :, :], s[:, :, :], over(br[:, :].unsqueeze(1), [P, TT, NE]), ALU.add))
                q = sb[:, :, :].rearrange("p t (g a b) -> p (t g) a b", g=NG, a=2)
                hv, lv = hi[:, :, :, :].rearrange("p t g a -> p (t g) a"), lo[:, :, :, :].rearrange("p t g a -> p (t g) a")
                gv, tv = gs[:, :, :].rearrange("p t g -> p (t g)"), g1t[:, :, :].rearrange("p t g -> p (t g)")
                L(V.tensor_tensor(hv, q[:, :, :, 0], q[:, :, :, 1], ALU.max))
                L(V.tensor_tensor(lv, q[:, :, :, 0], q[:, :, :, 1], ALU.min))
                L(V.tensor_tensor(gv, hv[:, :, 0], hv[:, :, 1], ALU.max))
                L(V.tensor_tensor(tv, hv[:, :, 0], hv[:, :, 1], ALU.min))
                L(V.tensor_tensor(lv[:, :, 0], lv[:, :, 0], lv[:, :, 1], ALU.max))
                L(V.tensor_tensor(tv, tv, lv[:, :, 0], ALU.max))
                L(V.tensor_tensor(gv, gv, tv, ALU.add))

                def first_max(out, val, n):
                    iota = over(cols(m, "iota16")[:, 0:n].unsqueeze(1), [P, TT, n])
                    L(V.tensor_reduce(idx[:, :], val, AX.X, ALU.max))
                    L(V.tensor_tensor(out, val, over(idx[:, :].unsqueeze(2), [P, TT, n]), ALU.is_equal))
                    L(V.scalar_tensor_tensor(out, out, -100.0, iota, ALU.mult, ALU.add))
                    L(V.tensor_reduce(idx[:, :], out, AX.X, ALU.min))
                    L(V.tensor_tensor(out, out, over(idx[:, :].unsqueeze(2), [P, TT, n]), ALU.is_equal))
                first_max(gm[:, :, :], gs[:, :, :], NG)
                L(V.tensor_scalar(gm[:, :, :], gm[:, :, :], -NEG, NEG, ALU.mult, ALU.add))
                L(V.tensor_tensor(sb[:, :, :].rearrange("p t (g e) -> p (t g) e", g=NG), sb[:, :, :].rearrange("p t (g e) -> p (t g) e", g=NG),
                                  over(gm[:, :, :].rearrange("p t g -> p (t g)").unsqueeze(2), [P, TT * NG, EG]), ALU.add))
                first_max(e1[:, :, :], sb[:, :, :], NE)
                L(V.scalar_tensor_tensor(sb[:, :, :], e1[:, :, :], -1e35, sb[:, :, :], ALU.mult, ALU.add))
                first_max(e2[:, :, :], sb[:, :, :], NE)
                for e, wk in ((e1, w1), (e2, w2)):
                    L(V.tensor_tensor(tmp[:, :, :], e[:, :, :], s[:, :, :], ALU.mult))
                    L(V.tensor_reduce(wk[:, :], tmp[:, :, :], AX.X, ALU.add))
                L(V.tensor_tensor(tot[:, :], w1[:, :], w2[:, :], ALU.add))
                L(V.reciprocal(tot[:, :], tot[:, :]))
                L(V.tensor_tensor(gate[:, 0, :], w1[:, :], tot[:, :], ALU.mult))
                L(V.tensor_tensor(gate[:, 1, :], w2[:, :], tot[:, :], ALU.mult))
                L(V.tensor_scalar(bound[:, :], cols(m, "slotid"), float(P), None, ALU.mult))
                V.tensor_tensor(both[:, :, :], e1[:, :, :], e2[:, :, :], ALU.add).then_inc(both_ready, 1)
                dve.wait_ge(ranked, 1)
                tot16 = p2[:, 0:TT * NE].rearrange("p (t e) -> p t e", e=NE)
                for t in range(1, TT):
                    L(V.tensor_tensor(before[:, t, :], before[:, t - 1, :], tot16[:, t - 1, :], ALU.add))
                L(V.tensor_tensor(count[:, :], before[:, TT - 1, :], tot16[:, TT - 1, :], ALU.add))
                L(V.tensor_tensor(ge[:, :, :], over(count[:, :].unsqueeze(2), [P, NE, 9]),
                                  over(cols(m, "tiles128").unsqueeze(1), [P, NE, 9]), ALU.is_gt))
                L(V.tensor_reduce(ntile[:, :], ge[:, :, :], AX.X, ALU.add))
                L(V.tensor_tensor_scan(cum[:, :], ones[:, 0:NE], ntile[:, :], 0.0, ALU.mult, ALU.add))
                L(V.tensor_tensor(start[:, :], cum[:, :], ntile[:, :], ALU.subtract))
                L(V.tensor_tensor(pos[:, :, :], p1[:, 0:TT * NE].rearrange("p (t e) -> p t e", e=NE), before[:, :, :], ALU.add))
                L(V.scalar_tensor_tensor(pos[:, :, :], over(start[:, :].unsqueeze(1), [P, TT, NE]), float(P), pos[:, :, :],
                                         ALU.mult, ALU.add))
                for k, e in enumerate((e1, e2)):
                    L(V.tensor_tensor(tmp[:, :, :], e[:, :, :], pos[:, :, :], ALU.mult))
                    L(V.tensor_reduce(slotf[:, k, :], tmp[:, :, :], AX.X, ALU.add))
                by_slot = [P, 2, TT, SLOTS]
                L(V.tensor_tensor(past128[:, :, :, :], over(slotf[:, :, :].unsqueeze(3), by_slot),
                                  over(bound[:, :].unsqueeze(1).unsqueeze(1), by_slot), ALU.is_ge))
                L(V.tensor_reduce(tile_of[:, :, :], past128[:, :, :, :], AX.X, ALU.add))
                L(V.tensor_scalar(tile_of[:, :, :], tile_of[:, :, :], -float(P), float(P), ALU.mult, ALU.add))
                L(V.tensor_tensor(lane_of[:, :, :], slotf[:, :, :], tile_of[:, :, :], ALU.add))
                L(V.tensor_tensor(in_tile[:, :, :, 0:SLOTS - 1], past128[:, :, :, 0:SLOTS - 1], past128[:, :, :, 1:SLOTS], ALU.subtract))
                L(V.tensor_copy(in_tile[:, :, :, SLOTS - 1], past128[:, :, :, SLOTS - 1]))
                for k in range(2):
                    L(V.tensor_tensor(entry[:, k, :, 0, :], in_tile[:, k, :, :], over(cols(m, "rowid").unsqueeze(2), [P, TT, SLOTS]), ALU.mult))
                    L(V.tensor_tensor(entry[:, k, :, 1, :], in_tile[:, k, :, :], over(gate[:, k, :].unsqueeze(2), [P, TT, SLOTS]), ALU.mult))
                dve.wait_ge(lane_in, 16)
                V.tensor_tensor(in_lane[:, :, :, :], over(lane_of[:, :, :].unsqueeze(3), [P, 2, TT, P]),
                                over(lane[:, :].unsqueeze(1).unsqueeze(1), [P, 2, TT, P]), ALU.is_equal).then_inc(entries_ready, 1)
                L(V.tensor_tensor(tge[:, :, :], over(cum[:, :].unsqueeze(1), [P, SLOTS, NE]),
                                  over(cols(m, "slotid").unsqueeze(2), [P, SLOTS, NE]), ALU.is_le))
                L(V.tensor_reduce(eidf[:, :], tge[:, :, :], AX.X, ALU.add))
                L(V.tensor_scalar(eidf[:, :], eidf[:, :], float(NE - 1), None, ALU.min))
                L(V.tensor_copy(m.eid[:, :], eidf[:, :]))
                L(V.tensor_copy(m.ends[:, :], cum[:, :]))
                for c in range(RING, NE, RING):
                    L(V.tensor_scalar(past[:, :], eidf[:, :], float(c), -float(RING), ALU.is_ge, ALU.mult))
                    if c == RING:
                        L(V.tensor_copy(less[:, :], past[:, :]))
                    else:
                        L(V.tensor_tensor(less[:, :], less[:, :], past[:, :], ALU.add))
                L(V.tensor_tensor(eidf[:, :], eidf[:, :], less[:, :], ALU.add))
                L(V.tensor_copy(m.wslot[:, :], eidf[:, :]))
                L(V.tensor_copy(m.slot[:, :, :], slotf[:, :, :]))
                dve.wait_ge(table_made, 1)
                V.tensor_copy(m.token[:, :], p3[:, 0:SLOTS])
                V.tensor_copy(m.gate[:, :], p3[:, SLOTS:2 * SLOTS])


def phase_moe(nc, m, d):
    with ExitStack() as ctx:
        sem = Semaphores(nc, "p9_")
        al = Bump(m, "p9_", m.MOE_O, m.CO)
        wgu, wd = m.wgu, m.wd
        x, xT, ys = al("x", [P, 3, D]), al("xT", [P, 3, KD, P]), al("ys", [P, 3, D])
        he, sg, heT = al("he", [P, 3, DE]), al("sg", [P, 3, DE]), al("heT", [P, 3, 2, P])
        entry, gate = al("entry", [P, 3, 1], I32), al("gate", [P, 3, 1])
        pT = ctx.enter_context(nc.psum_tensor("p9_T", [P, KD, P], F32))
        pG = [ctx.enter_context(nc.psum_tensor(f"p9_G{i}", [P, 512], F32)) for i in range(3)]
        pH = ctx.enter_context(nc.psum_tensor("p9_H", [P, 2, P], F32))
        pY = ctx.enter_context(nc.psum_tensor("p9_Y", [P, 2, 512], F32))
        (w_in, gather_held, gate_ready, entry_ready, turned, xT_copied, gu_ready, silu_ready, he_ready, h_turned, heT_ready, y_ready, ys_ready, held) = (
            sem(n) for n in "w_in gather_held gate_ready entry_ready turned xT_copied gu_ready silu_ready he_ready h_turned heT_ready y_ready ys_ready held".split())
        x_in, ys_out = ([sem(f"{n}{u}") for u in range(3)] for n in ("x_in", "ys_out"))
        R = SLOTS // 3
        assert SLOTS == 3 * R

        def turns(eng, step):
            for u in range(3):
                step(0, u, False)
            with eng.Fori(1, R) as r:
                for u in range(3):
                    step(r, u, True)

        ctx.enter_context(sem)
        with nc.Block() as block:
            @block.sync
            def _(sp):
                def load(e, u):
                    sp.dma_start(wgu[:, u, :, :], d["w_gu"][ds(e, 1), :, :, :].rearrange("a p k n -> p (a k) n")).then_inc(w_in, 16)
                    sp.dma_start(wd[:, u, :, :], d["w_down"][ds(e, 1), :, :, :].rearrange("a p k n -> p (a k) n")).then_inc(w_in, 16)
                    sp.wait_ge(w_in, 32 * e + 32)
                    sp.sem_inc(held, 1)

                sp.sem_inc(w_in, 32 * EARLY)
                for u in range(3):
                    sp.wait_ge(x_in[u], 16)
                for e in range(EARLY, RING):
                    load(e, e)
                with sp.Fori(1, NE // RING) as r:
                    for u in range(RING):
                        last = sp.value_load(m.ends[0:1, ds(RING * r + (u - RING), 1)], min_val=0, max_val=SLOTS)
                        sp.wait_ge(y_ready, last)
                        sp.sem_inc(held, 1)
                        load(RING * r + u, u)

            @block.gpsimd
            def _(pool):
                def step(r, u, later):
                    t = 3 * r + u
                    if later:
                        pool.wait_ge(turned, t - 2)
                    nc.gpsimd.tensor_copy(entry[:, u, :], m.token[:, ds(t, 1)]).then_inc(entry_ready, 1)
                    pool.wait_ge(entry_ready, t + 1)
                    pool.sem_inc(gather_held, 1)
                    pool.indirect_dma_start(x[:, u, :], None, m.h1_dram[:, :],
                                            bass.IndirectOffsetOnAxis(entry[:, u, 0:1].bitcast(U32), 0)).then_inc(x_in[u], 16)
                turns(pool, step)

            @block.vector
            def _(dve):
                def step(r, u, later):
                    t = 3 * r + u
                    if later:
                        dve.wait_ge(he_ready, t - 2)
                    nc.vector.tensor_copy(gate[:, u, :], m.gate[:, ds(t, 1)]).then_inc(gate_ready, 1)
                    dve.wait_ge(gate_ready, t + 1)
                    dve.wait_ge(silu_ready, t + 1)
                    if later:
                        dve.wait_ge(h_turned, t - 2)
                    nc.vector.scalar_tensor_tensor(he[:, u, :], sg[:, u, :], gate[:, u, :], pG[u][:, DE:2 * DE],
                                                   ALU.mult, ALU.mult).then_inc(he_ready, 1)
                    dve.wait_ge(h_turned, t + 1)
                    if later:
                        dve.wait_ge(y_ready, t - 2)
                    nc.vector.tensor_copy(heT[:, u, :, :], pH[:, :, :]).then_inc(heT_ready, 1)
                    dve.wait_ge(y_ready, t + 1)
                    if later:
                        dve.wait_ge(ys_out[u], 16 * r)
                    nc.vector.tensor_copy(ys[:, u, :], pY[:, :, :].rearrange("p a b -> p (a b)")).then_inc(ys_ready, 1)
                turns(dve, step)

            @block.scalar
            def _(act):
                def copy_x(r, u, later):
                    t = 3 * r + u
                    act.wait_ge(turned, t + 1)
                    if later:
                        act.wait_ge(gu_ready, t - 2)
                    for b in range(2):
                        nc.scalar.copy(xT[:, u, 4 * b:4 * b + 4, :], pT[:, 4 * b:4 * b + 4, :]).then_inc(xT_copied, 1)

                def step(r, u, later):
                    t = 3 * r + u
                    act.wait_ge(gu_ready, t + 1)
                    if later:
                        act.wait_ge(he_ready, t - 2)
                    nc.scalar.activation(sg[:, u, :], pG[u][:, 0:DE], ACT.Silu).then_inc(silu_ready, 1)

                def store(r, u):
                    t = 3 * r + u
                    act.wait_ge(ys_ready, t + 1)
                    act.dma_start(m.ys_dram[ds(t * P, P), :], ys[:, u, :]).then_inc(ys_out[u], 16)
                copy_x(0, 0, False)
                copy_x(0, 1, False)
                step(0, 0, False)
                copy_x(0, 2, False)
                step(0, 1, False)
                store(0, 0)
                copy_x(1, 0, True)
                step(0, 2, False)
                store(0, 1)
                with act.Fori(1, R - 1) as r:
                    for u in range(3):
                        if u < 2:
                            copy_x(r, u + 1, True)
                        else:
                            copy_x(r + 1, 0, True)
                        step(r, u, True)
                        if u:
                            store(r, u - 1)
                        else:
                            store(r - 1, 2)
                r = R - 1
                copy_x(r, 1, True)
                step(r, 0, True)
                store(r - 1, 2)
                copy_x(r, 2, True)
                step(r, 1, True)
                store(r, 0)
                step(r, 2, True)
                store(r, 1)
                store(r, 2)
                for u in range(3):
                    act.wait_ge(ys_out[u], 16 * R)

            @block.tensor
            def _(pe):
                def turn(r, u, later):
                    t = 3 * r + u
                    pe.wait_ge(x_in[u], 16 * r + 16)
                    if later or u:
                        pe.wait_ge(xT_copied, 2 * t)
                    for k in range(KD):
                        mm = nc.tensor.transpose(pT[:, k, :], x[:, u, k * P:(k + 1) * P], cols(m, "ident"))
                    mm.then_inc(turned, 1)

                def up(r, u, later):
                    t = 3 * r + u
                    e = pe.value_load(m.eid[0:1, ds(t, 1)], min_val=0, max_val=NE - 1)
                    slot = pe.value_load(m.wslot[0:1, ds(t, 1)], min_val=0, max_val=RING - 1)
                    pe.wait_ge(xT_copied, 2 * t + 2)
                    pe.wait_ge(w_in, 32 * e + 32)
                    if later:
                        pe.wait_ge(he_ready, t - 2)
                    for k in range(KD):
                        mm = nc.tensor.matmul(pG[u][:, :], xT[:, u, k, :], wgu[:, ds(slot, 1), k, :].rearrange("p a n -> p (a n)"),
                                              start=k == 0, stop=k == KD - 1)
                    mm.then_inc(gu_ready, 1)

                def down(r, u, later):
                    t = 3 * r + u
                    slot = pe.value_load(m.wslot[0:1, ds(t, 1)], min_val=0, max_val=RING - 1)
                    pe.wait_ge(he_ready, t + 1)
                    if later or u:
                        pe.wait_ge(heT_ready, t)
                    for k in range(2):
                        mm = nc.tensor.transpose(pH[:, k, :], he[:, u, k * P:(k + 1) * P], cols(m, "ident"))
                    mm.then_inc(h_turned, 1)
                    pe.wait_ge(heT_ready, t + 1)
                    if later or u:
                        pe.wait_ge(ys_ready, t)
                    for b in range(2):
                        for k in range(2):
                            mm = nc.tensor.matmul(pY[:, b, :], heT[:, u, k, :],
                                                  wd[:, ds(slot, 1), k, 512 * b:512 * b + 512].rearrange("p a n -> p (a n)"),
                                                  start=k == 0, stop=k == 1)
                    mm.then_inc(y_ready, 1)
                turn(0, 0, False)
                turn(0, 1, False)
                up(0, 0, False)
                turn(0, 2, False)
                up(0, 1, False)
                down(0, 0, False)
                turn(1, 0, True)
                up(0, 2, False)
                down(0, 1, False)
                with pe.Fori(1, R - 1) as r:
                    for u in range(3):
                        if u < 2:
                            turn(r, u + 1, True)
                        else:
                            turn(r + 1, 0, True)
                        up(r, u, True)
                        if u:
                            down(r, u - 1, True)
                        else:
                            down(r - 1, 2, True)
                r = R - 1
                turn(r, 1, True)
                up(r, 0, True)
                down(r - 1, 2, True)
                turn(r, 2, True)
                up(r, 1, True)
                down(r, 0, True)
                up(r, 2, True)
                down(r, 1, True)
                down(r, 2, True)


def phase_finish(nc, m, d):
    with ExitStack() as ctx:
        sem = Semaphores(nc, "pa_")
        al = Bump(m, "pa_", m.TMO + 1024, m.CO)
        gb = al("gb", [P, 2, D])
        a, b = (al(n, [P, TT, D]) for n in ("a", "b"))
        h1, y = m.h1, al("y", [P, 3, D])
        pre = h1
        stats, mv = al("stats", [P, 3, 2, 6]), al("mv", [P, 3, 4])
        (g_in, dve_own, act_own, sum_ready, var_ready, rstd_ready, scaled, y_ready) = (sem(n) for n in (
            "g_in dve_own act_own sum_ready var_ready rstd_ready scaled y_ready").split())
        ab_in = [sem(f"ab_in{t}") for t in range(TT)]
        y_out = [sem(f"y_out{u}") for u in range(3)]

        ctx.enter_context(sem)
        with nc.Block() as block:
            @block.sync
            def _(sp):
                sp.dma_start(gb[:, :, :], d["ln2_gb"].partition_broadcast(P)).then_inc(g_in, 16)
                for t in range(TT):
                    sp.wait_ge(y_ready, t + 1)
                    sp.dma_start(d["y"][t * P:(t + 1) * P, :], y[:, t % 3, :]).then_inc(y_out[t % 3], 16)
                for u in range(3):
                    sp.wait_ge(y_out[u], 16 * (TT // 3))

            @block.gpsimd
            def _(pool):
                for t in range(TT):
                    for k, dst in ((0, a), (1, b)):
                        pool.indirect_dma_start(dst[:, t, :], None, m.ys_dram[:, :],
                                                bass.IndirectOffsetOnAxis(m.slot[:, k, t:t + 1], 0)).then_inc(ab_in[t], 16)
                for t in range(TT):
                    pool.wait_ge(scaled, t + 1)
                    nc.gpsimd.tensor_tensor(y[:, t % 3, :], y[:, t % 3, :], gb[:, 1, :], ALU.add).then_inc(y_ready, 1)

            @block.vector
            def _(dve):
                own = Chain(dve, dve_own)

                def total(t, u):
                    dve.wait_ge(ab_in[t], 32)
                    own.link(nc.vector.tensor_tensor(a[:, t, :], a[:, t, :], b[:, t, :], ALU.add))
                    nc.vector.scalar_tensor_tensor(pre[:, t, :], h1[:, t, :], ALPHA, a[:, t, :],
                                                   ALU.mult, ALU.add).then_inc(sum_ready, 1)
                    dve.wait_ge(sum_ready, t + 1)
                    nc.vector.bn_stats(stats[:, u, 0, :], pre[:, t, 0:512])
                    own.link(nc.vector.bn_stats(stats[:, u, 1, :], pre[:, t, 512:1024]))
                    own.link(nc.vector.bn_aggr(mv[:, u, 0:2], stats[:, u, :, :]))
                    nc.vector.tensor_scalar(mv[:, u, 3:4], mv[:, u, 1:2], EPS, None, ALU.add).then_inc(var_ready, 1)

                def normal(t, u):
                    dve.wait_ge(rstd_ready, t + 1)
                    if t >= 3:
                        dve.wait_ge(y_out[u], 16 * (t // 3))
                    own.link(nc.vector.tensor_scalar(y[:, u, :], pre[:, t, :], mv[:, u, 0:1], mv[:, u, 3:4],
                                                     ALU.subtract, ALU.mult))
                    nc.vector.tensor_tensor(y[:, u, :], y[:, u, :], gb[:, 0, :], ALU.mult).then_inc(scaled, 1)
                dve.wait_ge(g_in, 16)
                for t in range(TT):
                    total(t, t % 3)
                    if t:
                        normal(t - 1, (t - 1) % 3)
                normal(TT - 1, (TT - 1) % 3)

            @block.scalar
            def _(act):
                own = Chain(act, act_own)
                for t in range(TT):
                    act.wait_ge(var_ready, t + 1)
                    own.link(nc.scalar.activation(mv[:, t % 3, 3:4], mv[:, t % 3, 3:4], ACT.Ln))
                    nc.scalar.activation(mv[:, t % 3, 3:4], mv[:, t % 3, 3:4], ACT.Exp, scale=-0.5).then_inc(rstd_ready, 1)


class Shared:
    pass


def build(nc, d):
    m = Shared()
    base = (nc.sbuf_base + 63) // 64 * 64

    def at(name, shape, offset, dtype=F32):
        return nc.alloc_sbuf_tensor_at(name, shape, dtype, offset=base + offset)
    m.at = at
    m.TMO = 0
    m.FMO = m.TMO + (TT + 1) * TM * 4
    m.HTO = m.FMO + FM * ALL * 4
    m.CO = m.HTO + KD * ALL * 4
    m.SCR = m.CO + (NCONST * 4 + 63) // 64 * 64
    m.END = (nc.sbuf_usable_end - base) // 64 * 64
    m.tm = at("tm", [P, TT + 1, TM], m.TMO)
    m.fm = at("fm", [P, FM, ALL], m.FMO)
    m.hT = at("hT", [P, KD, ALL], m.HTO)
    m.const = at("const", [P, NCONST], m.CO)
    m.h0_dram = nc.dram_tensor("h0_rows", (TOK, D), F32, kind="Internal").ap()
    m.h1_dram = nc.dram_tensor("h1_rows", (TOK, D), F32, kind="Internal").ap()
    m.ys_dram = nc.dram_tensor("expert_rows", (SLOTS * P, D), F32, kind="Internal").ap()
    for phase in PHASES:
        phase(nc, m, d)


OUTS = {
    "y": (TOK, D),
    "p_k": (PROMPT, 128), "p_v": (PROMPT, 128), "p_kidx": (PROMPT, DI),
    "p_gla": (HA, DKA, DVA), "p_c": (HB, DHB, DHB), "p_n": (HB, DHB), "p_m": (HB, 1), "p_conv": (4, P, 3),
    "s_k": (P, 128), "s_v": (P, 128), "s_kidx": (P, DI),
    "s_gla": (HA, DKA, NSEQ, DVA), "s_c": (HB, DHB, NSEQ, DHB), "s_n": (HB, DHB, NSEQ), "s_m": (HB, NSEQ),
    "s_conv": (4, P, NSEQ, 3),
}


def constants():
    p = np.arange(P)[:, None]
    c = lambda n: np.arange(n)[None, :]
    selM = np.zeros((P, 512), np.float32)
    selM[0:HB] = c(512) // P == np.arange(HB)[:, None]
    selB = np.zeros((P, 256), np.float32)
    selB[0:HB] = c(256) // DHB == np.arange(HB)[:, None]
    v = {
        "ident": p == c(P), "headA": p // DKA == c(HA), "bdA": p // DKA == c(256) // DVA,
        "causal": p <= c(P), "blocked": (p <= c(P)) & (p // SLEN == c(P) // SLEN),
        "seqmask": p // SLEN == c(NSEQ), "bdB": p // DHB == c(130) // 65, "headB": p // DHB == c(2),
        "otherseq": np.where(p // SLEN == c(P) // SLEN, 0.0, NEG), "tri": p < c(P),
        "iota16": c(NE) + 0 * p, "tiles128": P * c(9) + 0 * p, "rowid": p + P * c(TT), "slotid": c(33) + 0 * p, "selM": selM, "selB": selB,
    }
    return np.ascontiguousarray(np.concatenate([np.asarray(v[n], np.float32) for n in CONSTS], axis=1))


def lay_out(q):
    w, b = q["w_in"][0], q["b_in"][0]
    names = (('a_q', 128), ('a_k', 128), ('a_v', 256), ('a_g', 16), ('a_r', 256), ('b_qk', 512), ('b_v', 256),
             ('b_i', 4), ('b_f', 4), ('b_o', 256), ('c_q', 512), ('c_k', 128), ('c_v', 128), ('c_qi', 128),
             ('c_w', 4), ('c_ki', 32))
    s, at = {}, 0
    for n, k in names:
        s[n] = np.arange(at, at + k)
        at += k

    def pick(parts):
        return (np.concatenate([w[:, x] if not isinstance(x, int) else np.zeros((D, x), w.dtype) for x in parts], axis=1),
                np.concatenate([b[x] if not isinstance(x, int) else np.zeros((x,), b.dtype) for x in parts]))

    wt, bt = pick([s["a_v"], s["a_r"], s["b_v"], s["b_o"], s["c_v"], s["c_w"], TP - CW - 4])
    cq = [np.concatenate([s["c_q"][64 * j:64 * j + 64], s["c_q"][64 * (j + 4):64 * (j + 4) + 64]]) for j in range(4)]
    wf, bf = pick([s["c_qi"]] + [s["c_ki"]] * HI + [s["a_q"], s["a_k"], s["b_qk"]] + cq
                  + [s["c_k"], s["a_g"], 16, s["b_i"], 28, s["b_f"], 60])
    o = {
        "consts": constants(), "lane": np.tile(np.arange(P, dtype=np.float32), (P, 1)),
        "x": np.concatenate([q["x_prompt"][0], q["x_sample"].reshape(P, D), q["meta_tokens"]]),
        "ln_in_gb": np.stack([q["ln_in_g"], q["ln_in_b"]]),
        "w_tm": wt.reshape(KD, P, TP).transpose(1, 0, 2), "b_tm": bt,
        "w_fm": wf.reshape(KD, P, FM, P).transpose(2, 1, 0, 3), "b_fm": bf.reshape(FM, P).T,
    }
    o.update(lay_out_rest(q))
    return {k: np.ascontiguousarray(v) for k, v in o.items()}


def kernel(**inputs):
    import concourse.bacc as bacc
    from concourse.bass_utils import run_bass_kernel_spmd

    q = {k: np.asarray(v) for k, v in inputs.items()}
    arrays = lay_out(q)
    nc = bacc.Bacc("TRN2", target_bir_lowering=False, num_devices=1)
    d = {k: nc.dram_tensor("in_" + k, v.shape, F32, kind="ExternalInput").ap() for k, v in arrays.items()}
    d.update({k: nc.dram_tensor("out_" + k, s, F32, kind="ExternalOutput").ap() for k, s in OUTS.items()})
    build(nc, d)
    r = run_bass_kernel_spmd(nc, [{"in_" + k: v for k, v in arrays.items()}], core_ids=[0]).results[0]
    g = {k: np.asarray(r["out_" + k]) for k in OUTS}
    rows = lambda n, *s: g[n].reshape(*s)
    return (
        g["y"][0:SEQ].reshape(1, SEQ, D), g["y"][SEQ:TOK].reshape(NSEQ, SLEN, D),
        rows("p_k", 1, 1, PROMPT, KVC, DHC), rows("p_v", 1, 1, PROMPT, KVC, DHC), rows("p_kidx", 1, 1, PROMPT, DI),
        g["p_gla"][None, None], g["p_c"].transpose(0, 2, 1)[None, None], g["p_n"][None, None],
        g["p_m"].reshape(1, 1, HB), g["p_conv"].transpose(2, 0, 1).reshape(1, 1, 3, 512),
        rows("s_k", 1, NSEQ, SLEN, KVC, DHC), rows("s_v", 1, NSEQ, SLEN, KVC, DHC), rows("s_kidx", 1, NSEQ, SLEN, DI),
        g["s_gla"].transpose(2, 0, 1, 3)[None], g["s_c"].transpose(2, 0, 3, 1)[None], g["s_n"].transpose(2, 0, 1)[None],
        g["s_m"].T[None], g["s_conv"].transpose(2, 3, 0, 1).reshape(1, NSEQ, 3, 512),
    )
def lay_out_rest(q):
    P, NSEQ = 128, 8
    cw, cb = q["conv_w"][0], q["conv_b"][0]
    bd = np.zeros((HA, DKA, NSEQ, HA, DVA), np.float32)
    for h in range(HA):
        bd[h, :, :, h, :] = q["state_gla"][0][:, h].transpose(1, 0, 2)
    cbd = np.zeros((2, 2, DHB, NSEQ, 2, DHB + 1), np.float32)
    for h in range(HB):
        cbd[h // 2, h % 2, :, :, h % 2, 0:DHB] = q["state_mlstm_c"][0][:, h].transpose(2, 0, 1)
        cbd[h // 2, h % 2, :, :, h % 2, DHB] = q["state_mlstm_n"][0][:, h].T
    wo = q["w_out"][0]
    wo = np.concatenate([wo[512:768], wo[0:256], wo[768:1024], wo[256:512]])
    e = lambda w, k: w.reshape(NE, k, P, -1).transpose(0, 2, 1, 3)
    return {
        "w_out": wo.reshape(KD, P, D).transpose(1, 0, 2), "ln1_gb": np.stack([q["ln1_g"][0], q["ln1_b"][0]]),
        "w_router": q["w_router"].reshape(KD, P, NE).transpose(1, 0, 2), "b_router": q["b_router"],
        "w_gu": e(np.concatenate([q["w_gate"][0], q["w_up"][0]], axis=2), KD), "w_down": e(q["w_down"][0], 2),
        "ln2_gb": np.stack([q["ln2_g"][0], q["ln2_b"][0]]),
        "kT_cache": q["cache_k"][0].transpose(2, 3, 0, 1).reshape(P, NSEQ, P),
        "kiT_cache": np.concatenate([q["cache_kidx"][0].transpose(2, 0, 1)] * HI),
        "v_cache": q["cache_v"][0].transpose(1, 0, 2, 3).reshape(P, NSEQ, P),
        "mlstm_bd": cbd.reshape(2, P, NSEQ, 2 * DHB + 2).transpose(1, 0, 2, 3), "m0": q["state_mlstm_m"][0].T,
        "b_forget": q["b_forget"][0].reshape(HB, 1), "g_norms": np.stack([q["g_gla_norm"][0], q["g_mlstm_norm"][0]]),
        "conv_hist": q["state_conv"][0].reshape(NSEQ, 3, 4, P).transpose(3, 2, 0, 1),
        "conv_wb": np.concatenate([cw, cb[None]]).reshape(5, 4, P).transpose(2, 1, 0),
        "w_gla_gate": q["w_gla_gate"][0], "b_gla_gate": q["b_gla_gate"][0].reshape(P, 1),
        "gla_bd": bd.reshape(P, NSEQ, 256),
    }
PHASES = [phase_norm_in, phase_project, phase_gla, phase_mlstm, phase_dsa,
          phase_out, phase_route, phase_moe, phase_finish]
```
